# Optimizing a Trainium2 kernel written in Bass

```python
import math
import jax
import jax.numpy as jnp
from jax import lax
import numpy as np
import jax, jax.numpy as jnp

D_MODEL = 1024
BATCH = 1
SEQ = 256
DEPTH = 2

GRID_W = 64
CTX_LEN = 256
N_MIXERS = 4
N_MOD = 9
BLOCK_Q = 128
ROPE_BASE = 10000.0
EPS = 1e-6
NEG_INF = -1e30
D_FF = 2816

GQA_HEADS = 16
GQA_KV_HEADS = 4
GQA_HEAD_DIM = 64
GQA_WINDOW = 128

DIFF_HEADS = 8
DIFF_HEAD_DIM = 64

HGRN_HEADS = 8
HGRN_KEY_DIM = 128
HGRN_VAL_DIM = D_MODEL // HGRN_HEADS
HGRN_CHUNK = 64

MLA_HEADS = 16
MLA_Q_LORA = 256
MLA_KV_LORA = 256
MLA_NOPE = 64
MLA_ROPE = 32
MLA_V_DIM = 64


def _rmsnorm(x, w):
    xf = x.astype(jnp.float32)
    y = xf * lax.rsqrt(jnp.mean(xf * xf, axis=-1, keepdims=True) + EPS)
    return (y * w.astype(jnp.float32)).astype(x.dtype)

def _pre(h, gain, shift, scale):
    return _rmsnorm(h, gain) * (1.0 + scale) + shift

def _swiglu(h, w_gate, w_up, w_down):
    return (jax.nn.silu(h @ w_gate) * (h @ w_up)) @ w_down

def _axial_rope_tables(n_tokens, rot_dim):
    rows = n_tokens // GRID_W
    row = jnp.repeat(jnp.arange(rows, dtype=jnp.float32), GRID_W)
    col = jnp.tile(jnp.arange(GRID_W, dtype=jnp.float32), rows)
    axis_dim = rot_dim // 2
    inv_freq = ROPE_BASE ** (-jnp.arange(0, axis_dim, 2, dtype=jnp.float32) / axis_dim)
    ang_r = row[:, None] * inv_freq[None, :]
    ang_c = col[:, None] * inv_freq[None, :]
    ang = jnp.concatenate([ang_r, ang_r, ang_c, ang_c], axis=-1)
    return jnp.cos(ang), jnp.sin(ang)

def _apply_rope(x, cos, sin):
    a = x.shape[-1] // 2
    f = a // 2
    rot = jnp.concatenate([-x[..., f:a], x[..., :f], -x[..., a + f:], x[..., a:a + f]], axis=-1)
    out = x.astype(jnp.float32) * cos[None, :, None, :] + rot.astype(jnp.float32) * sin[None, :, None, :]
    return out.astype(x.dtype)

def _to_blocks(a):
    b, s = a.shape[:2]
    return jnp.moveaxis(a.reshape((b, s // BLOCK_Q, BLOCK_Q) + a.shape[2:]), 1, 0)

def _from_blocks(o):
    nb, b, bq = o.shape[:3]
    return jnp.moveaxis(o, 0, 1).reshape((b, nb * bq) + o.shape[3:])

def _gqa_window_mixer(hx, hc, w_in, w_out, sinks, cos, sin, with_ctx_out):
    B, S, _ = hx.shape
    H, KV, HD = GQA_HEADS, GQA_KV_HEADS, GQA_HEAD_DIM
    G = H // KV
    QD, KD = H * HD, KV * HD
    scale = HD ** -0.5
    sink = sinks.astype(jnp.float32).reshape(1, KV, G, 1, 1)

    def proj_q(h):
        return (h @ w_in[:, :QD]).reshape(h.shape[0], h.shape[1], H, HD)

    def proj_kv(h):
        p = h @ w_in[:, QD:]
        return (p[..., :KD].reshape(h.shape[0], h.shape[1], KV, HD),
                p[..., KD:].reshape(h.shape[0], h.shape[1], KV, HD))

    def sink_softmax(s):
        m = jnp.maximum(jnp.max(s, axis=-1, keepdims=True), sink)
        e = jnp.exp(s - m)
        return e / (jnp.sum(e, axis=-1, keepdims=True) + jnp.exp(sink - m))

    kx, vx = proj_kv(hx)
    kc, vc = proj_kv(hc)
    kx = _apply_rope(kx, cos, sin)
    qx = _apply_rope(proj_q(hx), cos, sin).reshape(B, S, KV, G, HD)

    span = BLOCK_Q + 2 * GQA_WINDOW
    pad = ((0, 0), (GQA_WINDOW, GQA_WINDOW), (0, 0), (0, 0))
    kxp, vxp = jnp.pad(kx, pad), jnp.pad(vx, pad)
    k_off = jnp.arange(span) - GQA_WINDOW
    band = jnp.abs(jnp.arange(BLOCK_Q)[:, None] - k_off[None, :]) <= GQA_WINDOW

    def block(args):
        start, qb = args
        kb = lax.dynamic_slice_in_dim(kxp, start, span, axis=1)
        vb = lax.dynamic_slice_in_dim(vxp, start, span, axis=1)
        k_abs = start + k_off
        mask = band & ((k_abs >= 0) & (k_abs < S))[None, :]
        s_loc = jnp.where(mask, jnp.einsum('bqkgd,bskd->bkgqs', qb, kb).astype(jnp.float32) * scale, NEG_INF)
        s_ctx = jnp.einsum('bqkgd,bckd->bkgqc', qb, kc).astype(jnp.float32) * scale
        p = sink_softmax(jnp.concatenate([s_loc, s_ctx], axis=-1)).astype(vb.dtype)
        return (jnp.einsum('bkgqs,bskd->bqkgd', p[..., :span], vb)
                + jnp.einsum('bkgqc,bckd->bqkgd', p[..., span:], vc))

    starts = jnp.arange(S // BLOCK_Q, dtype=jnp.int32) * BLOCK_Q
    ox = _from_blocks(lax.map(block, (starts, _to_blocks(qx))))
    ox = ox.reshape(B, S, QD) @ w_out
    oc = None
    if with_ctx_out:
        bc, nc = hc.shape[:2]
        qc = proj_q(hc).reshape(bc, nc, KV, G, HD)
        s = jnp.einsum('bqkgd,bckd->bkgqc', qc, kc).astype(jnp.float32) * scale
        p = sink_softmax(s).astype(vc.dtype)
        oc = jnp.einsum('bkgqc,bckd->bqkgd', p, vc).reshape(bc, nc, QD) @ w_out
    return ox, oc

def _diff_attn_mixer(hx, hc, w_in, w_out, lam_params, subln_w, lambda_init, cos, sin, with_ctx_out):
    B, S, _ = hx.shape
    H, HD = DIFF_HEADS, DIFF_HEAD_DIM
    QK = H * 2 * HD
    scale = HD ** -0.5
    lp = lam_params.astype(jnp.float32)
    lam = jnp.exp(jnp.sum(lp[0] * lp[1])) - jnp.exp(jnp.sum(lp[2] * lp[3])) + lambda_init

    def proj_q(h):
        return (h @ w_in[:, :QK]).reshape(h.shape[0], h.shape[1], H, 2, HD)

    def proj_kv(h):
        p = h @ w_in[:, QK:]
        return (p[..., :QK].reshape(h.shape[0], h.shape[1], H, 2, HD),
                p[..., QK:].reshape(h.shape[0], h.shape[1], H, 2 * HD))

    def rope(t):
        return _apply_rope(t.reshape(B, S, H * 2, HD), cos, sin).reshape(B, S, H, 2, HD)

    def diff_probs(s):
        p = jax.nn.softmax(s * scale, axis=-1)
        return p[:, :, 0] - lam * p[:, :, 1]

    def head_out(o):
        o = _rmsnorm(o, subln_w) * (1.0 - lambda_init)
        return o.reshape(o.shape[0], o.shape[1], H * 2 * HD) @ w_out

    kx, vx = proj_kv(hx)
    kc, vc = proj_kv(hc)
    kx = rope(kx)
    qx = rope(proj_q(hx))

    def block(qb):
        s_lat = jnp.einsum('bqhjd,bkhjd->bhjqk', qb, kx)
        s_ctx = jnp.einsum('bqhjd,bchjd->bhjqc', qb, kc)
        p = diff_probs(jnp.concatenate([s_lat, s_ctx], axis=-1).astype(jnp.float32)).astype(vx.dtype)
        return (jnp.einsum('bhqk,bkhe->bqhe', p[..., :S], vx)
                + jnp.einsum('bhqc,bche->bqhe', p[..., S:], vc))

    ox = head_out(_from_blocks(lax.map(block, _to_blocks(qx))))
    oc = None
    if with_ctx_out:
        qc = proj_q(hc)
        p = diff_probs(jnp.einsum('bqhjd,bchjd->bhjqc', qc, kc).astype(jnp.float32)).astype(vc.dtype)
        oc = head_out(jnp.einsum('bhqc,bche->bqhe', p, vc))
    return ox, oc

def _hgrn2_chunk_scan(q, k, v, logf, s0):
    B, T, H, DK = q.shape
    DV = v.shape[-1]
    C = HGRN_CHUNK
    N = T // C

    def chunks(a):
        return a.reshape(B, N, C, H, a.shape[-1]).transpose(1, 0, 3, 2, 4)

    q, k, v, logf = chunks(q), chunks(k), chunks(v), chunks(logf)
    g = jnp.cumsum(logf, axis=3)
    g_mid = g[:, :, :, C // 2:C // 2 + 1, :]
    g_last = g[:, :, :, C - 1:, :]
    a = jnp.einsum('nbhtd,nbhsd->nbhts', q * jnp.exp(g - g_mid), k * jnp.exp(g_mid - g))
    lower = jnp.arange(C)[:, None] >= jnp.arange(C)[None, :]
    a = jnp.where(lower, a, 0.0)
    o_intra = jnp.einsum('nbhts,nbhse->nbhte', a, v)

    def step(state, inp):
        q_in, k_out, v_c, decay = inp
        o = jnp.einsum('bhtd,bhde->bhte', q_in, state)
        state = state * decay[..., None] + jnp.einsum('bhsd,bhse->bhde', k_out, v_c)
        return state, o

    s_fin, o_inter = lax.scan(step, s0, (q * jnp.exp(g), k * jnp.exp(g_last - g), v, jnp.exp(g_last[:, :, :, 0, :])))
    o = (o_intra + o_inter).transpose(1, 0, 3, 2, 4).reshape(B, T, H, DV)
    return o, s_fin

def _hgrn2_mixer(hx, hc, w_in, w_out, norm_w, lb, with_ctx_out):
    H, DK, DV = HGRN_HEADS, HGRN_KEY_DIM, HGRN_VAL_DIM
    KD, VD = H * DK, H * DV

    def proj(h):
        b, t = h.shape[:2]
        p = (h @ w_in).astype(jnp.float32)
        q = jax.nn.silu(p[..., :KD]).reshape(b, t, H, DK)

        def forget(z):
            f = lb + (1.0 - lb) * jax.nn.sigmoid(z)
            return jnp.log(f).reshape(b, t, H, DK), (1.0 - f).reshape(b, t, H, DK)

        fwd = forget(p[..., KD:2 * KD])
        bwd = forget(p[..., 2 * KD:3 * KD])
        v = p[..., 3 * KD:3 * KD + VD].reshape(b, t, H, DV)
        gate = p[..., 3 * KD + VD:]
        return q, fwd, bwd, v, gate

    def flip(a):
        return jnp.flip(a, axis=1)

    def readout(o, gate, dtype):
        b, t = o.shape[:2]
        y = _rmsnorm(o, norm_w).reshape(b, t, VD) * jax.nn.silu(gate)
        return y.astype(dtype) @ w_out

    qc, (lfc, kfc), (lbc, kbc), vc, gc = proj(hc)
    qx, (lfx, kfx), (lbx, kbx), vx, gx = proj(hx)
    zero = jnp.zeros((hx.shape[0], H, DK, DV), jnp.float32)
    oc_f, sc_f = _hgrn2_chunk_scan(qc, kfc, vc, lfc, zero)
    oc_b, sc_b = _hgrn2_chunk_scan(flip(qc), flip(kbc), flip(vc), flip(lbc), zero)
    ox_f, _ = _hgrn2_chunk_scan(qx, kfx, vx, lfx, sc_f)
    ox_b, _ = _hgrn2_chunk_scan(flip(qx), flip(kbx), flip(vx), flip(lbx), sc_b)
    ox = readout(ox_f + flip(ox_b), gx, hx.dtype)
    oc = readout(oc_f + flip(oc_b), gc, hc.dtype) if with_ctx_out else None
    return ox, oc

def _mla_mixer(hx, hc, w_down, q_norm_w, kv_norm_w, w_uq, w_ukv, w_out, cos, sin, with_ctx_out):
    B, S, _ = hx.shape
    H, NOPE, R, VD = MLA_HEADS, MLA_NOPE, MLA_ROPE, MLA_V_DIM
    scale = (NOPE + R) ** -0.5

    def proj_q(h, rotate):
        b, t = h.shape[:2]
        cq = _rmsnorm(h @ w_down[:, :MLA_Q_LORA], q_norm_w)
        q = (cq @ w_uq).reshape(b, t, H, NOPE + R)
        qn, qr = q[..., :NOPE], q[..., NOPE:]
        if rotate:
            qr = _apply_rope(qr, cos, sin)
        return qn, qr

    def proj_kv(h, rotate):
        b, t = h.shape[:2]
        p = h @ w_down[:, MLA_Q_LORA:]
        ckv = _rmsnorm(p[..., :MLA_KV_LORA], kv_norm_w)
        kr = p[..., MLA_KV_LORA:]
        if rotate:
            kr = _apply_rope(kr[:, :, None, :], cos, sin)[:, :, 0, :]
        kv = (ckv @ w_ukv).reshape(b, t, H, NOPE + VD)
        return kv[..., :NOPE], kr, kv[..., NOPE:]

    def logits(qn, qr, kn, kr):
        s = jnp.einsum('bqhd,bkhd->bhqk', qn, kn) + jnp.einsum('bqhr,bkr->bhqk', qr, kr)
        return s.astype(jnp.float32) * scale

    knx, krx, vx = proj_kv(hx, True)
    knc, krc, vc = proj_kv(hc, False)
    qnx, qrx = proj_q(hx, True)

    def block(args):
        qn, qr = args
        s = jnp.concatenate([logits(qn, qr, knx, krx), logits(qn, qr, knc, krc)], axis=-1)
        p = jax.nn.softmax(s, axis=-1).astype(vx.dtype)
        return (jnp.einsum('bhqk,bkhe->bqhe', p[..., :S], vx)
                + jnp.einsum('bhqc,bche->bqhe', p[..., S:], vc))

    ox = _from_blocks(lax.map(block, (_to_blocks(qnx), _to_blocks(qrx))))
    ox = ox.reshape(B, S, H * VD) @ w_out
    oc = None
    if with_ctx_out:
        qnc, qrc = proj_q(hc, False)
        p = jax.nn.softmax(logits(qnc, qrc, knc, krc), axis=-1).astype(vc.dtype)
        oc = jnp.einsum('bhqc,bche->bqhe', p, vc)
        oc = oc.reshape(oc.shape[0], oc.shape[1], H * VD) @ w_out
    return ox, oc

def _layers_of(kind):
    return len(range(kind, DEPTH, N_MIXERS))

def first_inputs(seed: int = 0) -> dict:
    key = jax.random.key(seed)
    keys = iter(jax.random.split(key, 40))

    def nrm(shape, std):
        return jax.random.normal(next(keys), shape, jnp.float32) * std

    D = D_MODEL
    n_gqa, n_diff, n_hgrn, n_mla = (_layers_of(k) for k in range(N_MIXERS))
    gqa_in = (GQA_HEADS + 2 * GQA_KV_HEADS) * GQA_HEAD_DIM
    gqa_o = GQA_HEADS * GQA_HEAD_DIM
    diff_o = DIFF_HEADS * 2 * DIFF_HEAD_DIM
    hk, hv = HGRN_HEADS * HGRN_KEY_DIM, HGRN_HEADS * HGRN_VAL_DIM
    mla_down = MLA_Q_LORA + MLA_KV_LORA + MLA_ROPE
    mla_o = MLA_HEADS * MLA_V_DIM
    return {
        'x': nrm((BATCH, SEQ, D), 1.0),
        'c': nrm((BATCH, D), 1.0),
        'ctx': nrm((BATCH, CTX_LEN, D), 1.0),
        'c_ctx': nrm((D,), 1.0),
        'ada_w': nrm((DEPTH, D, N_MOD * D), 0.5 * D ** -0.5),
        'ada_b': nrm((DEPTH, N_MOD * D), 0.02),
        'norm_w': 1.0 + nrm((DEPTH, 3, D), 0.05),
        'final_norm_w': 1.0 + nrm((D,), 0.05),
        'ffn_w_gate': nrm((DEPTH, 2, D, D_FF), D ** -0.5),
        'ffn_w_up': nrm((DEPTH, 2, D, D_FF), D ** -0.5),
        'ffn_w_down': nrm((DEPTH, 2, D_FF, D), D_FF ** -0.5),
        'gqa_w_in': nrm((n_gqa, D, gqa_in), D ** -0.5),
        'gqa_w_out': nrm((n_gqa, gqa_o, D), gqa_o ** -0.5),
        'gqa_sinks': nrm((n_gqa, GQA_HEADS), 0.5),
        'diff_w_in': nrm((n_diff, D, 3 * diff_o), D ** -0.5),
        'diff_w_out': nrm((n_diff, diff_o, D), diff_o ** -0.5),
        'diff_lambda': nrm((n_diff, 4, DIFF_HEAD_DIM), 0.1),
        'diff_subln_w': 1.0 + nrm((n_diff, 2 * DIFF_HEAD_DIM), 0.05),
        'hgrn_w_in': nrm((n_hgrn, D, 3 * hk + 2 * hv), D ** -0.5),
        'hgrn_w_out': nrm((n_hgrn, hv, D), hv ** -0.5),
        'hgrn_norm_w': 1.0 + nrm((n_hgrn, HGRN_VAL_DIM), 0.05),
        'hgrn_lower_bounds': nrm((DEPTH, hk), 0.5),
        'mla_w_down': nrm((n_mla, D, mla_down), D ** -0.5),
        'mla_q_norm_w': 1.0 + nrm((n_mla, MLA_Q_LORA), 0.05),
        'mla_kv_norm_w': 1.0 + nrm((n_mla, MLA_KV_LORA), 0.05),
        'mla_w_uq': nrm((n_mla, MLA_Q_LORA, MLA_HEADS * (MLA_NOPE + MLA_ROPE)), MLA_Q_LORA ** -0.5),
        'mla_w_ukv': nrm((n_mla, MLA_KV_LORA, MLA_HEADS * (MLA_NOPE + MLA_V_DIM)), MLA_KV_LORA ** -0.5),
        'mla_w_out': nrm((n_mla, mla_o, D), mla_o ** -0.5),
    }

def first_block(x, c, ctx, c_ctx, ada_w, ada_b, norm_w, final_norm_w, ffn_w_gate, ffn_w_up, ffn_w_down,
              gqa_w_in, gqa_w_out, gqa_sinks, diff_w_in, diff_w_out, diff_lambda, diff_subln_w,
              hgrn_w_in, hgrn_w_out, hgrn_norm_w, hgrn_lower_bounds,
              mla_w_down, mla_q_norm_w, mla_kv_norm_w, mla_w_uq, mla_w_ukv, mla_w_out):
    B, S, D = x.shape
    cos_h, sin_h = _axial_rope_tables(S, GQA_HEAD_DIM)
    cos_m, sin_m = _axial_rope_tables(S, MLA_ROPE)
    lb_soft = jax.nn.softmax(hgrn_lower_bounds.astype(jnp.float32), axis=0)
    lb_all = jnp.cumsum(lb_soft, axis=0) - lb_soft[0:1]
    silu_c = jax.nn.silu(c)
    silu_cc = jax.nn.silu(c_ctx)
    hx, hc = x, ctx
    for i in range(DEPTH):
        kind, j = i % N_MIXERS, i // N_MIXERS
        with_ctx_out = i < DEPTH - 1
        mx = (silu_c @ ada_w[i] + ada_b[i]).reshape(B, N_MOD, 1, D)
        mc = (silu_cc @ ada_w[i] + ada_b[i]).reshape(N_MOD, D)
        fx = _swiglu(_pre(hx, norm_w[i, 0], mx[:, 0], mx[:, 1]), ffn_w_gate[i, 0], ffn_w_up[i, 0], ffn_w_down[i, 0])
        fc = _swiglu(_pre(hc, norm_w[i, 0], mc[0], mc[1]), ffn_w_gate[i, 0], ffn_w_up[i, 0], ffn_w_down[i, 0])
        hx = hx + 0.5 * mx[:, 2] * fx
        hc = hc + 0.5 * mc[2] * fc
        ax = _pre(hx, norm_w[i, 1], mx[:, 3], mx[:, 4])
        ac = _pre(hc, norm_w[i, 1], mc[3], mc[4])
        if kind == 0:
            ox, oc = _gqa_window_mixer(ax, ac, gqa_w_in[j], gqa_w_out[j], gqa_sinks[j], cos_h, sin_h, with_ctx_out)
        elif kind == 1:
            lambda_init = 0.8 - 0.6 * math.exp(-0.3 * i)
            ox, oc = _diff_attn_mixer(ax, ac, diff_w_in[j], diff_w_out[j], diff_lambda[j], diff_subln_w[j],
                                      lambda_init, cos_h, sin_h, with_ctx_out)
        elif kind == 2:
            ox, oc = _hgrn2_mixer(ax, ac, hgrn_w_in[j], hgrn_w_out[j], hgrn_norm_w[j], lb_all[i], with_ctx_out)
        else:
            ox, oc = _mla_mixer(ax, ac, mla_w_down[j], mla_q_norm_w[j], mla_kv_norm_w[j], mla_w_uq[j],
                                mla_w_ukv[j], mla_w_out[j], cos_m, sin_m, with_ctx_out)
        hx = hx + mx[:, 5] * ox
        fx = _swiglu(_pre(hx, norm_w[i, 2], mx[:, 6], mx[:, 7]), ffn_w_gate[i, 1], ffn_w_up[i, 1], ffn_w_down[i, 1])
        hx = hx + 0.5 * mx[:, 8] * fx
        if with_ctx_out:
            hc = hc + mc[5] * oc
            fc = _swiglu(_pre(hc, norm_w[i, 2], mc[6], mc[7]), ffn_w_gate[i, 1], ffn_w_up[i, 1], ffn_w_down[i, 1])
            hc = hc + 0.5 * mc[8] * fc
    return _rmsnorm(hx, final_norm_w)


RET_HEADS = 4
RET_DK = 128
RET_DV = 128
RET_CHUNK = 128
RET_THETA = 10000.0
DIL_HEADS = 8
DIL_DH = 64
DIL_PATTERNS = ((128, 1), (512, 4), (2048, 16))
DIL_BLOCK = 128
ROPE_THETA = 500000.0
ROT_DIM = DIL_DH // 4
GLA_HEADS = 4
GLA_DK = (D_MODEL // 2) // GLA_HEADS
GLA_DV = D_MODEL // GLA_HEADS
GLA_LOWRANK = 16
GLA_TAU = 16.0
GLA_CHUNK = 64
FFN_HIDDEN = 2816

EVEN_SIZES = (RET_HEADS * RET_DK, RET_HEADS * RET_DK, RET_HEADS * RET_DV, RET_HEADS * RET_DV,
              DIL_HEADS * DIL_DH, DIL_HEADS * DIL_DH, DIL_HEADS * DIL_DH)
EVEN_IN = sum(EVEN_SIZES)
EVEN_MIX = RET_HEADS * RET_DV + DIL_HEADS * DIL_DH
GLA_SIZES = (GLA_HEADS * GLA_DK, GLA_HEADS * GLA_DK, GLA_HEADS * GLA_DV, GLA_HEADS * GLA_DV, GLA_LOWRANK)
GLA_IN = sum(GLA_SIZES)
GLA_MIX = GLA_HEADS * GLA_DV


def _split(p, sizes):
    out, start = [], 0
    for s in sizes:
        out.append(p[..., start:start + s])
        start += s
    return out

def _rmsnorm_2(x, g):
    xf = x.astype(jnp.float32)
    y = xf * lax.rsqrt(jnp.mean(xf * xf, axis=-1, keepdims=True) + EPS)
    return (y * g.astype(jnp.float32)).astype(x.dtype)

def _head_norm(o):
    mu = jnp.mean(o, axis=-1, keepdims=True)
    var = jnp.mean(jnp.square(o - mu), axis=-1, keepdims=True)
    return (o - mu) * lax.rsqrt(var + EPS)

def _swiglu_2(h, wg, wu, wd):
    return (jax.nn.silu(h @ wg) * (h @ wu)) @ wd

def _rotary(x, inv_freq):
    rot = 2 * inv_freq.shape[0]
    pos = jnp.arange(x.shape[1], dtype=jnp.float32)
    ang = pos[:, None] * inv_freq[None, :]
    cos = jnp.cos(ang)[None, :, None, :].astype(x.dtype)
    sin = jnp.sin(ang)[None, :, None, :].astype(x.dtype)
    x1 = x[..., :rot // 2]
    x2 = x[..., rot // 2:rot]
    return jnp.concatenate([x1 * cos - x2 * sin, x2 * cos + x1 * sin, x[..., rot:]], axis=-1)

def _retention(q, k, v):
    B, S, H, Dk = q.shape
    Dv = v.shape[-1]
    C = RET_CHUNK
    N = S // C
    log_g = jnp.log(1.0 - 2.0 ** (-5.0 - jnp.arange(H, dtype=jnp.float32)))
    to_chunks = lambda t: t.reshape(B, N, C, H, t.shape[-1]).transpose(0, 3, 1, 2, 4)
    qc, kc, vc = to_chunks(q), to_chunks(k), to_chunks(v)
    i = jnp.arange(C, dtype=jnp.float32)
    rel = i[:, None] - i[None, :]
    dmask = jnp.where(rel >= 0, jnp.exp(log_g[:, None, None] * jnp.maximum(rel, 0.0)), 0.0)
    scores = jnp.einsum('bhnid,bhnjd->bhnij', qc, kc) * dmask[None, :, None]
    inner = jnp.einsum('bhnij,bhnje->bhnie', scores, vc)
    k_dec = kc * jnp.exp(log_g[:, None] * (C - 1 - i))[None, :, None, :, None]
    kv = jnp.einsum('bhnjd,bhnje->nbhde', k_dec, vc)
    chunk_decay = jnp.exp(log_g * C)[None, :, None, None]

    def step(s, kv_n):
        return s * chunk_decay + kv_n, s

    _, s_prev = lax.scan(step, jnp.zeros((B, H, Dk, Dv), jnp.float32), kv)
    q_dec = qc * jnp.exp(log_g[:, None] * (i + 1.0))[None, :, None, :, None]
    cross = jnp.einsum('bhnid,nbhde->bhnie', q_dec, s_prev)
    o = inner + cross
    return o.transpose(0, 2, 3, 1, 4).reshape(B, S, H, Dv)

def _dilated_branch(q, k, v, window, dil):
    B, S, H, Dh = q.shape
    L = S // dil
    W = window // dil
    c = DIL_BLOCK
    nb = -(-L // c)
    Lp = nb * c

    def split(t):
        return t.reshape(B, L, dil, H, Dh).transpose(0, 2, 3, 1, 4).reshape(B * dil, H, L, Dh)

    qs = jnp.pad(split(q), ((0, 0), (0, 0), (0, Lp - L), (0, 0))).reshape(B * dil, H, nb, c, Dh)

    def kblocks(t):
        t = jnp.pad(split(t), ((0, 0), (0, 0), (c, Lp - L), (0, 0))).reshape(B * dil, H, nb + 1, c, Dh)
        return jnp.concatenate([t[:, :, :-1], t[:, :, 1:]], axis=3)

    kb, vb = kblocks(k), kblocks(v)
    s = jnp.einsum('zhnqd,zhnkd->zhnqk', qs, kb).astype(jnp.float32) * (Dh ** -0.5)
    qi = jnp.arange(c)[:, None]
    kj = jnp.arange(2 * c)[None, :]
    dist = qi + c - kj
    blk = jnp.arange(nb)[:, None, None]
    valid = (dist >= 0) & (dist <= W) & (blk * c + kj - c >= 0)
    s = jnp.where(valid, s, -jnp.inf)
    m = jnp.max(s, axis=-1, keepdims=True)
    p = jnp.exp(s - m)
    l = jnp.sum(p, axis=-1, keepdims=True)
    o = jnp.einsum('zhnqk,zhnkd->zhnqd', p, vb.astype(jnp.float32)) / l
    lse = (m + jnp.log(l))[..., 0]
    o = o.reshape(B, dil, H, Lp, Dh)[:, :, :, :L].transpose(0, 3, 1, 2, 4).reshape(B, S, H, Dh)
    lse = lse.reshape(B, dil, H, Lp)[..., :L].transpose(0, 3, 1, 2).reshape(B, S, H)
    return o, lse

def _dilated_attention(q, k, v):
    outs, lses = [], []
    for window, dil in DIL_PATTERNS:
        o, lse = _dilated_branch(q, k, v, window, dil)
        outs.append(o)
        lses.append(lse)
    w = jax.nn.softmax(jnp.stack(lses, axis=0), axis=0)
    return jnp.sum(w[..., None] * jnp.stack(outs, axis=0), axis=0)

def _retention_dilated_mixer(h, w_in, w_out):
    B, S, _ = h.shape
    rq, rk, rv, rg, dq, dk, dv = _split(h @ w_in, EVEN_SIZES)
    ret_freq = RET_THETA ** (-jnp.linspace(0.0, 1.0, RET_DK // 2, dtype=jnp.float32))
    rq = _rotary(rq.reshape(B, S, RET_HEADS, RET_DK), ret_freq).astype(jnp.float32)
    rk = _rotary(rk.reshape(B, S, RET_HEADS, RET_DK), ret_freq).astype(jnp.float32) * (RET_DK ** -0.5)
    rv = rv.reshape(B, S, RET_HEADS, RET_DV).astype(jnp.float32)
    o_r = _head_norm(_retention(rq, rk, rv)).reshape(B, S, RET_HEADS * RET_DV)
    o_r = o_r * jax.nn.silu(rg.astype(jnp.float32))
    rope_freq = ROPE_THETA ** (-jnp.arange(0, ROT_DIM, 2, dtype=jnp.float32) / ROT_DIM)
    dq = _rotary(dq.reshape(B, S, DIL_HEADS, DIL_DH), rope_freq)
    dk = _rotary(dk.reshape(B, S, DIL_HEADS, DIL_DH), rope_freq)
    dv = dv.reshape(B, S, DIL_HEADS, DIL_DH)
    o_d = _dilated_attention(dq, dk, dv).reshape(B, S, DIL_HEADS * DIL_DH)
    cat = jnp.concatenate([o_r.astype(h.dtype), o_d.astype(h.dtype)], axis=-1)
    return cat @ w_out

def _gla(q, k, v, log_a):
    B, S, H, Dk = q.shape
    Dv = v.shape[-1]
    C = GLA_CHUNK
    N = S // C
    to_chunks = lambda t: t.reshape(B, N, C, H, t.shape[-1]).transpose(0, 3, 1, 2, 4)
    qc, kc, vc, lac = to_chunks(q), to_chunks(k), to_chunks(v), to_chunks(log_a)
    b = jnp.cumsum(lac, axis=3)
    b_last = b[:, :, :, -1:]
    q_t = qc * jnp.exp(b)
    k_t = kc * jnp.exp(-b)
    causal = jnp.tril(jnp.ones((C, C), dtype=bool))
    scores = jnp.where(causal, jnp.einsum('bhnid,bhnjd->bhnij', q_t, k_t), 0.0)
    inner = jnp.einsum('bhnij,bhnje->bhnie', scores, vc)
    kv = jnp.einsum('bhnjd,bhnje->nbhde', kc * jnp.exp(b_last - b), vc)
    decay = jnp.exp(b_last[:, :, :, 0]).transpose(2, 0, 1, 3)

    def step(s, inp):
        kv_n, d_n = inp
        return s * d_n[..., None] + kv_n, s

    _, s_prev = lax.scan(step, jnp.zeros((B, H, Dk, Dv), jnp.float32), (kv, decay))
    cross = jnp.einsum('bhnid,nbhde->bhnie', q_t, s_prev)
    o = inner + cross
    return o.transpose(0, 2, 3, 1, 4).reshape(B, S, H, Dv)

def _gla_mixer(h, w_in, w_a2, b_a, w_out):
    B, S, _ = h.shape
    q, k, v, r, a_low = _split(h @ w_in, GLA_SIZES)
    log_a = jax.nn.log_sigmoid((a_low @ w_a2 + b_a).astype(jnp.float32)) / GLA_TAU
    q = q.reshape(B, S, GLA_HEADS, GLA_DK).astype(jnp.float32) * (GLA_DK ** -0.5)
    k = k.reshape(B, S, GLA_HEADS, GLA_DK).astype(jnp.float32)
    v = v.reshape(B, S, GLA_HEADS, GLA_DV).astype(jnp.float32)
    log_a = log_a.reshape(B, S, GLA_HEADS, GLA_DK)
    o = _head_norm(_gla(q, k, v, log_a)).reshape(B, S, GLA_MIX)
    o = o * jax.nn.silu(r.astype(jnp.float32))
    return o.astype(h.dtype) @ w_out

def second_inputs(seed: int = 0) -> dict:
    key = jax.random.key(seed)
    ks = jax.random.split(key, 24)
    n_even = (DEPTH + 1) // 2
    n_odd = DEPTH // 2
    f32 = jnp.float32

    def w(k, shape, fan_in):
        return jax.random.normal(k, shape, f32) * (fan_in ** -0.5)

    def gain(k, shape):
        return 1.0 + 0.05 * jax.random.normal(k, shape, f32)

    return {
        "x": jax.random.normal(ks[0], (BATCH, SEQ, D_MODEL), f32),
        "ffn_pre_norm": gain(ks[1], (DEPTH, D_MODEL)),
        "ffn_pre_w_gate": w(ks[2], (DEPTH, D_MODEL, FFN_HIDDEN), D_MODEL),
        "ffn_pre_w_up": w(ks[3], (DEPTH, D_MODEL, FFN_HIDDEN), D_MODEL),
        "ffn_pre_w_down": w(ks[4], (DEPTH, FFN_HIDDEN, D_MODEL), FFN_HIDDEN),
        "mix_norm": gain(ks[5], (DEPTH, D_MODEL)),
        "ab_w_in": w(ks[6], (n_even, D_MODEL, EVEN_IN), D_MODEL),
        "ab_w_out": w(ks[7], (n_even, EVEN_MIX, D_MODEL), EVEN_MIX),
        "gla_w_in": w(ks[8], (n_odd, D_MODEL, GLA_IN), D_MODEL),
        "gla_w_a2": w(ks[9], (n_odd, GLA_LOWRANK, GLA_HEADS * GLA_DK), GLA_LOWRANK),
        "gla_b_a": 0.1 * jax.random.normal(ks[10], (n_odd, GLA_HEADS * GLA_DK), f32),
        "gla_w_out": w(ks[11], (n_odd, GLA_MIX, D_MODEL), GLA_MIX),
        "ffn_post_norm": gain(ks[12], (DEPTH, D_MODEL)),
        "ffn_post_w_gate": w(ks[13], (DEPTH, D_MODEL, FFN_HIDDEN), D_MODEL),
        "ffn_post_w_up": w(ks[14], (DEPTH, D_MODEL, FFN_HIDDEN), D_MODEL),
        "ffn_post_w_down": w(ks[15], (DEPTH, FFN_HIDDEN, D_MODEL), FFN_HIDDEN),
        "final_norm": gain(ks[16], (D_MODEL,)),
    }

def second_block(x, ffn_pre_norm, ffn_pre_w_gate, ffn_pre_w_up, ffn_pre_w_down, mix_norm,
              ab_w_in, ab_w_out, gla_w_in, gla_w_a2, gla_b_a, gla_w_out,
              ffn_post_norm, ffn_post_w_gate, ffn_post_w_up, ffn_post_w_down, final_norm):
    for l in range(DEPTH):
        h = _rmsnorm_2(x, ffn_pre_norm[l])
        x = x + 0.5 * _swiglu_2(h, ffn_pre_w_gate[l], ffn_pre_w_up[l], ffn_pre_w_down[l])
        h = _rmsnorm_2(x, mix_norm[l])
        if l % 2 == 0:
            x = x + _retention_dilated_mixer(h, ab_w_in[l // 2], ab_w_out[l // 2])
        else:
            x = x + _gla_mixer(h, gla_w_in[l // 2], gla_w_a2[l // 2], gla_b_a[l // 2], gla_w_out[l // 2])
        h = _rmsnorm_2(x, ffn_post_norm[l])
        x = x + 0.5 * _swiglu_2(h, ffn_post_w_gate[l], ffn_post_w_up[l], ffn_post_w_down[l])
    return _rmsnorm_2(x, final_norm)


def setup_inputs(seed=0):
    out = dict(first_inputs(seed))
    for name, value in second_inputs(seed + 1).items():
        if name != "x":
            out[name + "_2"] = value
    return out


def reference(
    x, c, ctx, c_ctx, ada_w, ada_b, norm_w, final_norm_w, ffn_w_gate, ffn_w_up, ffn_w_down,
    gqa_w_in, gqa_w_out, gqa_sinks, diff_w_in, diff_w_out, diff_lambda, diff_subln_w, hgrn_w_in,
    hgrn_w_out, hgrn_norm_w, hgrn_lower_bounds, mla_w_down, mla_q_norm_w, mla_kv_norm_w,
    mla_w_uq, mla_w_ukv, mla_w_out, ffn_pre_norm_2, ffn_pre_w_gate_2, ffn_pre_w_up_2,
    ffn_pre_w_down_2, mix_norm_2, ab_w_in_2, ab_w_out_2, gla_w_in_2, gla_w_a2_2, gla_b_a_2,
    gla_w_out_2, ffn_post_norm_2, ffn_post_w_gate_2, ffn_post_w_up_2, ffn_post_w_down_2,
    final_norm_2,
):
    x = first_block(
        x, c, ctx, c_ctx, ada_w, ada_b, norm_w, final_norm_w, ffn_w_gate, ffn_w_up, ffn_w_down,
        gqa_w_in, gqa_w_out, gqa_sinks, diff_w_in, diff_w_out, diff_lambda, diff_subln_w,
        hgrn_w_in, hgrn_w_out, hgrn_norm_w, hgrn_lower_bounds, mla_w_down, mla_q_norm_w,
        mla_kv_norm_w, mla_w_uq, mla_w_ukv, mla_w_out,
    )
    return second_block(
        x, ffn_pre_norm_2, ffn_pre_w_gate_2, ffn_pre_w_up_2, ffn_pre_w_down_2, mix_norm_2,
        ab_w_in_2, ab_w_out_2, gla_w_in_2, gla_w_a2_2, gla_b_a_2, gla_w_out_2, ffn_post_norm_2,
        ffn_post_w_gate_2, ffn_post_w_up_2, ffn_post_w_down_2, final_norm_2,
    )


_drawn_inputs = setup_inputs


def setup_inputs(seed=0):
    import zlib

    import numpy as np

    out = dict(_drawn_inputs(seed))
    spreads = {}
    factors = {'gqa_sinks': 8.0, 'diff_subln_w': 2.794, 'gla_b_a_2': 2.782}
    for name, (base, spread) in spreads.items():
        noise = np.random.default_rng([zlib.crc32(name.encode()), seed]).standard_normal(out[name].shape)
        drawn = base * np.exp(spread * noise) if base else spread * noise
        out[name] = jnp.asarray(drawn.astype(out[name].dtype))
    for name, factor in factors.items():
        out[name] = (out[name] * factor).astype(out[name].dtype)
    return out
```

```python
import math
from contextlib import ExitStack

import numpy as np

import concourse.bass as bass
from concourse import mybir

F32 = mybir.dt.float32
F32R = mybir.dt.float32r
U32 = mybir.dt.uint32
ACTF = mybir.ActivationFunctionType
ALU = mybir.AluOpType
AX = mybir.AxisListType

P = 128
S = 256
D = 1024
DT = D // P
FF = 2816
FT = FF // P
KH = FT // 2
NMOD = 9
EPS = 1e-6
NEG = -1e30
H_GQA, KV_GQA, HD = 16, 4, 64
H_DIFF = 8
LAMBDA_INIT = 0.8 - 0.6 * math.exp(-0.3 * 1)
H_RET, H_DIL = 4, 8
H_GLA, GLA_DV, GLA_C, GLA_R = 4, 256, 64, 16
ADA_SLOTS = 6
ADA_UNITS = 2 * NMOD * D // 256
ADA_TILES = NMOD * DT


def rope_rotation(dim, half, period):
    r = np.zeros((P, P), np.float32)
    for base in range(0, P, period):
        for block in range(0, dim, 2 * half):
            for j in range(half):
                lo, hi = base + block + j, base + block + half + j
                r[hi, lo] = -1.0
                r[lo, hi] = 1.0
    return r


def rope_angles(kind):
    pos = np.arange(S, dtype=np.float32)
    if kind == "axial":
        inv = (10000.0 ** (-np.arange(0, 32, 2, dtype=np.float32) / 32)).astype(np.float32)
        row, col = np.floor(pos / 64), pos % 64
        ang = np.concatenate([row[:, None] * inv, row[:, None] * inv, col[:, None] * inv, col[:, None] * inv], -1)
        return np.tile(ang, (1, 2)).T
    if kind == "ret":
        inv = (10000.0 ** (-np.linspace(0.0, 1.0, 64, dtype=np.float32))).astype(np.float32)
        ang = pos[:, None] * inv
        return np.concatenate([ang, ang], -1).T
    inv = (500000.0 ** (-np.arange(0, 16, 2, dtype=np.float32) / 16)).astype(np.float32)
    ang = pos[:, None] * inv
    one = np.concatenate([ang, ang, np.zeros((S, 48), np.float32)], -1)
    return np.tile(one, (1, 2)).T


def constants():
    c = {}
    i, j = np.arange(S)[:, None], np.arange(S)[None, :]
    for kind in ("axial", "ret", "dil"):
        ang = rope_angles(kind).astype(np.float32)
        c[f"{kind}_cos"], c[f"{kind}_sin"] = np.cos(ang), np.sin(ang)
    c["axial_rot"] = rope_rotation(64, 16, 64)
    c["ret_rot"] = rope_rotation(128, 64, 128)
    c["dil_rot"] = rope_rotation(16, 8, 64)
    swap = np.zeros((P, P), np.float32)
    swap[np.arange(P), (np.arange(P) + 64) % P] = 1.0
    c["swap"] = swap
    c["ident"] = np.eye(P, dtype=np.float32)
    band = np.where(np.abs(i - j) <= 128, 0.0, NEG)
    full = np.concatenate([band, np.zeros((S, S))], 1)
    c["gqa_mask"] = full.reshape(2, P, 2 * S).transpose(1, 0, 2)
    dist = i - j
    count = np.zeros((S, S))
    for window, dil in ((128, 1), (512, 4), (2048, 16)):
        count += (dist >= 0) & (dist <= window) & (dist % dil == 0)
    c["dil_mask"] = np.where(count > 0, np.log(np.maximum(count, 1)) * 8.0, NEG).reshape(2, P, S).transpose(1, 0, 2)
    decay = np.zeros((P, H_RET, 384))
    for h in range(H_RET):
        log_g = np.log(1.0 - 2.0 ** (-5.0 - h))
        m = np.where(dist >= 0, np.exp(log_g * np.maximum(dist, 0)), 0.0).T * 128 ** -0.5
        decay[:, h, 0:256] = m[0:128, :]
        decay[:, h, 256:384] = m[128:256, 128:256]
    c["ret_mask"] = decay
    a, b = np.arange(P)[:, None], np.arange(P)[None, :]
    inside = (a // GLA_C == b // GLA_C) & (a <= b)
    c["gla_sum"] = inside / 16.0
    c["gla_mask"] = np.tile(inside, (1, 2)).astype(np.uint32)
    return {k: np.ascontiguousarray(v.astype(v.dtype if v.dtype == np.uint32 else np.float32)) for k, v in c.items()}


COLS = {"norm_w": 48, "final_norm_w": 8, "ada_b": 144, "pre2": 16, "mix2": 16, "post2": 16, "final2": 8,
        "subln": 1, "sinks": 16}
COL_AT = dict(zip(COLS, np.cumsum([0] + list(COLS.values()))[:-1].tolist()))
N_COLS = sum(COLS.values())


class Gemm:

    def __init__(self, kind, iters, k, t, src, rhs, ready, dst=None, gate=None, hid0=0):
        self.kind, self.iters, self.k, self.t, self.src, self.rhs, self.ready = kind, iters, k, t, src, rhs, ready
        self.dst, self.gate, self.hid0 = dst, gate, hid0
        self.p0 = self.e0 = self.r0 = 0


def build(nc, A):
    ctx = ExitStack()
    with ctx:
        def sem(name):
            return ctx.enter_context(nc.semaphore(name))

        def sb(name, shape, dt=F32, stack=ctx):
            return stack.enter_context(nc.sbuf_tensor(name, shape, dt))

        xT = sb("xT", [P, DT, 2 * S])
        XH = sb("XH", [P, DT, 2 * S], F32R)
        XL = sb("XL", [P, DT, 2 * S], F32R)
        raw = sb("raw", [P, 2, KH, 256])
        WH = sb("WH", [P, 4, KH, P], F32R)
        WL = sb("WL", [P, 4, KH, P], F32R)
        mods = sb("mods", [P, 2 * ADA_TILES, 2])
        scaleA = sb("scaleA", [P, 2, 3, DT, 2])
        gates = sb("gates", [P, 2, 3, DT, 2])
        halves = sb("halves", [P, 2, DT])
        cols = sb("cols", [P, N_COLS])
        csil = sb("csil", [P, DT, 2])
        ones_d = sb("ones_d", [P, P])
        ones_e = sb("ones_e", [P, P])
        ones_1 = sb("ones_1", [P, P])
        ident = sb("ident", [P, P])
        sq = sb("sq", [P, 2, 2 * S])
        rstd = sb("rstd", [P, 2 * S])
        tn = sb("tn", [P, 2, 2 * S])
        sg = sb("sg", [P, 2, 2 * S])
        hf = tn
        eps = sb("eps", [P, 1])
        token = sb("token", [P, 16])

        def arena(*specs):
            stack = ExitStack()
            got = [sb(n, s, d, stack) for n, s, d in specs]
            stack.close()
            return got

        (ada_ring,) = arena(("ada_ring", [P, ADA_SLOTS, DT, 256], F32))
        HH, HL = arena(("HH", [P, FT, 2 * S], F32R), ("HL", [P, FT, 2 * S], F32R))
        att_tiles = lambda n: [(f"{n}_s", [P, 2, 2, 512], F32), (f"{n}_p", [P, 2, 512], F32),
                               (f"{n}_pt", [P, 2, 512], F32), (f"{n}_small", [P, 64, 8], F32)]
        rope_t = lambda n: [(f"{n}_cos", [P, S], F32), (f"{n}_sin", [P, S], F32), (f"{n}_rot", [P, P], F32)]
        (g_proj, g_ks, g_vn, g_mask, g_swap, g_rt, g_nsink, g_cos, g_sin, g_rot, *g_att) = arena(
            ("g_proj", [P, 12, 2 * S], F32), ("g_ks", [P, 2, 2 * S], F32), ("g_vn", [P, 4, 256], F32),
            ("g_mask", [P, 2, 512], F32), ("g_swap", [P, P], F32), ("g_rt", [P, 2, S], F32),
            ("g_nsink", [P, 16], F32), *rope_t("g"), *att_tiles("g"))
        (d_q, d_kv, d_vn, d_o, d_rt, d_lam, d_lw, d_zero, d_cos, d_sin, d_rot, *d_att) = arena(
            ("d_q", [P, 8, S], F32), ("d_kv", [P, 16, 2 * S], F32), ("d_vn", [P, 4, 1024], F32),
            ("d_o", [P, 8, S], F32), ("d_rt", [P, 2, S], F32), ("d_lam", [64, 4], F32), ("d_lw", [P, 16], F32),
            ("d_zero", [P, 1], F32), *rope_t("d"), *att_tiles("d"))
        (r_proj, r_vn, r_o, r_rt, r_mask, r_dmask, r_sm, r_cos, r_sin, r_rot, l_cos, l_sin, l_rot, *l_att) = arena(
            ("r_proj", [P, 28, S], F32), ("r_vn", [P, 2, 1024], F32), ("r_o", [P, 4, S], F32),
            ("r_rt", [P, 2, S], F32), ("r_mask", [P, 4, 384], F32), ("r_dmask", [P, 2, S], F32),
            ("r_sm", [P, 2, 384], F32), *rope_t("r"), *rope_t("l"), *att_tiles("l"))
        (a_proj, a_vn, a_kn, a_o, a_la, a_zm, a_b, a_el, a_st, a_sm, a_sum, a_mask, a_low, a_w2, a_ba,
         a_wr, a_wh, a_wl) = arena(
            ("a_proj", [P, 24, S], F32), ("a_vn", [P, 2, 1024], F32), ("a_kn", [P, 2, 512], F32),
            ("a_o", [P, 8, S], F32), ("a_la", [P, 2, 512], F32), ("a_zm", [P, 2, 512], F32),
            ("a_b", [P, 4, S], F32), ("a_el", [P, 4, S], F32),
            ("a_st", [P, 2, 3, S], F32), ("a_sm", [P, 2, S], F32), ("a_sum", [P, P], F32), ("a_mask", [P, S], U32),
            ("a_low", [GLA_R, S], F32), ("a_w2", [GLA_R, 512], F32), ("a_ba", [1, 512], F32),
            ("a_wr", [P, DT, P], F32), ("a_wh", [P, DT, P], F32R), ("a_wl", [P, DT, P], F32R))
        a_eb = a_zm[:, :, :].rearrange("p a (h n) -> p (a h) n", h=2)
        a_en = a_b

        bank = [ctx.enter_context(nc.psum_tensor(f"bank{i}", [P, 512], F32)) for i in range(8)]

        in_loaded = sem("in_loaded")
        raw_ready = [sem("raw_ready0"), sem("raw_ready1")]
        ada_ready = [sem(f"ada_ready{n}") for n in range(ADA_SLOTS)]
        ada_used = sem("ada_used")
        ada_out = sem("ada_out")
        csil_ready = sem("csil_ready")
        mods_ready = sem("mods_ready")
        setup_done = sem("setup_done")
        h_done = sem("h_done")
        split_done = sem("split_done")
        piece_done = sem("piece_done")
        act_bank = sem("act_bank")
        dve_bank = sem("dve_bank")
        res_done = sem("res_done")
        hid_high = sem("hid_high")
        hid_low = sem("hid_low")
        sq_ready = sem("sq_ready")
        sq_sum = sem("sq_sum")
        n_root = sem("n_root")
        n_mul = sem("n_mul")
        n_high = sem("n_high")
        n_low = sem("n_low")
        dve_self = sem("dve_self")
        act_self = sem("act_self")
        tables = sem("tables")
        arena_free = sem("arena_free")
        out_done = sem("out_done")

        def rows(w):
            return w.rearrange("(k p) n -> p k n", p=P)

        gemms = []
        state = {"p0": 0, "e0": 0, "r0": 0, "norms": 0, "hid": 0, "split": 0}
        steps = []

        def add(g):
            g.p0, g.e0, g.r0 = state["p0"], state["e0"], state["r0"]
            state["p0"] += 4 * g.iters
            if g.kind == "res":
                state["r0"] += (2 if g.k == KH else 4) * g.iters
            else:
                state["e0"] += g.iters
            gemms.append(g)
            steps.append(("gemm", g))
            return g

        def x_in(k, t):
            return XH[:, k, 0:t], XL[:, k, 0:t]

        def hid_in(k, t):
            return HH[:, k, 0:t], HL[:, k, 0:t]

        def norm(t, weight, shift=None, mode="split"):
            n = dict(i=state["norms"], t=t, weight=weight, shift=shift, mode=mode, h0=state["split"],
                     last=gemms[-1] if gemms and steps[-1][0] != "norm" else None)
            state["norms"] += 1
            state["split"] += DT if mode == "split" else 0
            steps.append(("norm", n))
            return n

        def ada_norm(l, n, t):
            return norm(t, lambda k, half: scaleA[:, l, n, k, half:half + 1],
                        lambda k, half: mods[:, l * ADA_TILES + 3 * n * DT + k, half:half + 1])

        def plain_norm(name, l, mode="split"):
            at = COL_AT[name] + DT * l
            return norm(S, lambda k, half: cols[:, at + k:at + k + 1], None, mode)

        def ffn(n, t, gate, wg, wu, wd):
            wg, wu, wd = rows(wg), rows(wu), rows(wd)
            up = add(Gemm("up", KH, DT, t, lambda i, a: (wg, wu)[a][:, :, bass.ds(i * 256, 256)],
                          x_in, lambda k: (n_low, n["h0"] + k + 1), hid0=state["hid"]))
            add(Gemm("res", 4, KH, t, lambda i, a: wd[:, KH * a:KH * a + KH, bass.ds(i * 256, 256)],
                     hid_in, lambda k: (hid_low, up.hid0 + k + 3), gate=gate))
            state["hid"] += FT
            steps.append(("ffn_end", None))

        def proj(n, w, iters, t, dst, col0=0):
            w = rows(w)
            return add(Gemm("proj", iters, DT, t, lambda i, a: w[:, :, bass.ds(i * 512 + (col0 + 256 * a), 256)],
                            x_in, lambda k: (n_low, n["h0"] + k + 1), dst=dst))

        def out_proj(w, t, ready, gate):
            w = rows(w)
            return add(Gemm("res", 2, DT, t, lambda i, a: w[:, :, bass.ds(i * 512 + 256 * a, 256)],
                            x_in, ready, gate=gate))

        gate1 = lambda l, n: (lambda d, half: gates[:, l, n, bass.ds(d, 1), half:half + 1].rearrange("p o h -> p (o h)"))
        gate2 = lambda n: (lambda d, half: halves[:, n, bass.ds(d, 1)])
        mix_out = [sem(f"mix_out{m}") for m in range(4)]
        dil_out = sem("dil_out")
        mix_ready = [lambda k: (mix_out[0], k + 1), lambda k: (mix_out[1], k + 1),
                     lambda k: (mix_out[2], k + 1) if k < 4 else (dil_out, k - 3), lambda k: (mix_out[3], k + 1)]

        def mixer(m, n, projs, w_out, t, gate):
            for w, iters, tt, dst, col0 in projs:
                proj(n, w, iters, tt, dst, col0)
            steps.append(("mix", m))
            out_proj(w_out, t, mix_ready[m], gate)

        for l in range(2):
            ffn(ada_norm(l, 0, 2 * S), 2 * S, gate1(l, 0), A["ffn_w_gate"][l, 0], A["ffn_w_up"][l, 0], A["ffn_w_down"][l, 0])
            if l == 0:
                mixer(0, ada_norm(0, 1, 2 * S), [(A["gqa_w_in"][0], 3, 2 * S, g_proj, 0)], A["gqa_w_out"][0], 2 * S, gate1(0, 1))
            else:
                mixer(1, ada_norm(1, 1, 2 * S), [(A["diff_w_in"][0], 2, S, d_q, 0), (A["diff_w_in"][0], 4, 2 * S, d_kv, 1024)],
                      A["diff_w_out"][0], S, gate1(1, 1))
            t = 2 * S if l == 0 else S
            ffn(ada_norm(l, 2, t), t, gate1(l, 2), A["ffn_w_gate"][l, 1], A["ffn_w_up"][l, 1], A["ffn_w_down"][l, 1])
        plain_norm("final_norm_w", 0, "replace")
        for l in range(2):
            n = plain_norm("pre2", l)
            ffn(n, S, gate2(0), A["ffn_pre_w_gate_2"][l], A["ffn_pre_w_up_2"][l], A["ffn_pre_w_down_2"][l])
            n = plain_norm("mix2", l)
            if l == 0:
                mixer(2, n, [(A["ab_w_in_2"][0], 7, S, r_proj, 0)], A["ab_w_out_2"][0], S, gate2(1))
            else:
                mixer(3, n, [(A["gla_w_in_2"][0], 6, S, a_proj, 0)], A["gla_w_out_2"][0], S, gate2(1))
            n = plain_norm("post2", l)
            ffn(n, S, gate2(0), A["ffn_post_w_gate_2"][l], A["ffn_post_w_up_2"][l], A["ffn_post_w_down_2"][l])
        plain_norm("final2", 0, "out")
        following = {id(g): nxt for g, nxt in zip(gemms, gemms[1:] + [None])}

        def res_tile(g, i, b):
            return i * 2 + b // 2 if g.k == KH else i * 4 + (2 * (b % 2) + b // 2)

        def x_ready(n, k):
            g = n["last"]
            if g.k == KH:
                return g.r0 + k + 3
            i, rest = divmod(k, 4)
            return g.r0 + 4 * i + 2 * (rest % 2) + rest // 2 + 3

        def gqa_jobs():
            jobs = []
            for h in range(H_GQA):
                kv, qb = h // 4, 64 * (h % 2)
                ksrc = g_proj[:, 8 + kv // 2, :] if 64 * (kv % 2) == qb else g_ks[:, kv // 2, :]
                for t in range(4):
                    keys = (0, 512) if t < 2 else (256, 512)
                    jobs.append(dict(
                        maps=[(g_proj[qb:qb + 64, h // 2, t * P:(t + 1) * P], ksrc[qb:qb + 64, keys[0]:keys[1]])],
                        nk=keys[1] - keys[0], mask=g_mask[:, t, :] if t < 2 else g_mask[:, 0, 256:512], head=h,
                        v=[g_vn[:, keys[0] // P + j, kv * 64:kv * 64 + 64] for j in range((keys[1] - keys[0]) // P)],
                        o=h // 2, base=qb, rows=64, q0=t * P, last=(h % 2 == 1 and t == 3), first=(h % 2 == 0 and t == 0)))
            return jobs

        def diff_jobs():
            jobs = []
            for h in range(H_DIFF):
                for t in range(2):
                    jobs.append(dict(
                        maps=[(d_q[64 * m:64 * m + 64, h, t * P:(t + 1) * P], d_kv[64 * m:64 * m + 64, h, :]) for m in range(2)],
                        nk=512, mask=d_zero[:, :].to_broadcast([P, 512]), head=None, v=[d_vn[:, j, h * P:(h + 1) * P] for j in range(4)],
                        o=h, base=0, rows=P, q0=t * P, last=t == 1, first=t == 0))
            return jobs

        def dil_jobs():
            jobs = []
            for h in range(H_DIL):
                qb = 64 * (h % 2)
                for t in range(2):
                    jobs.append(dict(
                        maps=[(r_proj[qb:qb + 64, 16 + h // 2, t * P:(t + 1) * P], r_proj[qb:qb + 64, 20 + h // 2, :])],
                        nk=256, mask=r_dmask[:, t, :], head=None,
                        v=[r_vn[:, j, 512 + h * 64:512 + h * 64 + 64] for j in range(2)],
                        o=h // 2, base=qb, rows=64, q0=t * P, last=(h % 2 == 1 and t == 1), first=(h % 2 == 0 and t == 0)))
            return jobs

        class Att:
            def __init__(self, name, jobs, tiles, cols_o, sink=False, keep=None, x0=0, out=None):
                self.jobs, (self.s, self.p, self.pt, self.small) = jobs, tiles
                self.cols, self.sink, self.keep, self.x0, self.out = cols_o, sink, keep, x0, out
                self.scores = sem(f"{name}_scores")
                self.max = sem(f"{name}_max")
                self.exp = sem(f"{name}_exp")
                self.norm = sem(f"{name}_norm")
                self.turned = sem(f"{name}_turned")
                self.pt_ready = sem(f"{name}_pt_ready")
                self.o_done = sem(f"{name}_o_done")
                self.o_high = sem(f"{name}_o_high")
                self.o_free = out if out is not None else sem(f"{name}_o_free")

        gqa = Att("gqa", gqa_jobs(), g_att, 512, sink=True, out=mix_out[0])
        dif = Att("dif", diff_jobs(), d_att, 256, keep=d_o)
        dil = Att("dil", dil_jobs(), l_att, 256, x0=4, out=dil_out)

        ropes = {
            0: [(g_proj, n, g_rot, g_cos, g_sin) for n in (8, 9, 0, 1, 2, 3, 4, 5, 6, 7)],
            1: [(d_kv, n, d_rot, d_cos, d_sin) for n in range(8)] + [(d_q, n, d_rot, d_cos, d_sin) for n in range(8)],
            2: [(r_proj, n, r_rot, r_cos, r_sin) for n in range(8)] + [(r_proj, n, l_rot, l_cos, l_sin) for n in range(16, 24)],
        }
        rope_tmp = {0: g_rt, 1: d_rt, 2: r_rt}
        rot_done = [sem(f"rot_done{m}") for m in range(3)]
        rot_read = [sem(f"rot_read{m}") for m in range(3)]
        roped = [sem(f"roped{m}") for m in range(3)]
        v_turned = [sem(f"v_turned{m}") for m in range(4)]
        v_stored = [sem(f"v_stored{m}") for m in range(4)]
        kswap = sem("kswap")
        kswap_stored = sem("kswap_stored")

        def v_groups(m):
            out = []
            if m == 0:
                for i in range(2):
                    out.append(([g_proj[:, 10 + i, t * P:(t + 1) * P] for t in range(4)], g_vn[:, :, i * P:(i + 1) * P]))
            if m == 1:
                for i in range(8):
                    out.append(([d_kv[:, 8 + i, t * P:(t + 1) * P] for t in range(4)], d_vn[:, :, i * P:(i + 1) * P]))
            if m == 2:
                for t in range(2):
                    for tile0, c0 in ((8, 0), (24, 512)):
                        out.append(([r_proj[:, tile0 + i, t * P:(t + 1) * P] for i in range(4)],
                                    r_vn[:, t, c0:c0 + 512].rearrange("p (g n) -> p g n", g=4)))
            if m == 3:
                for t in range(2):
                    for c0 in (0, 4):
                        out.append(([a_proj[:, 8 + c0 + i, t * P:(t + 1) * P] for i in range(4)],
                                    a_vn[:, t, c0 * P:c0 * P + 512].rearrange("p (g n) -> p g n", g=4)))
            return out

        def stat_of(h, b):
            if h.joined:
                return bank[b][:, 0:S].rearrange("p (o n) -> p o n", o=1).to_broadcast([P, 2, S])
            return bank[b][:, :].rearrange("p (e n) -> p e n", e=2)

        class HeadNorm:
            def __init__(self, name, data, chunks, joined, centre, gate, x0, out, scale=None):
                self.data, self.chunks, self.joined, self.centre = data, chunks, joined, centre
                self.gate, self.x0, self.out, self.scale = gate, x0, out, scale
                self.mean = sem(f"{name}_mean")
                self.centred = sem(f"{name}_centred")
                self.squared = sem(f"{name}_squared")
                self.var = sem(f"{name}_var")
                self.root = sem(f"{name}_root")
                self.gated = sem(f"{name}_gated")
                self.high = sem(f"{name}_high")
                self.sig = sem(f"{name}_sig")
        hn = {1: HeadNorm("dhn", d_o, 4, False, False, None, 0, mix_out[1], scale=d_lw),
              2: HeadNorm("rhn", r_o, 2, False, True, (r_proj, 12), 0, mix_out[2]),
              3: HeadNorm("ahn", a_o, 4, True, True, (a_proj, 16), 0, mix_out[3])}
        mix_in = [sem(f"mix_in{m}") for m in range(4)]
        ret_scores, ret_masked, ret_o = sem("ret_scores"), sem("ret_masked"), sem("ret_o")
        lam_prod, lam_sum, lam_exp, lam_done = sem("lam_prod"), sem("lam_sum"), sem("lam_exp"), sem("lam_done")
        gs = {n: sem("gla_" + n) for n in ("wsplit", "low", "lowc", "z", "znabs", "ln", "la", "b", "bs", "eb", "qt", "kt", "bd", "el",
                                           "ko", "kturn", "kstore", "sc", "sm", "kv", "st", "zero", "o")}

        last_proj = {}
        seen = None
        for kind, what in steps:
            if kind == "gemm":
                seen = what
            if kind == "mix":
                last_proj[what] = seen

        consts = {0: [(g_cos, "axial_cos"), (g_sin, "axial_sin"), (g_rot, "axial_rot"), (g_swap, "swap"), (g_mask, "gqa_mask")],
                  1: [(d_cos, "axial_cos"), (d_sin, "axial_sin"), (d_rot, "axial_rot"), (d_lam, "diff_lambda")],
                  2: [(r_cos, "ret_cos"), (r_sin, "ret_sin"), (r_rot, "ret_rot"), (l_cos, "dil_cos"), (l_sin, "dil_sin"),
                      (l_rot, "dil_rot"), (r_mask, "ret_mask"), (r_dmask, "dil_mask")],
                  3: [(a_sum, "gla_sum"), (a_mask, "gla_mask"), (a_w2, "gla_w_a2_2"), (a_ba, "gla_b_a_2"), (a_wr, None)]}
        tables_at = {}
        total = 0
        for m in range(4):
            total += 16 * len(consts[m])
            tables_at[m] = total
        turn_before_mix = {0: 2, 1: 5, 2: 8, 3: 11}

        block = ctx.enter_context(nc.Block())

        @block.sync
        def _(sp):
            ada = A["ada_w"].rearrange("l (k p) n -> p l k n", p=P)
            for l in range(2):
                def load_ada(i, first):
                    for s in range(ADA_SLOTS):
                        if not first:
                            sp.wait_ge(ada_used, i * ADA_SLOTS + (l * ADA_UNITS // 2 - ADA_SLOTS + s + 1))
                        sp.dma_start(ada_ring[:, s], ada[:, l, :, bass.ds(i * (256 * ADA_SLOTS) + 256 * s, 256)]).then_inc(ada_ready[s], 16)
                load_ada(0, l == 0)
                with sp.Fori(1, ADA_UNITS // 2 // ADA_SLOTS) as i:
                    load_ada(i, False)

            for g in gemms:
                def load(i):
                    it = g.p0 // 4 + i
                    for a in range(2):
                        if g.p0 > 0 or not isinstance(i, int):
                            sp.wait_ge(split_done, 4 * it - 1 + a)
                        sp.dma_start(raw[:, a, 0:g.k, :], g.src(i, a)).then_inc(raw_ready[a], 16)
                load(0)
                with sp.Fori(1, g.iters) as i:
                    load(i)

        @block.gpsimd
        def _(pool):
            pool.dma_start(cols[:, :], A["cols"]).then_inc(in_loaded, 16)
            pool.dma_start(csil[:, :, :], A["c_cols"]).then_inc(in_loaded, 16)
            pool.dma_start(ident[:, :], A["ident"]).then_inc(in_loaded, 16)
            pool.dma_start(xT[:, :, :], A["xT"].rearrange("(k p) n -> p k n", p=P)).then_inc(in_loaded, 16)
            for m in range(4):
                pool.wait_ge(arena_free, turn_before_mix[m])
                for dst, name in consts[m]:
                    if name is None:
                        pool.wait_ge(gs["zero"], 1)
                        pool.dma_start(a_wr[:, :, 0:GLA_R], rows(A["gla_w_in_2"][0])[:, :, 3072:3072 + GLA_R]).then_inc(tables, 16)
                    else:
                        src = A[name]
                        d = dst[tuple([slice(None)] * len(dst.shape))]
                        pool.dma_start(d, src).then_inc(tables, 16)
            pool.wait_ge(tables, tables_at[3])

        @block.tensor
        def _(pe):
            pe.wait_ge(csil_ready, 1)
            def ada_turn(i, first):
                for u in range(ADA_SLOTS):
                    pe.wait_ge(ada_ready[u], 16 * i + 16)
                    if u % 3 == 0 and not first:
                        pe.wait_ge(ada_out, 2 * i + (u // 3 - 1))
                    for half in range(2):
                        c0 = 2 * (2 * (u % 3) + half)
                        for k in range(DT):
                            last = nc.tensor.matmul(bank[6 + u // 3][:, c0:c0 + 2], ada_ring[:, u, k, half * P:(half + 1) * P],
                                                    csil[:, k, :], start=(k == 0), stop=(k == DT - 1))
                    last.then_inc(ada_used, 1)
            ada_turn(0, True)
            with pe.Fori(1, ADA_UNITS // ADA_SLOTS) as i:
                ada_turn(i, False)
            pe.wait_ge(ada_out, ADA_UNITS // 3)

            def piece(g, i, b, first):
                a = b % 2
                pe.wait_ge(split_done, g.p0 + 4 * i + (b + 1))
                down = g.k == KH
                if g.kind == "res":
                    out = bank[4 + (b // 2 if down else b % 2)]
                    if not down or a == 0:
                        r = g.r0 + (2 * i + b // 2 if down else 4 * i + b)
                        pe.wait_ge(res_done, r + 1)
                else:
                    out = bank[b]
                    pe.wait_ge(dve_bank if a else act_bank, 2 * (g.e0 + i) + (1 + b // 2))
                for k in range(g.k):
                    kk = k + (KH * a if down else 0)
                    if first and (b < 2 if down else b == 0):
                        pe.wait_ge(*g.ready(kk))
                    high, low = g.rhs(kk, g.t)
                    start = k == 0 and (a == 0 or not down)
                    stop = k == g.k - 1 and (a == 1 or not down)
                    o = out[:, 0:g.t]
                    nc.tensor.matmul(o, WH[:, b, k, :], high, start=start, stop=False)
                    nc.tensor.matmul(o, WH[:, b, k, :], low, start=False, stop=False)
                    last = nc.tensor.matmul(o, WL[:, b, k, :], high, start=False, stop=stop)
                last.then_inc(piece_done, 1)

            def gemm(g):
                for b in range(4):
                    piece(g, 0, b, True)
                with pe.Fori(1, g.iters) as i:
                    for b in range(4):
                        piece(g, i, b, False)

            def norm_sums(n):
                for k in range(DT):
                    pe.wait_ge(sq_ready, DT * n["i"] + k + 1)
                    nc.tensor.matmul(bank[6][:, 0:n["t"]], ones_d[:, :], sq[:, k % 2, 0:n["t"]], start=(k == 0),
                                     stop=(k == DT - 1)).then_inc(sq_sum, 1)

            def banks_free(g):
                pe.wait_ge(act_bank, 2 * (g.e0 + g.iters) + 2)
                pe.wait_ge(dve_bank, 2 * (g.e0 + g.iters) + 2)
                pe.wait_ge(res_done, g.r0 + 2)

            def rotate(m):
                for n, (src, tile, rot, _, _) in enumerate(ropes[m]):
                    if n >= 4:
                        pe.wait_ge(rot_read[m], n - 3)
                    nc.tensor.matmul(bank[n % 4][:, 0:S], rot[:, :], src[:, tile, 0:S], start=True,
                                     stop=True).then_inc(rot_done[m], 1)

            def turn_v(m):
                for n, (blocks, _) in enumerate(v_groups(m)):
                    if n >= 2:
                        pe.wait_ge(v_stored[m], n - 1)
                    for j, blk in enumerate(blocks):
                        last = nc.tensor.transpose(bank[6 + n % 2][:, j * P:(j + 1) * P], blk, ident[:, :])
                    last.then_inc(v_turned[m], 1)

            def attention(a):
                jobs = a.jobs
                for s in range(len(jobs) + 2):
                    if s < len(jobs):
                        j = jobs[s]
                        if s >= 2:
                            pe.wait_ge(a.max, len(j["maps"]) * (s - 1))
                        for m, (q, k) in enumerate(j["maps"]):
                            nc.tensor.matmul(bank[2 * (s % 2) + m][:, 0:j["nk"]], q, k, start=True,
                                             stop=True).then_inc(a.scores, 1)
                    if 1 <= s <= len(jobs):
                        j = jobs[s - 1]
                        pe.wait_ge(a.norm, s)
                        if s >= 3:
                            pe.wait_ge(a.pt_ready, s - 2)
                        for c in range(j["nk"] // P):
                            last = nc.tensor.transpose(bank[4 + (s - 1) % 2][:, c * P:(c + 1) * P],
                                                       a.p[:, (s - 1) % 2, c * P:(c + 1) * P], ident[:, :])
                        last.then_inc(a.turned, 1)
                    if s >= 2:
                        j = jobs[s - 2]
                        pe.wait_ge(a.pt_ready, s - 1)
                        if j["first"] and j["o"] >= 2:
                            pe.wait_ge(a.o_free, j["o"] - 1)
                        n = j["nk"] // P
                        for c in range(n):
                            last = nc.tensor.matmul(
                                bank[6 + j["o"] % 2][j["base"]:j["base"] + j["rows"], j["q0"]:j["q0"] + P], j["v"][c],
                                a.pt[:, s % 2, c * P:(c + 1) * P], start=(c == 0), stop=(c == n - 1))
                        if j["last"]:
                            last.then_inc(a.o_done, 1)
                pe.wait_ge(a.o_free, jobs[-1]["o"] + 1)

            def head_norm(h):
                w = S if h.joined else 2 * S
                def stat(c, src, b, done):
                    if h.joined:
                        for e in range(2):
                            last = nc.tensor.matmul(bank[b][:, 0:S], ones_e[:, :], src[:, e, :], start=(e == 0), stop=(e == 1))
                    else:
                        last = nc.tensor.matmul(bank[b][:, 0:w], ones_e[:, :], src, start=True, stop=True)
                    last.then_inc(done, 1)
                for c in range(h.chunks):
                    d = h.data[:, 2 * c:2 * c + 2, :]
                    if h.centre:
                        if c >= 2:
                            pe.wait_ge(h.centred, c - 1)
                        stat(c, d, c % 2, h.mean)
                    pe.wait_ge(h.squared, c + 1)
                    if c >= 2:
                        pe.wait_ge(h.gated, c - 1)
                    stat(c, sq[:, c % 2, :].rearrange("p (e n) -> p e n", e=2), 2 + c % 2, h.var)

            def mix0():
                pe.wait_ge(tables, tables_at[0])
                banks_free(last_proj[0])
                rotate(0)
                turn_v(0)
                for i in range(2):
                    pe.wait_ge(roped[0], i + 1)
                    nc.tensor.matmul(bank[4 + i][:, :], g_swap[:, :], g_proj[:, 8 + i, :], start=True, stop=True).then_inc(kswap, 1)
                pe.wait_ge(kswap_stored, 2)
                pe.wait_ge(v_stored[0], 2)
                pe.wait_ge(roped[0], len(ropes[0]))
                attention(gqa)

            def mix1():
                pe.wait_ge(tables, tables_at[1])
                banks_free(last_proj[1])
                pe.wait_ge(lam_prod, 1)
                nc.tensor.matmul(bank[4][:, 0:2], ones_1[0:64, :], d_lw[0:64, 8:10], start=True, stop=True).then_inc(lam_sum, 1)
                rotate(1)
                turn_v(1)
                pe.wait_ge(v_stored[1], 8)
                pe.wait_ge(lam_exp, 1)
                pe.wait_ge(roped[1], len(ropes[1]))
                attention(dif)
                head_norm(hn[1])

            def mix2():
                pe.wait_ge(tables, tables_at[2])
                banks_free(last_proj[2])
                rotate(2)
                turn_v(2)
                pe.wait_ge(v_stored[2], 4)
                pe.wait_ge(roped[2], len(ropes[2]))
                for h in range(H_RET):
                    if h >= 2:
                        pe.wait_ge(ret_masked, h - 1)
                    q, k = r_proj[:, h, :], r_proj[:, 4 + h, :]
                    nc.tensor.matmul(bank[h % 2][:, 0:256], k[:, 0:P], q[:, 0:256], start=True, stop=True)
                    nc.tensor.matmul(bank[h % 2][:, 256:384], k[:, P:256], q[:, P:256], start=True, stop=True).then_inc(ret_scores, 1)
                    pe.wait_ge(ret_masked, h + 1)
                    if h >= 2:
                        pe.wait_ge(mix_in[2], h - 1)
                    o = bank[2 + h % 2]
                    nc.tensor.matmul(o[:, 0:256], r_vn[:, 0, h * P:(h + 1) * P], r_sm[:, h % 2, 0:256], start=True, stop=False)
                    nc.tensor.matmul(o[:, P:256], r_vn[:, 1, h * P:(h + 1) * P], r_sm[:, h % 2, 256:384], start=False,
                                     stop=True).then_inc(ret_o, 1)
                pe.wait_ge(mix_in[2], H_RET)
                head_norm(hn[2])
                pe.wait_ge(hn[2].gated, 2)
                attention(dil)

            def mix3():
                pe.wait_ge(tables, tables_at[3])
                banks_free(last_proj[3])
                pe.wait_ge(gs["wsplit"], 1)
                for k in range(DT):
                    nc.tensor.matmul(bank[4][:, 0:S], a_wh[:, k, :], XH[:, k, 0:S], start=(k == 0), stop=False)
                    nc.tensor.matmul(bank[4][:, 0:S], a_wh[:, k, :], XL[:, k, 0:S], start=False, stop=False)
                    last = nc.tensor.matmul(bank[4][:, 0:S], a_wl[:, k, :], XH[:, k, 0:S], start=False, stop=(k == DT - 1))
                last.then_inc(gs["low"], 1)
                pe.wait_ge(gs["lowc"], 1)
                for t in range(2):
                    nc.tensor.matmul(bank[t][:, :], a_low[:, t * P:(t + 1) * P], a_w2[:, :], start=True, stop=False)
                    nc.tensor.matmul(bank[t][:, :], ones_1[0:1, :], a_ba[:, :], start=False, stop=True).then_inc(gs["z"], 1)
                turn_v(3)
                pe.wait_ge(gs["la"], 1)
                for h in range(H_GLA):
                    for t in range(2):
                        c0 = (h % 2) * S + t * P
                        last = nc.tensor.matmul(bank[2 + h // 2][:, c0:c0 + P], a_la[:, t, h * P:(h + 1) * P], a_sum[:, :],
                                                start=True, stop=True)
                last.then_inc(gs["b"], 1)
                pe.wait_ge(v_stored[3], 4)
                pe.wait_ge(gs["ko"], 1)
                for t in range(2):
                    for h in range(H_GLA):
                        last = nc.tensor.transpose(bank[6 + t][:, h * P:(h + 1) * P], a_el[:, h, t * P:(t + 1) * P], ident[:, :])
                    last.then_inc(gs["kturn"], 1)
                pe.wait_ge(gs["kstore"], 2)
                for h in range(H_GLA):
                    if h >= 2:
                        pe.wait_ge(gs["sm"], h - 1)
                    pe.wait_ge(gs["bs"], 1)
                    pe.wait_ge(gs["qt"], 1)
                    pe.wait_ge(gs["kt"], 1)
                    for t in range(2):
                        last = nc.tensor.matmul(bank[h % 2][:, t * P:(t + 1) * P], a_proj[:, 4 + h, t * P:(t + 1) * P],
                                                a_proj[:, h, t * P:(t + 1) * P], start=True, stop=True)
                    last.then_inc(gs["sc"], 1)
                    if h >= 1:
                        pe.wait_ge(gs["st"], 3 * h)
                    for n in range(3):
                        b0 = (n % 2) * 64
                        nc.tensor.matmul(bank[2 + n][:, 0:256], a_kn[b0:b0 + 64, n // 2, h * P:(h + 1) * P],
                                         a_vn[b0:b0 + 64, n // 2, h * 256:(h + 1) * 256], start=True, stop=True).then_inc(gs["kv"], 1)
                    pe.wait_ge(gs["sm"], h + 1)
                    pe.wait_ge(gs["st"], 3 * h + 3)
                    if h >= 2:
                        pe.wait_ge(mix_in[3], h - 1)
                    o = bank[6 + h % 2]
                    for e in range(2):
                        v0 = h * 256 + e * P
                        for t in range(2):
                            nc.tensor.matmul(o[:, e * 256 + t * P:e * 256 + (t + 1) * P], a_vn[:, t, v0:v0 + P],
                                             a_sm[:, h % 2, t * P:(t + 1) * P], start=(e == 0 and t == 0), stop=False)
                        for n in range(1, 4):
                            c0 = e * 256 + n * 64
                            last = nc.tensor.matmul(o[:, c0:c0 + 64], a_st[:, h % 2, n - 1, e * P:(e + 1) * P],
                                                    a_proj[:, h, n * 64:(n + 1) * 64], start=False, stop=(e == 1 and n == 3))
                    last.then_inc(gs["o"], 1)
                pe.wait_ge(mix_in[3], H_GLA)
                head_norm(hn[3])

            mixes = [mix0, mix1, mix2, mix3]
            for kind, what in steps:
                if kind == "gemm":
                    gemm(what)
                elif kind == "norm":
                    norm_sums(what)
                elif kind == "mix":
                    mixes[what]()

        @block.scalar
        def _(act):
            count = [0]

            def link(ins):
                count[0] += 1
                ins.then_inc(act_self, 1)
                act.wait_ge(act_self, count[0])

            act.wait_ge(in_loaded, 64)
            nc.scalar.activation(csil[:, :, :], csil[:, :, :], ACTF.Silu).then_inc(csil_ready, 1)

            def high(g, i, b):
                q, a = g.p0 + 4 * i + b, b % 2
                act.wait_ge(raw_ready[a], (g.p0 // 4 + i) * 16 + 16)
                if g.p0 > 0 or not isinstance(i, int):
                    act.wait_ge(piece_done, q - 3)
                c0 = (b // 2) * P
                nc.scalar.activation(WH[:, b, 0:g.k, :], raw[:, a, 0:g.k, c0:c0 + P], ACTF.Copy).then_inc(h_done, 1)

            for b in range(4):
                high(gemms[0], 0, b)

            def body(g, i, ahead):
                q = g.p0 + 4 * i
                t = g.t
                for b in range(4):
                    if g.kind == "up" and b % 2 == 0:
                        act.wait_ge(piece_done, q + (b + 1))
                        nc.scalar.activation(sg[:, b // 2, 0:t], bank[b][:, 0:t], ACTF.Silu).then_inc(act_bank, 1)
                    if g.kind == "proj" and b % 2 == 0:
                        act.wait_ge(piece_done, q + (b + 1))
                        nc.scalar.activation(g.dst[:, bass.ds(i * 4 + (b // 2), 1), 0:t], bank[b][:, 0:t].rearrange("p (o n) -> p o n", o=1),
                                             ACTF.Copy).then_inc(act_bank, 1)
                    if g.kind == "up" and b == 2:
                        hidden(g, i, 0)
                    if ahead:
                        high(*ahead, b)
                    if g.kind == "up" and b == 3:
                        hidden(g, i, 1)

            def hidden(g, i, half):
                f = 2 * i + half
                act.wait_ge(dve_bank, 2 * (g.e0 + i) + (3 + half))
                nc.scalar.activation(HH[:, bass.ds(f, 1), 0:g.t], hf[:, half:half + 1, 0:g.t], ACTF.Copy).then_inc(hid_high, 1)

            def gemm(g):
                if g.kind == "up":
                    act.wait_ge(arena_free, turn[0])
                if g.kind == "proj":
                    act.wait_ge(arena_free, turn[0])
                with act.Fori(0, g.iters - 1) as i:
                    body(g, i, (g, i + 1))
                nxt = following[id(g)]
                body(g, g.iters - 1, (nxt, 0) if nxt else None)

            def norm_act(n):
                t = n["t"]
                for k in range(DT):
                    if n["last"]:
                        act.wait_ge(res_done, x_ready(n, k))
                    if k == 0 and not n["last"] and n["i"] > 0:
                        act.wait_ge(n_mul, DT * n["i"])
                    if k >= 2 or n["i"] > 0:
                        act.wait_ge(sq_sum, DT * n["i"] + k - 1)
                    nc.scalar.activation(sq[:, k % 2, 0:t], xT[:, k, 0:t], ACTF.Square).then_inc(sq_ready, 1)
                act.wait_ge(sq_sum, DT * n["i"] + DT)
                nc.scalar.activation(rstd[:, 0:t], bank[6][:, 0:t], ACTF.Sqrt, bias=eps[:, 0:1]).then_inc(n_root, 1)
                if n["mode"] != "split":
                    return
                for k in range(DT):
                    act.wait_ge(n_mul, DT * n["i"] + k + 1)
                    if n["shift"]:
                        for half in range(t // S):
                            cs = slice(half * S, half * S + S)
                            last = nc.scalar.activation(XH[:, k, cs], tn[:, k % 2, cs], ACTF.Identity, bias=n["shift"](k, half))
                    else:
                        last = nc.scalar.activation(XH[:, k, 0:t], tn[:, k % 2, 0:t], ACTF.Copy)
                    last.then_inc(n_high, 1)

            def store_v(m):
                for n, (_, dst) in enumerate(v_groups(m)):
                    act.wait_ge(v_turned[m], n + 1)
                    nc.scalar.activation(dst, bank[6 + n % 2][:, :].rearrange("p (g n) -> p g n", g=4), ACTF.Copy).then_inc(v_stored[m], 1)

            def attention(a):
                jobs = a.jobs
                for s in range(len(jobs) + 3):
                    if s < len(jobs):
                        j = jobs[s]
                        nm = len(j["maps"])
                        sm = a.small[:, s, :]
                        act.wait_ge(a.max, nm * s + nm)
                        for m in range(nm):
                            act_in = a.s[:, s % 2, m, 0:j["nk"]]
                            last = nc.scalar.activation(act_in, act_in, ACTF.Exp, bias=sm[:, m:m + 1], scale=HD ** -0.5,
                                                        accum_out=sm[:, 2 + m:3 + m])
                        if a.sink:
                            c = COL_AT["sinks"] + j["head"]
                            last = nc.scalar.activation(sm[:, 4:5], cols[:, c:c + 1], ACTF.Exp, bias=sm[:, 0:1])
                        last.then_inc(a.exp, 1)
                    if 1 <= s <= len(jobs):
                        j = jobs[s - 1]
                        act.wait_ge(a.turned, s)
                        nc.scalar.activation(a.pt[:, (s - 1) % 2, 0:j["nk"]], bank[4 + (s - 1) % 2][:, 0:j["nk"]],
                                             ACTF.Copy).then_inc(a.pt_ready, 1)
                    if s >= 3 and jobs[s - 3]["last"]:
                        o = jobs[s - 3]["o"]
                        act.wait_ge(a.o_done, o + 1)
                        src = bank[6 + o % 2][:, 0:a.cols]
                        if a.keep is not None:
                            nc.scalar.activation(a.keep[:, o, :], src, ACTF.Copy).then_inc(a.o_free, 1)
                        else:
                            nc.scalar.activation(XH[:, a.x0 + o, 0:a.cols], src, ACTF.Copy).then_inc(a.o_high, 1)

            def head_norm(h):
                for c in range(h.chunks):
                    d = h.data[:, 2 * c:2 * c + 2, :]
                    dst = sq[:, c % 2, :].rearrange("p (e n) -> p e n", e=2)
                    if h.centre:
                        act.wait_ge(h.centred, c + 1)
                    if c >= 2:
                        act.wait_ge(h.var, c - 1)
                    nc.scalar.activation(dst, d, ACTF.Square).then_inc(h.squared, 1)
                    if h.gate:
                        src, t0 = h.gate
                        if c >= 2:
                            act.wait_ge(h.gated, c - 1)
                        nc.scalar.activation(sg[:, c % 2, :].rearrange("p (e n) -> p e n", e=2),
                                             src[:, t0 + 2 * c:t0 + 2 * c + 2, :], ACTF.Silu).then_inc(h.sig, 1)
                    act.wait_ge(h.var, c + 1)
                    nc.scalar.activation(tn[:, c % 2, :].rearrange("p (e n) -> p e n", e=2), stat_of(h, 2 + c % 2), ACTF.Sqrt,
                                         bias=eps[:, 0:1]).then_inc(h.root, 1)
                    act.wait_ge(h.gated, c + 1)
                    nc.scalar.activation(XH[:, h.x0 + 2 * c:h.x0 + 2 * c + 2, 0:S], h.data[:, 2 * c:2 * c + 2, :],
                                         ACTF.Copy).then_inc(h.high, 1)

            def mix0():
                act.wait_ge(act_bank, 2 * (last_proj[0].e0 + last_proj[0].iters) + 2)
                store_v(0)
                for i in range(2):
                    act.wait_ge(kswap, i + 1)
                    nc.scalar.activation(g_ks[:, i, :], bank[4 + i][:, :], ACTF.Copy).then_inc(kswap_stored, 1)
                attention(gqa)

            def mix1():
                act.wait_ge(lam_sum, 1)
                nc.scalar.activation(d_lw[:, 10:12], bank[4][:, 0:2], ACTF.Exp).then_inc(lam_exp, 1)
                store_v(1)
                attention(dif)
                act.wait_ge(dif.o_free, H_DIFF)
                head_norm(hn[1])

            def mix2():
                store_v(2)
                for h in range(H_RET):
                    act.wait_ge(ret_o, h + 1)
                    nc.scalar.activation(r_o[:, h, :], bank[2 + h % 2][:, 0:256], ACTF.Copy).then_inc(mix_in[2], 1)
                head_norm(hn[2])
                attention(dil)

            def mix3():
                act.wait_ge(gs["low"], 1)
                nc.scalar.activation(a_low[:, :], bank[4][0:GLA_R, 0:S], ACTF.Copy).then_inc(gs["lowc"], 1)
                store_v(3)
                act.wait_ge(gs["znabs"], 2)
                link(nc.scalar.activation(a_la[:, :, :], a_la[:, :, :], ACTF.Exp))
                nc.scalar.activation(a_la[:, :, :], a_la[:, :, :], ACTF.Ln, bias=ones_1[:, 0:1]).then_inc(gs["ln"], 1)
                act.wait_ge(gs["bs"], 1)
                nc.scalar.activation(a_eb[:, :, :], a_b[:, :, :], ACTF.Exp).then_inc(gs["eb"], 1)
                act.wait_ge(gs["bd"], 1)
                nc.scalar.activation(a_en[:, :, :], a_b[:, :, :], ACTF.Exp, scale=-1.0).then_inc(gs["eb"], 1)
                nc.scalar.activation(a_el[:, :, :], a_el[:, :, :], ACTF.Exp).then_inc(gs["el"], 1)
                for t in range(2):
                    act.wait_ge(gs["kturn"], t + 1)
                    nc.scalar.activation(a_kn[:, t, :], bank[6 + t][:, :], ACTF.Copy).then_inc(gs["kstore"], 1)
                for h in range(H_GLA):
                    act.wait_ge(gs["o"], h + 1)
                    nc.scalar.activation(a_o[:, 2 * h:2 * h + 2, :], bank[6 + h % 2][:, :].rearrange("p (e n) -> p e n", e=2),
                                         ACTF.Copy).then_inc(mix_in[3], 1)
                act.wait_ge(mix_in[3], H_GLA)
                head_norm(hn[3])

            mixes = [mix0, mix1, mix2, mix3]
            turn = [1]
            for kind, what in steps:
                if kind == "gemm":
                    gemm(what)
                elif kind == "norm":
                    norm_act(what)
                elif kind == "mix":
                    mixes[what]()
                    turn[0] += 1
                else:
                    turn[0] += 1
            act.wait_ge(n_mul, DT * state["norms"])
            act.dma_start(A["out"].rearrange("(k p) n -> p k n", p=P), xT[:, :, 0:S]).then_inc(out_done, 16)
            act.wait_ge(out_done, 16)

        @block.vector
        def _(dve):
            count = [0]

            def link(ins):
                count[0] += 1
                ins.then_inc(dve_self, 1)
                dve.wait_ge(dve_self, count[0])

            turns = [0]

            def release():
                turns[0] += 1
                nc.vector.memset(token[:, turns[0]:turns[0] + 1], 0.0).then_inc(arena_free, 1)

            nc.vector.memset(ones_d[:, :], 1.0 / D)
            nc.vector.memset(ones_1[:, :], 1.0)
            nc.vector.memset(eps[:, :], EPS).then_inc(hid_low, 2)
            nc.vector.memset(ones_e[:, :], 1.0 / P)
            nc.vector.memset(halves[:, 0, :], 0.5).then_inc(dve_bank, 2)
            nc.vector.memset(halves[:, 1, :], 1.0).then_inc(res_done, 2)
            nc.vector.memset(token[:, 0:1], 0.0).then_inc(act_bank, 2)

            def low(g, i, b):
                q, a = g.p0 + 4 * i + b, b % 2
                dve.wait_ge(h_done, q + 1)
                c0 = (b // 2) * P
                nc.vector.tensor_tensor(WL[:, b, 0:g.k, :], raw[:, a, 0:g.k, c0:c0 + P], WH[:, b, 0:g.k, :].bitcast(F32),
                                        ALU.subtract).then_inc(split_done, 1)

            dve.wait_ge(in_loaded, 64)
            ab = COL_AT["ada_b"]
            with dve.Fori(0, ADA_UNITS // ADA_SLOTS) as i:
                for half in range(2):
                    dve.wait_ge(ada_used, i * ADA_SLOTS + 3 * half + 3)
                    bias = cols[:, bass.ds(i * 12 + (ab + 6 * half), 6)].rearrange("p (n o) -> p n o", o=1).to_broadcast([P, 6, 2])
                    nc.vector.tensor_tensor(mods[:, bass.ds(i * 12 + 6 * half, 6), :],
                                            bank[6 + half][:, 0:12].rearrange("p (n o) -> p n o", o=2), bias, ALU.add).then_inc(ada_out, 1)
            dve.wait_ge(ada_out, ADA_UNITS // 3)
            for l in range(2):
                for n in range(3):
                    m0 = l * ADA_TILES + 3 * n * DT
                    w0 = COL_AT["norm_w"] + (3 * l + n) * DT
                    w = cols[:, w0:w0 + DT].rearrange("p (n o) -> p n o", o=1).to_broadcast([P, DT, 2])
                    nc.vector.scalar_tensor_tensor(out=scaleA[:, l, n], in0=mods[:, m0 + DT:m0 + 2 * DT, :], scalar=1.0, in1=w,
                                                   op0=ALU.add, op1=ALU.mult)
                    last = nc.vector.tensor_scalar(gates[:, l, n], mods[:, m0 + 2 * DT:m0 + 3 * DT, :], 1.0 if n == 1 else 0.5,
                                                   None, ALU.mult)
            last.then_inc(mods_ready, 1)
            dve.wait_ge(mods_ready, 1)
            release()

            for b in range(4):
                low(gemms[0], 0, b)

            def body(g, i, ahead):
                q, t = g.p0 + 4 * i, g.t
                down = g.k == KH
                for b in range(4):
                    if g.kind == "up":
                        half = b // 2
                        if b % 2:
                            dve.wait_ge(piece_done, q + (b + 1))
                            dve.wait_ge(act_bank, 2 * (g.e0 + i) + (3 + half))
                            dve.wait_ge(hid_low, 2 * i + (g.hid0 + half + 1))
                            nc.vector.tensor_tensor(hf[:, half, 0:t], sg[:, half, 0:t], bank[b][:, 0:t], ALU.mult).then_inc(dve_bank, 1)
                    if g.kind == "proj" and b % 2:
                        dve.wait_ge(piece_done, q + (b + 1))
                        nc.vector.tensor_copy(g.dst[:, bass.ds(i * 4 + (2 + b // 2), 1), 0:t],
                                              bank[b][:, 0:t].rearrange("p (o n) -> p o n", o=1)).then_inc(dve_bank, 1)
                    if g.kind == "res" and (b % 2 or not down):
                        dve.wait_ge(piece_done, q + (b + 1))
                        d = res_tile(g, i, b)
                        src = bank[4 + (b // 2 if down else b % 2)]
                        for half in range(t // S):
                            cs = slice(half * S, half * S + S)
                            x = xT[:, bass.ds(d, 1), cs]
                            last = nc.vector.scalar_tensor_tensor(
                                out=x, in0=src[:, cs].rearrange("p (o n) -> p o n", o=1), scalar=g.gate(d, half), in1=x,
                                op0=ALU.mult, op1=ALU.add)
                        last.then_inc(res_done, 1)
                    if g.kind == "up" and b == 2:
                        hidden_low(g, i, 0)
                    if ahead:
                        low(*ahead, b)
                    if g.kind == "up" and b == 3:
                        hidden_low(g, i, 1)

            def hidden_low(g, i, half):
                f = 2 * i + half
                dve.wait_ge(hid_high, g.hid0 + f + 1)
                nc.vector.tensor_tensor(HL[:, bass.ds(f, 1), 0:g.t], hf[:, half:half + 1, 0:g.t],
                                        HH[:, bass.ds(f, 1), 0:g.t].bitcast(F32), ALU.subtract).then_inc(hid_low, 1)

            def gemm(g):
                with dve.Fori(0, g.iters - 1) as i:
                    body(g, i, (g, i + 1))
                nxt = following[id(g)]
                body(g, g.iters - 1, (nxt, 0) if nxt else None)

            def norm_dve(n):
                t, i0 = n["t"], DT * n["i"]
                dve.wait_ge(n_root, n["i"] + 1)
                link(nc.vector.reciprocal(rstd[:, 0:t], rstd[:, 0:t]))

                def scaled(k):
                    if n["mode"] == "split" and k >= 2:
                        dve.wait_ge(n_low, n["h0"] + k - 1)
                    for half in range(t // S):
                        cs = slice(half * S, half * S + S)
                        dst = tn[:, k % 2, cs] if n["mode"] == "split" else xT[:, k, cs]
                        last = nc.vector.scalar_tensor_tensor(out=dst, in0=xT[:, k, cs], scalar=n["weight"](k, half),
                                                              in1=rstd[:, cs], op0=ALU.mult, op1=ALU.mult)
                    last.then_inc(n_mul, 1)

                def rest(k):
                    dve.wait_ge(n_high, n["h0"] + k + 1)
                    if n["shift"]:
                        for half in range(t // S):
                            cs = slice(half * S, half * S + S)
                            last = nc.vector.scalar_tensor_tensor(
                                out=XL[:, k, cs], in0=tn[:, k % 2, cs], scalar=n["shift"](k, half),
                                in1=XH[:, k, cs].bitcast(F32), op0=ALU.add, op1=ALU.subtract)
                    else:
                        last = nc.vector.tensor_tensor(XL[:, k, 0:t], tn[:, k % 2, 0:t], XH[:, k, 0:t].bitcast(F32), ALU.subtract)
                    last.then_inc(n_low, 1)

                if n["mode"] != "split":
                    for k in range(DT):
                        scaled(k)
                    return
                scaled(0)
                for k in range(DT):
                    if k + 1 < DT:
                        scaled(k + 1)
                    rest(k)

            def rotate(m):
                tmp = rope_tmp[m]
                dve.wait_ge(tables, tables_at[m])
                for n, (src, tile, _, cos, sin) in enumerate(ropes[m]):
                    dve.wait_ge(rot_done[m], n + 1)
                    x = src[:, tile, 0:S]
                    if n >= 2:
                        dve.wait_ge(roped[m], n - 1)
                    nc.vector.tensor_tensor(tmp[:, n % 2, :], bank[n % 4][:, 0:S], sin[:, :], ALU.mult).then_inc(rot_read[m], 1)
                    link(nc.vector.tensor_tensor(x, x, cos[:, :], ALU.mult))
                    nc.vector.tensor_tensor(x, x, tmp[:, n % 2, :], ALU.add).then_inc(roped[m], 1)

            def attention(a):
                jobs = a.jobs
                scale = HD ** -0.5
                for s in range(len(jobs) + 4):
                    if s < len(jobs):
                        j = jobs[s]
                        nm, sm, nk = len(j["maps"]), a.small[:, s, :], j["nk"]
                        if s >= 2:
                            dve.wait_ge(a.norm, s - 1)
                        for m in range(nm):
                            dve.wait_ge(a.scores, nm * s + m + 1)
                            link(nc.vector.tensor_tensor_reduce(
                                out=a.s[:, s % 2, m, 0:nk], in0=bank[2 * (s % 2) + m][:, 0:nk], in1=j["mask"], scale=1.0,
                                scalar=-3e38, op0=ALU.add, op1=ALU.max, accum_out=sm[:, 6 + m:7 + m]))
                            if a.sink:
                                nc.vector.tensor_scalar(sm[:, 0:1], sm[:, 6:7], -scale, g_nsink[:, j["head"]:j["head"] + 1],
                                                        ALU.mult, ALU.min).then_inc(a.max, 1)
                            else:
                                nc.vector.tensor_scalar(sm[:, m:m + 1], sm[:, 6 + m:7 + m], -scale, None, ALU.mult).then_inc(a.max, 1)
                    if 1 <= s <= len(jobs):
                        j = jobs[s - 1]
                        nm, sm, nk, p = len(j["maps"]), a.small[:, s - 1, :], j["nk"], (s - 1) % 2
                        dve.wait_ge(a.exp, s)
                        if s >= 3:
                            dve.wait_ge(a.turned, s - 2)
                        if a.sink:
                            link(nc.vector.tensor_tensor(sm[:, 2:3], sm[:, 2:3], sm[:, 4:5], ALU.add))
                        link(nc.vector.reciprocal(sm[:, 2:2 + nm], sm[:, 2:2 + nm]))
                        if nm == 1:
                            nc.vector.tensor_scalar(a.p[:, p, 0:nk], a.s[:, p, 0, 0:nk], sm[:, 2:3], None, ALU.mult).then_inc(a.norm, 1)
                        else:
                            nc.vector.tensor_scalar(a.p[:, p, 0:nk], a.s[:, p, 0, 0:nk], sm[:, 2:3], None, ALU.mult)
                            link(nc.vector.tensor_tensor(sm[:, 5:6], sm[:, 3:4], d_lw[:, 14:15], ALU.mult))
                            nc.vector.scalar_tensor_tensor(out=a.p[:, p, 0:nk], in0=a.s[:, p, 1, 0:nk], scalar=sm[:, 5:6],
                                                           in1=a.p[:, p, 0:nk], op0=ALU.mult, op1=ALU.add).then_inc(a.norm, 1)
                    if s >= 4 and jobs[s - 4]["last"] and a.keep is None:
                        o = jobs[s - 4]["o"]
                        dve.wait_ge(a.o_high, o + 1)
                        xh, xl = XH[:, a.x0 + o, 0:a.cols], XL[:, a.x0 + o, 0:a.cols]
                        low_part = nc.vector.tensor_tensor(xl, bank[6 + o % 2][:, 0:a.cols], xh.bitcast(F32), ALU.subtract)
                        low_part.then_inc(a.o_free, 1)

            def head_norm(h):
                for c in range(h.chunks):
                    d = h.data[:, 2 * c:2 * c + 2, :]
                    r = tn[:, c % 2, :].rearrange("p (e n) -> p e n", e=2)
                    if h.centre:
                        dve.wait_ge(h.mean, c + 1)
                        nc.vector.tensor_tensor(d, d, stat_of(h, c % 2), ALU.subtract).then_inc(h.centred, 1)
                    dve.wait_ge(h.root, c + 1)
                    link(nc.vector.reciprocal(r, r))
                    if h.gate:
                        link(nc.vector.tensor_tensor(d, d, r, ALU.mult))
                        dve.wait_ge(h.sig, c + 1)
                        nc.vector.tensor_tensor(d, d, sg[:, c % 2, :].rearrange("p (e n) -> p e n", e=2), ALU.mult).then_inc(h.gated, 1)
                    else:
                        nc.vector.scalar_tensor_tensor(out=d, in0=d, scalar=h.scale[:, 0:1], in1=r, op0=ALU.mult,
                                                       op1=ALU.mult).then_inc(h.gated, 1)
                    dve.wait_ge(h.high, c + 1)
                    nc.vector.tensor_tensor(XL[:, h.x0 + 2 * c:h.x0 + 2 * c + 2, 0:S], d,
                                            XH[:, h.x0 + 2 * c:h.x0 + 2 * c + 2, 0:S].bitcast(F32), ALU.subtract).then_inc(h.out, 2)

            def mix0():
                c = COL_AT["sinks"]
                rotate(0)
                link(nc.vector.tensor_scalar(g_nsink[:, :], cols[:, c:c + 16], -1.0, None, ALU.mult))
                attention(gqa)

            def mix1():
                dve.wait_ge(tables, tables_at[1])
                lp = d_lam[:, :].rearrange("p (a b) -> p a b", b=2)
                nc.vector.tensor_tensor(d_lw[0:64, 8:10], lp[:, :, 0], lp[:, :, 1], ALU.mult).then_inc(lam_prod, 1)
                c = COL_AT["subln"]
                nc.vector.tensor_scalar(d_lw[:, 0:1], cols[:, c:c + 1], 1.0 - LAMBDA_INIT, None, ALU.mult)
                link(nc.vector.memset(d_zero[:, :], 0.0))
                dve.wait_ge(lam_exp, 1)
                link(nc.vector.tensor_tensor(d_lw[:, 13:14], d_lw[:, 11:12], d_lw[:, 10:11], ALU.subtract))
                link(nc.vector.tensor_scalar(d_lw[:, 14:15], d_lw[:, 13:14], -LAMBDA_INIT, None, ALU.add))
                rotate(1)
                attention(dif)
                head_norm(hn[1])

            def mix2():
                rotate(2)
                for h in range(H_RET):
                    dve.wait_ge(ret_scores, h + 1)
                    if h >= 2:
                        dve.wait_ge(ret_o, h - 1)
                    nc.vector.tensor_tensor(r_sm[:, h % 2, :], bank[h % 2][:, 0:384], r_mask[:, h, :], ALU.mult).then_inc(ret_masked, 1)
                head_norm(hn[2])
                attention(dil)

            def mix3():
                dve.wait_ge(tables, tables_at[3])
                link(nc.vector.tensor_copy(a_wh[:, :, :], a_wr[:, :, :]))
                nc.vector.tensor_tensor(a_wl[:, :, :], a_wr[:, :, :], a_wh[:, :, :].bitcast(F32), ALU.subtract).then_inc(gs["wsplit"], 1)
                nc.vector.memset(ones_e[:, :], 1.0 / GLA_DV)
                nc.vector.memset(a_sm[:, :, :], 0.0)
                for t in range(2):
                    dve.wait_ge(gs["z"], t + 1)
                    nc.vector.tensor_scalar(a_zm[:, t, :], bank[t][:, :], 0.0, None, ALU.min)
                    link(nc.vector.tensor_scalar(a_la[:, t, :], bank[t][:, :], -1.0, None, ALU.mult))
                    nc.vector.tensor_tensor(a_la[:, t, :], a_la[:, t, :], bank[t][:, :], ALU.min).then_inc(gs["znabs"], 1)
                dve.wait_ge(gs["ln"], 1)
                nc.vector.tensor_tensor(a_la[:, :, :], a_zm[:, :, :], a_la[:, :, :], ALU.subtract).then_inc(gs["la"], 1)
                dve.wait_ge(gs["b"], 1)
                for i in range(2):
                    last = nc.vector.tensor_copy(a_b[:, 2 * i:2 * i + 2, :], bank[2 + i][:, :].rearrange("p (h n) -> p h n", h=2))
                last.then_inc(gs["bs"], 1)
                dve.wait_ge(gs["bs"], 1)
                b3 = a_b[:, :, :].rearrange("p h (c n) -> p (h c) n", n=GLA_C)
                e3 = a_el[:, :, :].rearrange("p h (c n) -> p (h c) n", n=GLA_C)
                nc.vector.tensor_tensor(e3, b3[:, :, GLA_C - 1:GLA_C].to_broadcast([P, 16, GLA_C]), b3, ALU.subtract).then_inc(gs["bd"], 1)
                q, k = a_proj[:, 0:4, :], a_proj[:, 4:8, :]
                dve.wait_ge(gs["eb"], 1)
                nc.vector.scalar_tensor_tensor(out=q, in0=q, scalar=P ** -0.5, in1=a_eb[:, :, :], op0=ALU.mult, op1=ALU.mult).then_inc(gs["qt"], 1)
                dve.wait_ge(gs["el"], 1)
                nc.vector.tensor_tensor(a_el[:, :, :], k, a_el[:, :, :], ALU.mult).then_inc(gs["ko"], 1)
                dve.wait_ge(gs["eb"], 2)
                dve.wait_ge(gs["ko"], 1)
                nc.vector.tensor_tensor(k, k, a_en[:, :, :], ALU.mult).then_inc(gs["kt"], 1)
                for h in range(H_GLA):
                    dve.wait_ge(gs["sc"], h + 1)
                    if h >= 2:
                        dve.wait_ge(gs["o"], h - 1)
                    nc.vector.copy_predicated(a_sm[:, h % 2, :], a_mask[:, :], bank[h % 2][:, 0:S]).then_inc(gs["sm"], 1)
                    for n in range(3):
                        dve.wait_ge(gs["kv"], 3 * h + n + 1)
                        if n == 0:
                            nc.vector.tensor_copy(a_st[:, h % 2, 0, :], bank[2][:, 0:256]).then_inc(gs["st"], 1)
                        else:
                            dve.wait_ge(gs["st"], 3 * h + n)
                            c0 = n * GLA_C + GLA_C - 1
                            nc.vector.scalar_tensor_tensor(out=a_st[:, h % 2, n, :], in0=a_st[:, h % 2, n - 1, :],
                                                           scalar=a_eb[:, h, c0:c0 + 1], in1=bank[2 + n][:, 0:256],
                                                           op0=ALU.mult, op1=ALU.add).then_inc(gs["st"], 1)
                head_norm(hn[3])

            mixes = [mix0, mix1, mix2, mix3]
            for kind, what in steps:
                if kind == "gemm":
                    if what.kind == "proj" and what is last_proj[3]:
                        nc.vector.memset(a_wr[:, :, :], 0.0).then_inc(gs["zero"], 1)
                    gemm(what)
                elif kind == "norm":
                    norm_dve(what)
                elif kind == "mix":
                    mixes[what]()
                    release()
                else:
                    release()


_FIXED = ["ffn_w_gate", "ffn_w_up", "ffn_w_down", "gqa_w_in", "gqa_w_out", "diff_w_in", "diff_w_out", "ada_w",
          "ffn_pre_w_gate_2", "ffn_pre_w_up_2", "ffn_pre_w_down_2", "ab_w_in_2", "ab_w_out_2", "gla_w_in_2", "gla_w_out_2",
          "ffn_post_w_gate_2", "ffn_post_w_up_2", "ffn_post_w_down_2"]


def kernel(**inputs):
    import concourse.bacc as bacc
    from concourse.bass_utils import run_bass_kernel_spmd as run

    def col(a):
        return np.asarray(a).reshape(-1, P).T

    arrays = {n: np.ascontiguousarray(inputs[n]) for n in _FIXED}
    arrays["xT"] = np.ascontiguousarray(np.concatenate([np.asarray(inputs["x"])[0].T, np.asarray(inputs["ctx"])[0].T], 1))
    packed = {"norm_w": col(inputs["norm_w"]), "final_norm_w": col(inputs["final_norm_w"]), "ada_b": col(inputs["ada_b"]),
              "pre2": col(inputs["ffn_pre_norm_2"]), "mix2": col(inputs["mix_norm_2"]), "post2": col(inputs["ffn_post_norm_2"]),
              "final2": col(inputs["final_norm_2"]), "subln": col(inputs["diff_subln_w"]),
              "sinks": np.broadcast_to(np.asarray(inputs["gqa_sinks"]).reshape(1, -1), (P, H_GQA))}
    arrays["cols"] = np.ascontiguousarray(np.concatenate([packed[n] for n in COLS], 1))
    arrays["c_cols"] = np.ascontiguousarray(np.stack([col(inputs["c"]), col(inputs["c_ctx"])], 2))
    arrays["diff_lambda"] = np.ascontiguousarray(np.asarray(inputs["diff_lambda"])[0].T)
    arrays["gla_w_a2_2"] = np.ascontiguousarray(np.asarray(inputs["gla_w_a2_2"])[0])
    arrays["gla_b_a_2"] = np.ascontiguousarray(np.asarray(inputs["gla_b_a_2"]))
    arrays.update(constants())

    nc = bacc.Bacc("TRN2", target_bir_lowering=False, num_devices=1, dynamic_dma_scratch_size=2048)
    A = {n: nc.dram_tensor(f"in_{n}", a.shape, mybir.dt.from_np(a.dtype), kind="ExternalInput").ap() for n, a in arrays.items()}
    A["out"] = nc.dram_tensor("out_T", (D, S), F32, kind="ExternalOutput").ap()
    build(nc, A)
    r = run(nc, [{f"in_{n}": a for n, a in arrays.items()}], core_ids=[0])
    return np.ascontiguousarray(r.results[0]["out_T"].T).reshape(1, S, D)
```

```python
import math
from contextlib import ExitStack

import numpy as np

import concourse.bass as bass
from concourse import mybir

F32 = mybir.dt.float32
F32R = mybir.dt.float32r
U32 = mybir.dt.uint32
ACTF = mybir.ActivationFunctionType
ALU = mybir.AluOpType
AX = mybir.AxisListType

P = 128
S = 256
D = 1024
DT = D // P
FF = 2816
FT = FF // P
KH = FT // 2
NMOD = 9
EPS = 1e-6
NEG = -1e30
H_GQA, KV_GQA, HD = 16, 4, 64
H_DIFF = 8
LAMBDA_INIT = 0.8 - 0.6 * math.exp(-0.3 * 1)
H_RET, H_DIL = 4, 8
H_GLA, GLA_DV, GLA_C, GLA_R = 4, 256, 64, 16
ADA_FIRST = 20
ADA_TILES = NMOD * DT


def rope_rotation(dim, half, period):
    r = np.zeros((P, P), np.float32)
    for base in range(0, P, period):
        for block in range(0, dim, 2 * half):
            for j in range(half):
                lo, hi = base + block + j, base + block + half + j
                r[hi, lo] = -1.0
                r[lo, hi] = 1.0
    return r


def rope_angles(kind):
    pos = np.arange(S, dtype=np.float32)
    if kind == "axial":
        inv = (10000.0 ** (-np.arange(0, 32, 2, dtype=np.float32) / 32)).astype(np.float32)
        row, col = np.floor(pos / 64), pos % 64
        ang = np.concatenate([row[:, None] * inv, row[:, None] * inv, col[:, None] * inv, col[:, None] * inv], -1)
        return np.tile(ang, (1, 2)).T
    if kind == "ret":
        inv = (10000.0 ** (-np.linspace(0.0, 1.0, 64, dtype=np.float32))).astype(np.float32)
        ang = pos[:, None] * inv
        return np.concatenate([ang, ang], -1).T
    inv = (500000.0 ** (-np.arange(0, 16, 2, dtype=np.float32) / 16)).astype(np.float32)
    ang = pos[:, None] * inv
    one = np.concatenate([ang, ang, np.zeros((S, 48), np.float32)], -1)
    return np.tile(one, (1, 2)).T


def constants():
    c = {}
    i, j = np.arange(S)[:, None], np.arange(S)[None, :]
    for kind in ("axial", "ret", "dil"):
        ang = rope_angles(kind).astype(np.float32)
        c[f"{kind}_cos"], c[f"{kind}_sin"] = np.cos(ang), np.sin(ang)
    c["axial_rot"] = rope_rotation(64, 16, 64)
    c["ret_rot"] = rope_rotation(128, 64, 128)
    c["dil_rot"] = rope_rotation(16, 8, 64)
    swap = np.zeros((P, P), np.float32)
    swap[np.arange(P), (np.arange(P) + 64) % P] = 1.0
    c["swap"] = swap
    c["ident"] = np.eye(P, dtype=np.float32)
    band = np.where(np.abs(i - j) <= 128, 0.0, NEG)
    full = np.concatenate([band, np.zeros((S, S))], 1)
    c["gqa_mask"] = full.reshape(2, P, 2 * S).transpose(1, 0, 2)
    dist = i - j
    count = np.zeros((S, S))
    for window, dil in ((128, 1), (512, 4), (2048, 16)):
        count += (dist >= 0) & (dist <= window) & (dist % dil == 0)
    c["dil_mask"] = np.where(count > 0, np.log(np.maximum(count, 1)) * 8.0, NEG).reshape(2, P, S).transpose(1, 0, 2)
    decay = np.zeros((P, H_RET, 384))
    for h in range(H_RET):
        log_g = np.log(1.0 - 2.0 ** (-5.0 - h))
        m = np.where(dist >= 0, np.exp(log_g * np.maximum(dist, 0)), 0.0).T * 128 ** -0.5
        decay[:, h, 0:256] = m[0:128, :]
        decay[:, h, 256:384] = m[128:256, 128:256]
    c["ret_mask"] = decay
    a, b = np.arange(P)[:, None], np.arange(P)[None, :]
    inside = (a // GLA_C == b // GLA_C) & (a <= b)
    c["gla_sum"] = inside / 16.0
    c["gla_mask"] = np.tile(inside, (1, 2)).astype(np.uint32)
    return {k: np.ascontiguousarray(v.astype(v.dtype if v.dtype == np.uint32 else np.float32)) for k, v in c.items()}


COLS = {"norm_w": 48, "final_norm_w": 8, "ada_b": 144, "pre2": 16, "mix2": 16, "post2": 16, "final2": 8,
        "subln": 1, "sinks": 16}
COL_AT = dict(zip(COLS, np.cumsum([0] + list(COLS.values()))[:-1].tolist()))
N_COLS = sum(COLS.values())


class Gemm:

    def __init__(self, kind, iters, k, t, src, rhs, ready, dst=None, gate=None, hid0=0, ada=None):
        self.kind, self.iters, self.k, self.t, self.src, self.rhs, self.ready = kind, iters, k, t, src, rhs, ready
        self.dst, self.gate, self.hid0 = dst, gate, hid0
        self.norm_sums = 0
        self.ada = ada
        self.p0 = self.e0 = self.r0 = 0


def build(nc, A):
    ctx = ExitStack()
    with ctx:
        def sem(name):
            return ctx.enter_context(nc.semaphore(name))

        def sb(name, shape, dt=F32, stack=ctx):
            return stack.enter_context(nc.sbuf_tensor(name, shape, dt))

        xT = sb("xT", [P, DT, 2 * S])
        XH = sb("XH", [P, DT, 2 * S], F32R)
        XL = sb("XL", [P, DT, 2 * S], F32R)
        raw = sb("raw", [P, 4, KH, P])
        WH = sb("WH", [P, 4, KH, P], F32R)
        WL = sb("WL", [P, 4, KH, P], F32R)
        mods = sb("mods", [P, 2 * ADA_TILES, 2])
        scaleA = sb("scaleA", [P, 2, 3, DT, 2])
        gates = sb("gates", [P, 2, 3, DT, 2])
        halves = sb("halves", [P, 2, DT])
        cols = sb("cols", [P, N_COLS])
        csil = sb("csil", [P, DT, 2])
        ones_d = sb("ones_d", [P, P])
        ones_e = sb("ones_e", [P, P])
        ones_1 = sb("ones_1", [P, P])
        ident = sb("ident", [P, P])
        sq = sb("sq", [P, 2, 2 * S])
        rstd = sb("rstd", [P, 2 * S])
        tn = sb("tn", [P, 2, 2 * S])
        sg = sb("sg", [P, 2, 2 * S])
        hf = tn
        eps = sb("eps", [P, 1])
        token = sb("token", [P, 16])

        def arena(*specs):
            stack = ExitStack()
            got = [sb(n, s, d, stack) for n, s, d in specs]
            stack.close()
            return got

        (ada_first,) = arena(("ada_first", [P, ADA_FIRST // 2, DT, 256], F32))
        ada_slot = sq[:, :, :].rearrange("p a (k n) -> p (a k) n", n=P)
        HH, HL = arena(("HH", [P, FT, 2 * S], F32R), ("HL", [P, FT, 2 * S], F32R))
        att_tiles = lambda n: [(f"{n}_s", [P, 4, 512], F32), (f"{n}_p", [P, 2, 512], F32),
                               (f"{n}_pt", [P, 2, 512], F32), (f"{n}_small", [P, 64, 8], F32)]
        rope_t = lambda n: [(f"{n}_cos", [P, S], F32), (f"{n}_sin", [P, S], F32), (f"{n}_rot", [P, P], F32)]
        (g_proj, g_ks, g_vn, g_o, g_mask, g_swap, g_rt, g_nsink, g_cos, g_sin, g_rot, *g_att) = arena(
            ("g_proj", [P, 12, 2 * S], F32), ("g_ks", [P, 2, 2 * S], F32), ("g_vn", [P, 4, 256], F32),
            ("g_o", [P, 4, 1024], F32), ("g_mask", [P, 2, 512], F32), ("g_swap", [P, P], F32), ("g_rt", [P, 2, S], F32),
            ("g_nsink", [P, 16], F32), *rope_t("g"), *att_tiles("g"))
        (d_q, d_kv, d_vn, d_o, d_ss, d_rt, d_lam, d_lw, d_zero, d_cos, d_sin, d_rot, *d_att) = arena(
            ("d_q", [P, 8, S], F32), ("d_kv", [P, 16, 2 * S], F32), ("d_vn", [P, 4, 1024], F32),
            ("d_o", [P, 2, 1024], F32), ("d_ss", [P, 16], F32), ("d_rt", [P, 2, S], F32), ("d_lam", [64, 4], F32), ("d_lw", [P, 16], F32),
            ("d_zero", [P, 1], F32), *rope_t("d"), *att_tiles("d"))
        (r_proj, r_vn, r_o, l_o, r_rt, r_mask, r_dmask, r_sm, r_cos, r_sin, r_rot, l_cos, l_sin, l_rot, *l_att) = arena(
            ("r_proj", [P, 28, S], F32), ("r_vn", [P, 2, 1024], F32), ("r_o", [P, 4, S], F32), ("l_o", [P, 2, 512], F32),
            ("r_rt", [P, 2, S], F32), ("r_mask", [P, 4, 384], F32), ("r_dmask", [P, 2, S], F32),
            ("r_sm", [P, 2, 384], F32), *rope_t("r"), *rope_t("l"), *att_tiles("l"))
        (a_proj, a_vn, a_kn, a_o, a_la, a_zm, a_b, a_el, a_st, a_sm, a_sum, a_mask, a_low, a_w2, a_ba,
         a_wr, a_wh, a_wl) = arena(
            ("a_proj", [P, 24, S], F32), ("a_vn", [P, 2, 1024], F32), ("a_kn", [P, 2, 512], F32),
            ("a_o", [P, 8, S], F32), ("a_la", [P, 2, 512], F32), ("a_zm", [P, 2, 512], F32),
            ("a_b", [P, 4, S], F32), ("a_el", [P, 4, S], F32),
            ("a_st", [P, 2, 3, S], F32), ("a_sm", [P, 2, S], F32), ("a_sum", [P, P], F32), ("a_mask", [P, S], U32),
            ("a_low", [GLA_R, S], F32), ("a_w2", [GLA_R, 512], F32), ("a_ba", [1, 512], F32),
            ("a_wr", [P, DT, P], F32), ("a_wh", [P, DT, P], F32R), ("a_wl", [P, DT, P], F32R))
        a_eb = a_zm[:, :, :].rearrange("p a (h n) -> p (a h) n", h=2)
        a_en = a_b

        bank = [ctx.enter_context(nc.psum_tensor(f"bank{i}", [P, 512], F32)) for i in range(8)]

        in_loaded = sem("in_loaded")
        raw_ready = [sem(f"raw_ready{b}") for b in range(4)]
        ada_first_ready = [sem(f"ada_first{n}") for n in range(ADA_FIRST // 2)]
        ada_ready = sem("ada_ready")
        ada_used = sem("ada_used")
        ada_out = sem("ada_out")
        csil_ready = sem("csil_ready")
        setup_done = sem("setup_done")
        h_done = sem("h_done")
        split_done = sem("split_done")
        piece_done = sem("piece_done")
        act_bank = sem("act_bank")
        dve_bank = sem("dve_bank")
        res_done = sem("res_done")
        hid_high = sem("hid_high")
        hid_low = sem("hid_low")
        sq_ready = sem("sq_ready")
        sq_sum = sem("sq_sum")
        n_root = sem("n_root")
        n_mul = sem("n_mul")
        n_high = sem("n_high")
        n_low = sem("n_low")
        dve_self = sem("dve_self")
        act_self = sem("act_self")
        tables = sem("tables")
        arena_free = sem("arena_free")
        out_done = sem("out_done")

        def rows(w):
            return w.rearrange("(k p) n -> p k n", p=P)

        gemms = []
        state = {"p0": 0, "e0": 0, "r0": 0, "norms": 0, "hid": 0, "split": 0}
        steps = []

        def add(g):
            g.p0, g.e0, g.r0 = state["p0"], state["e0"], state["r0"]
            state["p0"] += 4 * g.iters
            if g.kind == "res":
                state["r0"] += (2 if g.k == KH else 4) * g.iters
            else:
                state["e0"] += g.iters
            gemms.append(g)
            steps.append(("gemm", g))
            return g

        def x_in(k, t):
            return XH[:, k, 0:t], XL[:, k, 0:t]

        def hid_in(k, t):
            return HH[:, k, 0:t], HL[:, k, 0:t]

        def norm(t, weight, shift=None, mode="split"):
            n = dict(i=state["norms"], t=t, weight=weight, shift=shift, mode=mode, h0=state["split"],
                     last=gemms[-1] if gemms and steps[-1][0] != "norm" else None)
            state["norms"] += 1
            state["split"] += DT if mode == "split" else 0
            steps.append(("norm", n))
            return n

        def ada_norm(l, n, t):
            return norm(t, lambda k, half: scaleA[:, l, n, k, half:half + 1],
                        lambda k, half: mods[:, l * ADA_TILES + 3 * n * DT + k, half:half + 1])

        def plain_norm(name, l, mode="split"):
            at = COL_AT[name] + DT * l
            return norm(S, lambda k, half: cols[:, at + k:at + k + 1], None, mode)

        def ffn(n, t, gate, wg, wu, wd, ada=None):
            wg, wu, wd = rows(wg), rows(wu), rows(wd)
            first_sums = DT * (n["i"] + 1)
            up = add(Gemm("up", KH, DT, t, lambda i, b: (wg, wu)[b % 2][:, :, bass.ds(i * 256 + b // 2 * P, P)],
                          x_in, lambda k: (n_low, n["h0"] + k + 1), hid0=state["hid"], ada=ada))
            up.norm_sums = first_sums
            add(Gemm("res", 4, KH, t, lambda i, b: wd[:, KH * (b % 2):KH * (b % 2) + KH, bass.ds(i * 256 + b // 2 * P, P)],
                     hid_in, lambda k: (hid_low, up.hid0 + k + 3), gate=gate))
            state["hid"] += FT
            steps.append(("ffn_end", None))

        def proj(n, w, iters, t, dst, col0=0):
            w = rows(w)
            return add(Gemm("proj", iters, DT, t, lambda i, b: w[:, :, bass.ds(i * 512 + (col0 + P * b), P)],
                            x_in, lambda k: (n_low, n["h0"] + k + 1), dst=dst))

        def out_proj(w, t, ready, gate):
            w = rows(w)
            return add(Gemm("res", 2, DT, t, lambda i, b: w[:, :, bass.ds(i * 512 + P * b, P)],
                            x_in, ready, gate=gate))

        gate1 = lambda l, n: (lambda d, half: gates[:, l, n, bass.ds(d, 1), half:half + 1].rearrange("p o h -> p (o h)"))
        gate2 = lambda n: (lambda d, half: halves[:, n, bass.ds(d, 1)])
        mix_out = [sem(f"mix_out{m}") for m in range(4)]
        dil_out = sem("dil_out")
        mix_ready = [lambda k: (mix_out[0], k + 1), lambda k: (mix_out[1], k + 1),
                     lambda k: (mix_out[2], k + 1) if k < 4 else (dil_out, k - 3), lambda k: (mix_out[3], k + 1)]

        def mixer(m, n, projs, w_out, t, gate):
            steps.append(("mix_start", m))
            for w, iters, tt, dst, col0 in projs:
                proj(n, w, iters, tt, dst, col0)
            steps.append(("mix", m))
            out_proj(w_out, t, mix_ready[m], gate)

        for l in range(2):
            ffn(ada_norm(l, 0, 2 * S), 2 * S, gate1(l, 0), A["ffn_w_gate"][l, 0], A["ffn_w_up"][l, 0], A["ffn_w_down"][l, 0], ada=(ADA_FIRST, ADA_FIRST + 8 * KH)[l])
            if l == 0:
                mixer(0, ada_norm(0, 1, 2 * S), [(A["gqa_w_in"][0], 3, 2 * S, g_proj, 0)], A["gqa_w_out"][0], 2 * S, gate1(0, 1))
            else:
                mixer(1, ada_norm(1, 1, 2 * S), [(A["diff_w_in"][0], 2, S, d_q, 0), (A["diff_w_in"][0], 4, 2 * S, d_kv, 1024)],
                      A["diff_w_out"][0], S, gate1(1, 1))
            t = 2 * S if l == 0 else S
            ffn(ada_norm(l, 2, t), t, gate1(l, 2), A["ffn_w_gate"][l, 1], A["ffn_w_up"][l, 1], A["ffn_w_down"][l, 1], ada=(ADA_FIRST + 4 * KH, None)[l])
        plain_norm("final_norm_w", 0, "replace")
        for l in range(2):
            n = plain_norm("pre2", l)
            ffn(n, S, gate2(0), A["ffn_pre_w_gate_2"][l], A["ffn_pre_w_up_2"][l], A["ffn_pre_w_down_2"][l])
            n = plain_norm("mix2", l)
            if l == 0:
                mixer(2, n, [(A["ab_w_in_2"][0], 7, S, r_proj, 0)], A["ab_w_out_2"][0], S, gate2(1))
            else:
                mixer(3, n, [(A["gla_w_in_2"][0], 6, S, a_proj, 0)], A["gla_w_out_2"][0], S, gate2(1))
            n = plain_norm("post2", l)
            ffn(n, S, gate2(0), A["ffn_post_w_gate_2"][l], A["ffn_post_w_up_2"][l], A["ffn_post_w_down_2"][l])
        plain_norm("final2", 0, "out")
        following = {id(g): nxt for g, nxt in zip(gemms, gemms[1:] + [None])}

        def res_tile(g, i, b):
            return i * 2 + b // 2 if g.k == KH else i * 4 + b

        def x_ready(n, k):
            g = n["last"]
            return g.r0 + k + 3

        def gqa_jobs():
            jobs = []
            for h in range(H_GQA):
                kv, qb = h // 4, 64 * (h % 2)
                ksrc = g_proj[:, 8 + kv // 2, :] if 64 * (kv % 2) == qb else g_ks[:, kv // 2, :]
                for t in range(4):
                    keys = (0, 512) if t < 2 else (256, 512)
                    jobs.append(dict(
                        maps=[(g_proj[qb:qb + 64, h // 2, t * P:(t + 1) * P], ksrc[qb:qb + 64, keys[0]:keys[1]])],
                        nk=keys[1] - keys[0], mask=g_mask[:, t, :] if t < 2 else g_mask[:, 0, 256:512], head=h,
                        v=[g_vn[:, keys[0] // P + j, kv * 64:kv * 64 + 64] for j in range((keys[1] - keys[0]) // P)],
                        o=h // 2, t=t, c0=h * 64, width=64, last=(h % 2 == 1 and t == 3)))
            return jobs

        def diff_jobs():
            jobs = []
            for h in range(H_DIFF):
                for t in range(2):
                    jobs.append(dict(
                        maps=[(d_q[64 * m:64 * m + 64, h, t * P:(t + 1) * P], d_kv[64 * m:64 * m + 64, h, :]) for m in range(2)],
                        nk=512, mask=d_zero[:, :].to_broadcast([P, 512]), head=None, v=[d_vn[:, j, h * P:(h + 1) * P] for j in range(4)],
                        o=h, t=t, c0=h * P, width=P, last=False))
            return jobs

        def dil_jobs():
            jobs = []
            for h in range(H_DIL):
                qb = 64 * (h % 2)
                for t in range(2):
                    jobs.append(dict(
                        maps=[(r_proj[qb:qb + 64, 16 + h // 2, t * P:(t + 1) * P], r_proj[qb:qb + 64, 20 + h // 2, :])],
                        nk=256, mask=r_dmask[:, t, :], head=None,
                        v=[r_vn[:, j, 512 + h * 64:512 + h * 64 + 64] for j in range(2)],
                        o=h // 2, t=t, c0=h * 64, width=64, last=(h % 2 == 1 and t == 1)))
            return jobs

        class Att:

            def __init__(self, name, jobs, tiles, cols_o, onat, sink=False, x0=0, out=None, squares=None):
                self.jobs, (self.s, self.p, self.pt, self.small) = jobs, tiles
                self.cols, self.sink, self.onat, self.x0, self.squares = cols_o, sink, onat, x0, squares
                self.scores = sem(f"{name}_scores")
                self.max = sem(f"{name}_max")
                self.exp = sem(f"{name}_exp")
                self.norm = sem(f"{name}_norm")
                self.turned = sem(f"{name}_turned")
                self.pt_ready = sem(f"{name}_pt_ready")
                self.o_done = sem(f"{name}_o_done")
                self.o_read = sem(f"{name}_o_read")
                self.o_turned = sem(f"{name}_o_turned")
                self.o_high = sem(f"{name}_o_high")
                self.o_free = out
                self.squared = sem(f"{name}_squared")

            def logits(self, s, m=0):
                return self.s[:, (2 * (s % 2) + m) if len(self.jobs[s]["maps"]) == 2 else s % 4, 0:self.jobs[s]["nk"]]

        gqa = Att("gqa", gqa_jobs(), g_att, 512, g_o, sink=True, out=mix_out[0])
        dif = Att("dif", diff_jobs(), d_att, 256, d_o, squares=d_ss)
        dil = Att("dil", dil_jobs(), l_att, 256, l_o, x0=4, out=dil_out)
        dif_root, dif_scaled = sem("subln_root"), sem("subln_scaled")
        dif_turned, dif_high = sem("subln_turned"), sem("subln_high")

        ropes = {
            0: [(g_proj, n, g_rot, g_cos, g_sin) for n in (8, 9, 0, 1, 2, 3, 4, 5, 6, 7)],
            1: [(d_kv, n, d_rot, d_cos, d_sin) for n in range(8)] + [(d_q, n, d_rot, d_cos, d_sin) for n in range(8)],
            2: [(r_proj, n, r_rot, r_cos, r_sin) for n in range(8)] + [(r_proj, n, l_rot, l_cos, l_sin) for n in range(16, 24)],
        }
        rope_tmp = {0: g_rt, 1: d_rt, 2: r_rt}
        rot_done = [sem(f"rot_done{m}") for m in range(3)]
        rot_read = [sem(f"rot_read{m}") for m in range(3)]
        roped = [sem(f"roped{m}") for m in range(3)]
        v_turned = [sem(f"v_turned{m}") for m in range(4)]
        v_stored = [sem(f"v_stored{m}") for m in range(4)]
        kswap = sem("kswap")
        kswap_stored = sem("kswap_stored")

        def v_groups(m):
            out = []
            if m == 0:
                for i in range(2):
                    out.append(([g_proj[:, 10 + i, t * P:(t + 1) * P] for t in range(4)], g_vn[:, :, i * P:(i + 1) * P]))
            if m == 1:
                for i in range(8):
                    out.append(([d_kv[:, 8 + i, t * P:(t + 1) * P] for t in range(4)], d_vn[:, :, i * P:(i + 1) * P]))
            if m == 2:
                for t in range(2):
                    for tile0, c0 in ((8, 0), (24, 512)):
                        out.append(([r_proj[:, tile0 + i, t * P:(t + 1) * P] for i in range(4)],
                                    r_vn[:, t, c0:c0 + 512].rearrange("p (g n) -> p g n", g=4)))
            if m == 3:
                for t in range(2):
                    for c0 in (0, 4):
                        out.append(([a_proj[:, 8 + c0 + i, t * P:(t + 1) * P] for i in range(4)],
                                    a_vn[:, t, c0 * P:c0 * P + 512].rearrange("p (g n) -> p g n", g=4)))
            return out

        def stat_of(h, b):
            if h.joined:
                return bank[b][:, 0:S].rearrange("p (o n) -> p o n", o=1).to_broadcast([P, 2, S])
            return bank[b][:, :].rearrange("p (e n) -> p e n", e=2)

        class HeadNorm:
            def __init__(self, name, data, chunks, joined, centre, gate, x0, out, scale=None):
                self.data, self.chunks, self.joined, self.centre = data, chunks, joined, centre
                self.gate, self.x0, self.out, self.scale = gate, x0, out, scale
                self.mean = sem(f"{name}_mean")
                self.centred = sem(f"{name}_centred")
                self.squared = sem(f"{name}_squared")
                self.var = sem(f"{name}_var")
                self.root = sem(f"{name}_root")
                self.gated = sem(f"{name}_gated")
                self.high = sem(f"{name}_high")
                self.sig = sem(f"{name}_sig")
        hn = {2: HeadNorm("rhn", r_o, 2, False, True, (r_proj, 12), 0, mix_out[2]),
              3: HeadNorm("ahn", a_o, 4, True, True, (a_proj, 16), 0, mix_out[3])}
        mix_in = [sem(f"mix_in{m}") for m in range(4)]
        ret_scores, ret_masked, ret_o = sem("ret_scores"), sem("ret_masked"), sem("ret_o")
        lam_prod, lam_sum, lam_exp, lam_done = sem("lam_prod"), sem("lam_sum"), sem("lam_exp"), sem("lam_done")
        gs = {n: sem("gla_" + n) for n in ("wsplit", "low", "lowc", "z", "znabs", "ln", "la", "b", "bs", "eb", "qt", "kt", "bd", "el",
                                           "ko", "kturn", "kstore", "sc", "sm", "kv", "st", "zero", "o")}

        last_proj = {}
        seen = None
        for kind, what in steps:
            if kind == "gemm":
                seen = what
            if kind == "mix":
                last_proj[what] = seen

        consts = {0: [(g_cos, "axial_cos"), (g_sin, "axial_sin"), (g_rot, "axial_rot"), (g_swap, "swap"), (g_mask, "gqa_mask")],
                  1: [(d_cos, "axial_cos"), (d_sin, "axial_sin"), (d_rot, "axial_rot"), (d_lam, "diff_lambda")],
                  2: [(r_cos, "ret_cos"), (r_sin, "ret_sin"), (r_rot, "ret_rot"), (l_cos, "dil_cos"), (l_sin, "dil_sin"),
                      (l_rot, "dil_rot"), (r_mask, "ret_mask"), (r_dmask, "dil_mask")],
                  3: [(a_sum, "gla_sum"), (a_mask, "gla_mask"), (a_w2, "gla_w_a2_2"), (a_ba, "gla_b_a_2"), (a_wr, None)]}
        tables_at = {}
        total = 0
        for m in range(4):
            total += 16 * len(consts[m])
            tables_at[m] = total
        turn_before_mix = {0: 2, 1: 5, 2: 8, 3: 11}

        block = ctx.enter_context(nc.Block())

        @block.sync
        def _(sp):
            ada = rows(A["ada_w"][0])
            for u in range(ADA_FIRST // 2):
                sp.dma_start(ada_first[:, u], ada[:, :, u * 256:(u + 1) * 256]).then_inc(ada_first_ready[u], 16)

            for g in gemms:
                def load(i):
                    it = g.p0 // 4 + i
                    for b in range(4):
                        if g.p0 > 0 or not isinstance(i, int):
                            sp.wait_ge(split_done, 4 * it + (b - 3))
                        sp.dma_start(raw[:, b, 0:g.k, :], g.src(i, b)).then_inc(raw_ready[b], 16)
                load(0)
                with sp.Fori(1, g.iters) as i:
                    load(i)

        @block.gpsimd
        def _(pool):
            pool.dma_start(cols[:, :], A["cols"]).then_inc(in_loaded, 16)
            pool.dma_start(csil[:, :, :], A["c_cols"]).then_inc(in_loaded, 16)
            pool.dma_start(ident[:, :], A["ident"]).then_inc(in_loaded, 16)
            pool.dma_start(xT[:, :, :], A["xT"].rearrange("(k p) n -> p k n", p=P)).then_inc(in_loaded, 16)
            def stream_ada(g):
                pool.wait_ge(sq_sum, g.norm_sums)

                def load(tile, layer, col):
                    pool.wait_ge(ada_used, tile)
                    pool.dma_start(ada_slot[:, :, :], rows(A["ada_w"][layer])[:, :, bass.ds(col, P)]).then_inc(ada_ready, 16)

                tiles = min(4 * g.iters, 2 * ADA_TILES - g.ada)
                if g.ada < ADA_TILES < g.ada + tiles:
                    with pool.Fori(g.ada, ADA_TILES) as n:
                        load(n, 0, n * P)
                    with pool.Fori(ADA_TILES, g.ada + tiles) as n:
                        load(n, 1, n * P - ADA_TILES * P)
                else:
                    layer = g.ada // ADA_TILES
                    with pool.Fori(g.ada, g.ada + tiles) as n:
                        load(n, layer, n * P - layer * ADA_TILES * P)

            def load_tables(m):
                pool.wait_ge(arena_free, turn_before_mix[m])
                for dst, name in consts[m]:
                    if name is None:
                        pool.wait_ge(gs["zero"], 1)
                        pool.dma_start(a_wr[:, :, 0:GLA_R], rows(A["gla_w_in_2"][0])[:, :, 3072:3072 + GLA_R]).then_inc(tables, 16)
                    else:
                        src = A[name]
                        d = dst[tuple([slice(None)] * len(dst.shape))]
                        pool.dma_start(d, src).then_inc(tables, 16)

            for kind, what in steps:
                if kind == "gemm" and what.ada is not None:
                    stream_ada(what)
                if kind == "mix_start":
                    load_tables(what)
            pool.wait_ge(tables, tables_at[3])

        @block.tensor
        def _(pe):
            pe.wait_ge(csil_ready, 1)
            pe.wait_ge(setup_done, 1)
            for u in range(ADA_FIRST // 2):
                pe.wait_ge(ada_first_ready[u], 16)
                for half in range(2):
                    c0 = 2 * (2 * u + half)
                    for k in range(DT):
                        last = nc.tensor.matmul(bank[7][:, c0:c0 + 2], ada_first[:, u, k, half * P:(half + 1) * P],
                                                csil[:, k, :], start=(k == 0), stop=(k == DT - 1))
            last.then_inc(ada_used, ADA_FIRST)

            def ada_piece(g, i, b):
                n = 4 * i + (g.ada + b)
                pe.wait_ge(ada_ready, n * 16 - 16 * (ADA_FIRST - 1))
                if b == 0:
                    pe.wait_ge(ada_out, i + g.ada // 4)
                for k in range(DT):
                    last = nc.tensor.matmul(bank[7][:, 2 * b:2 * b + 2], ada_slot[:, k, :], csil[:, k, :],
                                            start=(k == 0), stop=(k == DT - 1))
                last.then_inc(ada_used, 1)

            def piece(g, i, b, first):
                a = b % 2
                pe.wait_ge(split_done, g.p0 + 4 * i + (b + 1))
                down = g.k == KH
                if g.kind == "res":
                    out = bank[4 + (b // 2 if down else b % 2)]
                    if not down or a == 0:
                        r = g.r0 + (2 * i + b // 2 if down else 4 * i + b)
                        pe.wait_ge(res_done, r + 1)
                else:
                    out = bank[b]
                    pe.wait_ge(dve_bank if a else act_bank, 2 * (g.e0 + i) + (1 + b // 2))
                for k in range(g.k):
                    kk = k + (KH * a if down else 0)
                    if first and (b < 2 if down else b == 0):
                        pe.wait_ge(*g.ready(kk))
                    high, low = g.rhs(kk, g.t)
                    start = k == 0 and (a == 0 or not down)
                    stop = k == g.k - 1 and (a == 1 or not down)
                    o = out[:, 0:g.t]
                    nc.tensor.matmul(o, WH[:, b, k, :], high, start=start, stop=False)
                    nc.tensor.matmul(o, WH[:, b, k, :], low, start=False, stop=False)
                    last = nc.tensor.matmul(o, WL[:, b, k, :], high, start=False, stop=stop)
                last.then_inc(piece_done, 1)

            def gemm(g):
                for b in range(4):
                    piece(g, 0, b, True)
                    if g.ada is not None:
                        ada_piece(g, 0, b)
                whole = g.iters if g.ada is None else min(g.iters, (2 * ADA_TILES - g.ada) // 4)
                with pe.Fori(1, whole) as i:
                    for b in range(4):
                        piece(g, i, b, False)
                        if g.ada is not None:
                            ada_piece(g, i, b)
                for i in range(whole, g.iters):
                    for b in range(4):
                        piece(g, i, b, False)

            def norm_sums(n):
                for k in range(DT):
                    pe.wait_ge(sq_ready, DT * n["i"] + k + 1)
                    nc.tensor.matmul(bank[6][:, 0:n["t"]], ones_d[:, :], sq[:, k % 2, 0:n["t"]], start=(k == 0),
                                     stop=(k == DT - 1)).then_inc(sq_sum, 1)

            def banks_free(g):
                pe.wait_ge(act_bank, 2 * (g.e0 + g.iters) + 2)
                pe.wait_ge(dve_bank, 2 * (g.e0 + g.iters) + 2)
                pe.wait_ge(res_done, g.r0 + 2)

            def rotate(m):
                for n, (src, tile, rot, _, _) in enumerate(ropes[m]):
                    if n >= 4:
                        pe.wait_ge(rot_read[m], n - 3)
                    nc.tensor.matmul(bank[n % 4][:, 0:S], rot[:, :], src[:, tile, 0:S], start=True,
                                     stop=True).then_inc(rot_done[m], 1)

            def turn_v(m):
                for n, (blocks, _) in enumerate(v_groups(m)):
                    if n >= 2:
                        pe.wait_ge(v_stored[m], n - 1)
                    for j, blk in enumerate(blocks):
                        last = nc.tensor.transpose(bank[6 + n % 2][:, j * P:(j + 1) * P], blk, ident[:, :])
                    last.then_inc(v_turned[m], 1)

            def attention(a):
                jobs, n = a.jobs, len(a.jobs)
                for s in range(n + 5):
                    if s < n:
                        j = jobs[s]
                        if s >= 2:
                            pe.wait_ge(a.max, len(j["maps"]) * (s - 1))
                        for m, (q, k) in enumerate(j["maps"]):
                            nc.tensor.matmul(bank[2 * (s % 2) + m][:, 0:j["nk"]], q, k, start=True,
                                             stop=True).then_inc(a.scores, 1)
                    if 2 <= s < n + 2:
                        j = jobs[s - 2]
                        two = len(j["maps"]) == 2
                        pe.wait_ge(a.norm if two else a.exp, s - 1)
                        if s >= 4:
                            pe.wait_ge(a.pt_ready, s - 3)
                        probs = a.p[:, s % 2, :] if two else a.logits(s - 2)
                        for c in range(j["nk"] // P):
                            last = nc.tensor.transpose(bank[4 + s % 2][:, c * P:(c + 1) * P], probs[:, c * P:(c + 1) * P], ident[:, :])
                        last.then_inc(a.turned, 1)
                    if 3 <= s < n + 3:
                        j = jobs[s - 3]
                        pe.wait_ge(a.pt_ready, s - 2)
                        if s >= 5:
                            pe.wait_ge(a.o_read, s - 4)
                        nk = j["nk"] // P
                        for c in range(nk):
                            last = nc.tensor.matmul(bank[6 + (s - 3) % 2][:, 0:j["width"]], a.pt[:, (s - 3) % 2, c * P:(c + 1) * P],
                                                    j["v"][c], start=(c == 0), stop=(c == nk - 1))
                        last.then_inc(a.o_done, 1)
                    if s >= 5 and jobs[s - 5]["last"]:
                        o = jobs[s - 5]["o"]
                        pe.wait_ge(a.o_read, s - 4)
                        if o >= 2:
                            pe.wait_ge(a.o_free, o - 1)
                        for t in range(a.cols // P):
                            last = nc.tensor.transpose(bank[1 + 2 * (o % 2)][:, t * P:(t + 1) * P],
                                                       a.onat[:, t, o * P:(o + 1) * P], ident[:, :])
                        last.then_inc(a.o_turned, 1)
                if a.squares is None:
                    pe.wait_ge(a.o_free, jobs[-1]["o"] + 1)

            def head_norm(h):
                w = S if h.joined else 2 * S
                def stat(c, src, b, done):
                    if h.joined:
                        for e in range(2):
                            last = nc.tensor.matmul(bank[b][:, 0:S], ones_e[:, :], src[:, e, :], start=(e == 0), stop=(e == 1))
                    else:
                        last = nc.tensor.matmul(bank[b][:, 0:w], ones_e[:, :], src, start=True, stop=True)
                    last.then_inc(done, 1)
                for c in range(h.chunks):
                    d = h.data[:, 2 * c:2 * c + 2, :]
                    if h.centre:
                        if c >= 2:
                            pe.wait_ge(h.centred, c - 1)
                        stat(c, d, c % 2, h.mean)
                    pe.wait_ge(h.squared, c + 1)
                    if c >= 2:
                        pe.wait_ge(h.gated, c - 1)
                    stat(c, sq[:, c % 2, :].rearrange("p (e n) -> p e n", e=2), 2 + c % 2, h.var)

            def mix0():
                pe.wait_ge(tables, tables_at[0])
                banks_free(last_proj[0])
                rotate(0)
                turn_v(0)
                for i in range(2):
                    pe.wait_ge(roped[0], i + 1)
                    nc.tensor.matmul(bank[4 + i][:, :], g_swap[:, :], g_proj[:, 8 + i, :], start=True, stop=True).then_inc(kswap, 1)
                pe.wait_ge(kswap_stored, 2)
                pe.wait_ge(v_stored[0], 2)
                pe.wait_ge(roped[0], len(ropes[0]))
                attention(gqa)

            def mix1():
                pe.wait_ge(tables, tables_at[1])
                banks_free(last_proj[1])
                pe.wait_ge(lam_prod, 1)
                nc.tensor.matmul(bank[4][:, 0:2], ones_1[0:64, :], d_lw[0:64, 8:10], start=True, stop=True).then_inc(lam_sum, 1)
                rotate(1)
                turn_v(1)
                pe.wait_ge(v_stored[1], 8)
                pe.wait_ge(lam_exp, 1)
                pe.wait_ge(roped[1], len(ropes[1]))
                attention(dif)
                for h in range(H_DIFF):
                    pe.wait_ge(dif_scaled, 1 + h // 4)
                    for t in range(2):
                        c0 = (h % 2) * S + t * P
                        last = nc.tensor.transpose(bank[h // 2][:, c0:c0 + P], d_o[:, t, h * P:(h + 1) * P], ident[:, :])
                    if h % 2:
                        last.then_inc(dif_turned, 1)

            def mix2():
                pe.wait_ge(tables, tables_at[2])
                banks_free(last_proj[2])
                rotate(2)
                turn_v(2)
                pe.wait_ge(v_stored[2], 4)
                pe.wait_ge(roped[2], len(ropes[2]))
                for h in range(H_RET):
                    if h >= 2:
                        pe.wait_ge(ret_masked, h - 1)
                    q, k = r_proj[:, h, :], r_proj[:, 4 + h, :]
                    nc.tensor.matmul(bank[h % 2][:, 0:256], k[:, 0:P], q[:, 0:256], start=True, stop=True)
                    nc.tensor.matmul(bank[h % 2][:, 256:384], k[:, P:256], q[:, P:256], start=True, stop=True).then_inc(ret_scores, 1)
                    pe.wait_ge(ret_masked, h + 1)
                    if h >= 2:
                        pe.wait_ge(mix_in[2], h - 1)
                    o = bank[2 + h % 2]
                    nc.tensor.matmul(o[:, 0:256], r_vn[:, 0, h * P:(h + 1) * P], r_sm[:, h % 2, 0:256], start=True, stop=False)
                    nc.tensor.matmul(o[:, P:256], r_vn[:, 1, h * P:(h + 1) * P], r_sm[:, h % 2, 256:384], start=False,
                                     stop=True).then_inc(ret_o, 1)
                pe.wait_ge(mix_in[2], H_RET)
                head_norm(hn[2])
                pe.wait_ge(hn[2].gated, 2)
                attention(dil)

            def mix3():
                pe.wait_ge(tables, tables_at[3])
                banks_free(last_proj[3])
                pe.wait_ge(gs["wsplit"], 1)
                for k in range(DT):
                    nc.tensor.matmul(bank[4][:, 0:S], a_wh[:, k, :], XH[:, k, 0:S], start=(k == 0), stop=False)
                    nc.tensor.matmul(bank[4][:, 0:S], a_wh[:, k, :], XL[:, k, 0:S], start=False, stop=False)
                    last = nc.tensor.matmul(bank[4][:, 0:S], a_wl[:, k, :], XH[:, k, 0:S], start=False, stop=(k == DT - 1))
                last.then_inc(gs["low"], 1)
                pe.wait_ge(gs["lowc"], 1)
                for t in range(2):
                    nc.tensor.matmul(bank[t][:, :], a_low[:, t * P:(t + 1) * P], a_w2[:, :], start=True, stop=False)
                    nc.tensor.matmul(bank[t][:, :], ones_1[0:1, :], a_ba[:, :], start=False, stop=True).then_inc(gs["z"], 1)
                turn_v(3)
                pe.wait_ge(gs["la"], 1)
                for h in range(H_GLA):
                    for t in range(2):
                        c0 = (h % 2) * S + t * P
                        last = nc.tensor.matmul(bank[2 + h // 2][:, c0:c0 + P], a_la[:, t, h * P:(h + 1) * P], a_sum[:, :],
                                                start=True, stop=True)
                last.then_inc(gs["b"], 1)
                pe.wait_ge(v_stored[3], 4)
                pe.wait_ge(gs["ko"], 1)
                for t in range(2):
                    for h in range(H_GLA):
                        last = nc.tensor.transpose(bank[6 + t][:, h * P:(h + 1) * P], a_el[:, h, t * P:(t + 1) * P], ident[:, :])
                    last.then_inc(gs["kturn"], 1)
                pe.wait_ge(gs["kstore"], 2)
                for h in range(H_GLA):
                    if h >= 2:
                        pe.wait_ge(gs["sm"], h - 1)
                    pe.wait_ge(gs["bs"], 1)
                    pe.wait_ge(gs["qt"], 1)
                    pe.wait_ge(gs["kt"], 1)
                    for t in range(2):
                        last = nc.tensor.matmul(bank[h % 2][:, t * P:(t + 1) * P], a_proj[:, 4 + h, t * P:(t + 1) * P],
                                                a_proj[:, h, t * P:(t + 1) * P], start=True, stop=True)
                    last.then_inc(gs["sc"], 1)
                    if h >= 1:
                        pe.wait_ge(gs["st"], 3 * h)
                    for n in range(3):
                        b0 = (n % 2) * 64
                        nc.tensor.matmul(bank[2 + n][:, 0:256], a_kn[b0:b0 + 64, n // 2, h * P:(h + 1) * P],
                                         a_vn[b0:b0 + 64, n // 2, h * 256:(h + 1) * 256], start=True, stop=True).then_inc(gs["kv"], 1)
                    pe.wait_ge(gs["sm"], h + 1)
                    pe.wait_ge(gs["st"], 3 * h + 3)
                    if h >= 2:
                        pe.wait_ge(mix_in[3], h - 1)
                    o = bank[6 + h % 2]
                    for e in range(2):
                        v0 = h * 256 + e * P
                        for t in range(2):
                            nc.tensor.matmul(o[:, e * 256 + t * P:e * 256 + (t + 1) * P], a_vn[:, t, v0:v0 + P],
                                             a_sm[:, h % 2, t * P:(t + 1) * P], start=(e == 0 and t == 0), stop=False)
                        for n in range(1, 4):
                            c0 = e * 256 + n * 64
                            last = nc.tensor.matmul(o[:, c0:c0 + 64], a_st[:, h % 2, n - 1, e * P:(e + 1) * P],
                                                    a_proj[:, h, n * 64:(n + 1) * 64], start=False, stop=(e == 1 and n == 3))
                    last.then_inc(gs["o"], 1)
                pe.wait_ge(mix_in[3], H_GLA)
                head_norm(hn[3])

            mixes = [mix0, mix1, mix2, mix3]
            for kind, what in steps:
                if kind == "gemm":
                    gemm(what)
                elif kind == "norm":
                    norm_sums(what)
                elif kind == "mix":
                    mixes[what]()

        @block.scalar
        def _(act):
            count = [0]

            def link(ins):
                count[0] += 1
                ins.then_inc(act_self, 1)
                act.wait_ge(act_self, count[0])

            act.wait_ge(in_loaded, 64)
            act.wait_ge(setup_done, 1)
            nc.scalar.activation(csil[:, :, :], csil[:, :, :], ACTF.Silu).then_inc(csil_ready, 1)

            def high(g, i, b):
                q = g.p0 + 4 * i + b
                act.wait_ge(raw_ready[b], (g.p0 // 4 + i) * 16 + 16)
                if g.p0 > 0 or not isinstance(i, int):
                    act.wait_ge(piece_done, q - 3)
                nc.scalar.activation(WH[:, b, 0:g.k, :], raw[:, b, 0:g.k, :], ACTF.Copy).then_inc(h_done, 1)

            for b in range(4):
                high(gemms[0], 0, b)

            def body(g, i, ahead):
                q = g.p0 + 4 * i
                t = g.t
                for b in range(4):
                    if g.kind == "up" and b % 2 == 0:
                        act.wait_ge(piece_done, q + (b + 1))
                        nc.scalar.activation(sg[:, b // 2, 0:t], bank[b][:, 0:t], ACTF.Silu).then_inc(act_bank, 1)
                    if g.kind == "proj" and b % 2 == 0:
                        act.wait_ge(piece_done, q + (b + 1))
                        nc.scalar.activation(g.dst[:, bass.ds(i * 4 + b, 1), 0:t], bank[b][:, 0:t].rearrange("p (o n) -> p o n", o=1),
                                             ACTF.Copy).then_inc(act_bank, 1)
                    if g.kind == "up" and b == 2:
                        hidden(g, i, 0)
                    if ahead:
                        high(*ahead, b)
                    if g.kind == "up" and b == 3:
                        hidden(g, i, 1)

            def hidden(g, i, half):
                f = 2 * i + half
                act.wait_ge(dve_bank, 2 * (g.e0 + i) + (3 + half))
                nc.scalar.activation(HH[:, bass.ds(f, 1), 0:g.t], hf[:, half:half + 1, 0:g.t], ACTF.Copy).then_inc(hid_high, 1)

            def gemm(g):
                if g.kind == "up":
                    act.wait_ge(arena_free, turn[0])
                if g.kind == "proj":
                    act.wait_ge(arena_free, turn[0])
                with act.Fori(0, g.iters - 1) as i:
                    body(g, i, (g, i + 1))
                nxt = following[id(g)]
                body(g, g.iters - 1, (nxt, 0) if nxt else None)

            def norm_act(n):
                t = n["t"]
                for k in range(DT):
                    if n["last"]:
                        act.wait_ge(res_done, x_ready(n, k))
                    if k == 0 and not n["last"] and n["i"] > 0:
                        act.wait_ge(n_mul, DT * n["i"])
                    if k >= 2 or n["i"] > 0:
                        act.wait_ge(sq_sum, DT * n["i"] + k - 1)
                    nc.scalar.activation(sq[:, k % 2, 0:t], xT[:, k, 0:t], ACTF.Square).then_inc(sq_ready, 1)
                act.wait_ge(sq_sum, DT * n["i"] + DT)
                nc.scalar.activation(rstd[:, 0:t], bank[6][:, 0:t], ACTF.Sqrt, bias=eps[:, 0:1]).then_inc(n_root, 1)
                if n["mode"] != "split":
                    return
                for k in range(DT):
                    act.wait_ge(n_mul, DT * n["i"] + k + 1)
                    if n["shift"]:
                        for half in range(t // S):
                            cs = slice(half * S, half * S + S)
                            last = nc.scalar.activation(XH[:, k, cs], tn[:, k % 2, cs], ACTF.Identity, bias=n["shift"](k, half))
                    else:
                        last = nc.scalar.activation(XH[:, k, 0:t], tn[:, k % 2, 0:t], ACTF.Copy)
                    last.then_inc(n_high, 1)

            def store_v(m):
                for n, (_, dst) in enumerate(v_groups(m)):
                    act.wait_ge(v_turned[m], n + 1)
                    nc.scalar.activation(dst, bank[6 + n % 2][:, :].rearrange("p (g n) -> p g n", g=4), ACTF.Copy).then_inc(v_stored[m], 1)

            def attention(a):
                jobs, n = a.jobs, len(a.jobs)
                for s in range(n + 6):
                    if 2 <= s < n + 2:
                        nk = jobs[s - 2]["nk"]
                        act.wait_ge(a.turned, s - 1)
                        nc.scalar.activation(a.pt[:, s % 2, 0:nk], bank[4 + s % 2][:, 0:nk], ACTF.Copy).then_inc(a.pt_ready, 1)
                    if s < n:
                        nm, sm = len(jobs[s]["maps"]), a.small[:, s, :]
                        act.wait_ge(a.max, nm * s + nm)
                        for m in range(nm):
                            last = nc.scalar.activation(a.logits(s, m), a.logits(s, m), ACTF.Exp, bias=sm[:, m:m + 1],
                                                        scale=HD ** -0.5, accum_out=sm[:, 2 + m:3 + m])
                        if a.sink:
                            c = COL_AT["sinks"] + jobs[s]["head"]
                            last = nc.scalar.activation(sm[:, 4:5], cols[:, c:c + 1], ACTF.Exp, bias=sm[:, 0:1])
                        last.then_inc(a.exp, 1)
                    if a.squares is not None and 5 <= s < n + 5:
                        j = jobs[s - 5]
                        act.wait_ge(a.o_read, s - 4)
                        if s >= 13:
                            act.wait_ge(a.squared, s - 12)
                        i = s - 5
                        nc.scalar.activation(sq[:, (i // 4) % 2, (i % 4) * P:(i % 4 + 1) * P], a.onat[:, j["t"], j["c0"]:j["c0"] + P],
                                             ACTF.Square, accum_out=a.squares[:, j["t"] * 8 + j["o"]:j["t"] * 8 + j["o"] + 1]).then_inc(a.squared, 1)
                    if a.squares is None and s >= 6 and jobs[s - 6]["last"]:
                        o = jobs[s - 6]["o"]
                        act.wait_ge(a.o_turned, o + 1)
                        nc.scalar.activation(XH[:, a.x0 + o, 0:a.cols], bank[1 + 2 * (o % 2)][:, 0:a.cols], ACTF.Copy).then_inc(a.o_high, 1)

            def head_norm(h):
                for c in range(h.chunks):
                    d = h.data[:, 2 * c:2 * c + 2, :]
                    dst = sq[:, c % 2, :].rearrange("p (e n) -> p e n", e=2)
                    if h.centre:
                        act.wait_ge(h.centred, c + 1)
                    if c >= 2:
                        act.wait_ge(h.var, c - 1)
                    nc.scalar.activation(dst, d, ACTF.Square).then_inc(h.squared, 1)
                    if h.gate:
                        src, t0 = h.gate
                        if c >= 2:
                            act.wait_ge(h.gated, c - 1)
                        nc.scalar.activation(sg[:, c % 2, :].rearrange("p (e n) -> p e n", e=2),
                                             src[:, t0 + 2 * c:t0 + 2 * c + 2, :], ACTF.Silu).then_inc(h.sig, 1)
                    act.wait_ge(h.var, c + 1)
                    nc.scalar.activation(tn[:, c % 2, :].rearrange("p (e n) -> p e n", e=2), stat_of(h, 2 + c % 2), ACTF.Sqrt,
                                         bias=eps[:, 0:1]).then_inc(h.root, 1)
                    act.wait_ge(h.gated, c + 1)
                    nc.scalar.activation(XH[:, h.x0 + 2 * c:h.x0 + 2 * c + 2, 0:S], h.data[:, 2 * c:2 * c + 2, :],
                                         ACTF.Copy).then_inc(h.high, 1)

            def mix0():
                act.wait_ge(act_bank, 2 * (last_proj[0].e0 + last_proj[0].iters) + 2)
                store_v(0)
                for i in range(2):
                    act.wait_ge(kswap, i + 1)
                    nc.scalar.activation(g_ks[:, i, :], bank[4 + i][:, :], ACTF.Copy).then_inc(kswap_stored, 1)
                attention(gqa)

            def mix1():
                act.wait_ge(lam_sum, 1)
                nc.scalar.activation(d_lw[:, 10:12], bank[4][:, 0:2], ACTF.Exp).then_inc(lam_exp, 1)
                store_v(1)
                attention(dif)
                act.wait_ge(dif.squared, len(dif.jobs))
                nc.scalar.activation(d_ss[:, :], d_ss[:, :], ACTF.Sqrt, scale=1.0 / P, bias=eps[:, 0:1]).then_inc(dif_root, 1)
                for i in range(4):
                    act.wait_ge(dif_turned, i + 1)
                    nc.scalar.activation(XH[:, 2 * i:2 * i + 2, 0:S], bank[i][:, :].rearrange("p (e n) -> p e n", e=2), ACTF.Copy,
                                         scale=d_lw[:, 0:1]).then_inc(dif_high, 1)

            def mix2():
                store_v(2)
                for h in range(H_RET):
                    act.wait_ge(ret_o, h + 1)
                    nc.scalar.activation(r_o[:, h, :], bank[2 + h % 2][:, 0:256], ACTF.Copy).then_inc(mix_in[2], 1)
                head_norm(hn[2])
                attention(dil)

            def mix3():
                act.wait_ge(gs["low"], 1)
                nc.scalar.activation(a_low[:, :], bank[4][0:GLA_R, 0:S], ACTF.Copy).then_inc(gs["lowc"], 1)
                store_v(3)
                act.wait_ge(gs["znabs"], 2)
                link(nc.scalar.activation(a_la[:, :, :], a_la[:, :, :], ACTF.Exp))
                nc.scalar.activation(a_la[:, :, :], a_la[:, :, :], ACTF.Ln, bias=ones_1[:, 0:1]).then_inc(gs["ln"], 1)
                act.wait_ge(gs["bs"], 1)
                nc.scalar.activation(a_eb[:, :, :], a_b[:, :, :], ACTF.Exp).then_inc(gs["eb"], 1)
                act.wait_ge(gs["bd"], 1)
                nc.scalar.activation(a_en[:, :, :], a_b[:, :, :], ACTF.Exp, scale=-1.0).then_inc(gs["eb"], 1)
                nc.scalar.activation(a_el[:, :, :], a_el[:, :, :], ACTF.Exp).then_inc(gs["el"], 1)
                for t in range(2):
                    act.wait_ge(gs["kturn"], t + 1)
                    nc.scalar.activation(a_kn[:, t, :], bank[6 + t][:, :], ACTF.Copy).then_inc(gs["kstore"], 1)
                for h in range(H_GLA):
                    act.wait_ge(gs["o"], h + 1)
                    nc.scalar.activation(a_o[:, 2 * h:2 * h + 2, :], bank[6 + h % 2][:, :].rearrange("p (e n) -> p e n", e=2),
                                         ACTF.Copy).then_inc(mix_in[3], 1)
                act.wait_ge(mix_in[3], H_GLA)
                head_norm(hn[3])

            mixes = [mix0, mix1, mix2, mix3]
            turn = [1]
            for kind, what in steps:
                if kind == "gemm":
                    gemm(what)
                elif kind == "norm":
                    norm_act(what)
                elif kind == "mix":
                    mixes[what]()
                    turn[0] += 1
                elif kind == "ffn_end":
                    turn[0] += 1
            act.wait_ge(n_mul, DT * state["norms"])
            act.dma_start(A["out"].rearrange("(k p) n -> p k n", p=P), xT[:, :, 0:S]).then_inc(out_done, 16)
            act.wait_ge(out_done, 16)

        @block.vector
        def _(dve):
            count = [0]

            def link(ins):
                count[0] += 1
                ins.then_inc(dve_self, 1)
                dve.wait_ge(dve_self, count[0])

            turns = [0]

            def release():
                turns[0] += 1
                nc.vector.memset(token[:, turns[0]:turns[0] + 1], 0.0).then_inc(arena_free, 1)

            nc.vector.memset(ones_d[:, :], 1.0 / D)
            nc.vector.memset(ones_1[:, :], 1.0)
            nc.vector.memset(eps[:, :], EPS).then_inc(hid_low, 2)
            nc.vector.memset(ones_e[:, :], 1.0 / P).then_inc(setup_done, 1)
            nc.vector.memset(halves[:, 0, :], 0.5).then_inc(dve_bank, 2)
            nc.vector.memset(halves[:, 1, :], 1.0).then_inc(res_done, 2)
            nc.vector.memset(token[:, 0:1], 0.0).then_inc(act_bank, 2)

            def low(g, i, b):
                dve.wait_ge(h_done, g.p0 + 4 * i + (b + 1))
                nc.vector.tensor_tensor(WL[:, b, 0:g.k, :], raw[:, b, 0:g.k, :], WH[:, b, 0:g.k, :].bitcast(F32),
                                        ALU.subtract).then_inc(split_done, 1)

            ab = COL_AT["ada_b"]

            def ada_store(tile0, tiles):
                bias = cols[:, bass.ds(tile0 + ab, tiles)].rearrange("p (n o) -> p n o", o=1).to_broadcast([P, tiles, 2])
                nc.vector.tensor_tensor(mods[:, bass.ds(tile0, tiles), :], bank[7][:, 0:2 * tiles].rearrange("p (n o) -> p n o", o=2),
                                        bias, ALU.add).then_inc(ada_out, tiles // 4)

            def derive(t0, t1):
                dve.wait_ge(ada_out, t1 // 4)
                for l in range(2):
                    for n in range(3):
                        m0 = l * ADA_TILES + 3 * n * DT
                        if t0 < m0 + 2 * DT <= t1:
                            w0 = COL_AT["norm_w"] + (3 * l + n) * DT
                            w = cols[:, w0:w0 + DT].rearrange("p (n o) -> p n o", o=1).to_broadcast([P, DT, 2])
                            link(nc.vector.scalar_tensor_tensor(out=scaleA[:, l, n], in0=mods[:, m0 + DT:m0 + 2 * DT, :], scalar=1.0,
                                                                in1=w, op0=ALU.add, op1=ALU.mult))
                        if t0 < m0 + 3 * DT <= t1:
                            link(nc.vector.tensor_scalar(gates[:, l, n], mods[:, m0 + 2 * DT:m0 + 3 * DT, :],
                                                         1.0 if n == 1 else 0.5, None, ALU.mult))

            dve.wait_ge(in_loaded, 64)
            dve.wait_ge(ada_used, ADA_FIRST)
            ada_store(0, ADA_FIRST)
            derive(0, ADA_FIRST)
            release()

            for b in range(4):
                low(gemms[0], 0, b)

            def body(g, i, ahead):
                q, t = g.p0 + 4 * i, g.t
                down = g.k == KH
                for b in range(4):
                    if g.kind == "up":
                        half = b // 2
                        if b % 2:
                            dve.wait_ge(piece_done, q + (b + 1))
                            dve.wait_ge(act_bank, 2 * (g.e0 + i) + (3 + half))
                            dve.wait_ge(hid_low, 2 * i + (g.hid0 + half + 1))
                            nc.vector.tensor_tensor(hf[:, half, 0:t], sg[:, half, 0:t], bank[b][:, 0:t], ALU.mult).then_inc(dve_bank, 1)
                    if g.kind == "proj" and b % 2:
                        dve.wait_ge(piece_done, q + (b + 1))
                        nc.vector.tensor_copy(g.dst[:, bass.ds(i * 4 + b, 1), 0:t],
                                              bank[b][:, 0:t].rearrange("p (o n) -> p o n", o=1)).then_inc(dve_bank, 1)
                    if g.kind == "res" and (b % 2 or not down):
                        dve.wait_ge(piece_done, q + (b + 1))
                        d = res_tile(g, i, b)
                        src = bank[4 + (b // 2 if down else b % 2)]
                        for half in range(t // S):
                            cs = slice(half * S, half * S + S)
                            x = xT[:, bass.ds(d, 1), cs]
                            last = nc.vector.scalar_tensor_tensor(
                                out=x, in0=src[:, cs].rearrange("p (o n) -> p o n", o=1), scalar=g.gate(d, half), in1=x,
                                op0=ALU.mult, op1=ALU.add)
                        last.then_inc(res_done, 1)
                    if g.kind == "up" and b == 2:
                        hidden_low(g, i, 0)
                    if ahead:
                        low(*ahead, b)
                    if g.kind == "up" and b == 3:
                        hidden_low(g, i, 1)

            def hidden_low(g, i, half):
                f = 2 * i + half
                dve.wait_ge(hid_high, g.hid0 + f + 1)
                nc.vector.tensor_tensor(HL[:, bass.ds(f, 1), 0:g.t], hf[:, half:half + 1, 0:g.t],
                                        HH[:, bass.ds(f, 1), 0:g.t].bitcast(F32), ALU.subtract).then_inc(hid_low, 1)

            def gemm(g):
                nxt = following[id(g)]
                if g.ada is None:
                    with dve.Fori(0, g.iters - 1) as i:
                        body(g, i, (g, i + 1))
                    body(g, g.iters - 1, (nxt, 0) if nxt else None)
                    return

                def store(i):
                    dve.wait_ge(ada_used, 4 * i + (g.ada + 4))
                    ada_store(i * 4 + g.ada, 4)

                whole = min(g.iters, (2 * ADA_TILES - g.ada) // 4)
                with dve.Fori(0, min(whole, g.iters - 1)) as i:
                    body(g, i, (g, i + 1))
                    store(i)
                for i in range(whole, g.iters - 1):
                    body(g, i, (g, i + 1))
                body(g, g.iters - 1, (nxt, 0))
                if whole == g.iters:
                    store(g.iters - 1)
                derive(g.ada, g.ada + 4 * whole)

            def norm_dve(n):
                t, i0 = n["t"], DT * n["i"]
                dve.wait_ge(n_root, n["i"] + 1)
                link(nc.vector.reciprocal(rstd[:, 0:t], rstd[:, 0:t]))

                def scaled(k):
                    if n["mode"] == "split" and k >= 2:
                        dve.wait_ge(n_low, n["h0"] + k - 1)
                    for half in range(t // S):
                        cs = slice(half * S, half * S + S)
                        dst = tn[:, k % 2, cs] if n["mode"] == "split" else xT[:, k, cs]
                        last = nc.vector.scalar_tensor_tensor(out=dst, in0=xT[:, k, cs], scalar=n["weight"](k, half),
                                                              in1=rstd[:, cs], op0=ALU.mult, op1=ALU.mult)
                    last.then_inc(n_mul, 1)

                def rest(k):
                    dve.wait_ge(n_high, n["h0"] + k + 1)
                    if n["shift"]:
                        for half in range(t // S):
                            cs = slice(half * S, half * S + S)
                            last = nc.vector.scalar_tensor_tensor(
                                out=XL[:, k, cs], in0=tn[:, k % 2, cs], scalar=n["shift"](k, half),
                                in1=XH[:, k, cs].bitcast(F32), op0=ALU.add, op1=ALU.subtract)
                    else:
                        last = nc.vector.tensor_tensor(XL[:, k, 0:t], tn[:, k % 2, 0:t], XH[:, k, 0:t].bitcast(F32), ALU.subtract)
                    last.then_inc(n_low, 1)

                if n["mode"] != "split":
                    for k in range(DT):
                        scaled(k)
                    return
                scaled(0)
                for k in range(DT):
                    if k + 1 < DT:
                        scaled(k + 1)
                    rest(k)

            def rotate(m):
                tmp = rope_tmp[m]
                dve.wait_ge(tables, tables_at[m])
                for n, (src, tile, _, cos, sin) in enumerate(ropes[m]):
                    dve.wait_ge(rot_done[m], n + 1)
                    x = src[:, tile, 0:S]
                    if n >= 2:
                        dve.wait_ge(roped[m], n - 1)
                    nc.vector.tensor_tensor(tmp[:, n % 2, :], bank[n % 4][:, 0:S], sin[:, :], ALU.mult).then_inc(rot_read[m], 1)
                    link(nc.vector.tensor_tensor(x, x, cos[:, :], ALU.mult))
                    nc.vector.tensor_tensor(x, x, tmp[:, n % 2, :], ALU.add).then_inc(roped[m], 1)

            def attention(a):
                jobs, n = a.jobs, len(a.jobs)
                for s in range(n + 7):
                    if 1 <= s <= n:
                        nm, sm, nk = len(jobs[s - 1]["maps"]), a.small[:, s - 1, :], jobs[s - 1]["nk"]
                        dve.wait_ge(a.exp, s)
                        if a.sink:
                            link(nc.vector.tensor_tensor(sm[:, 2:3], sm[:, 2:3], sm[:, 4:5], ALU.add))
                        if nm == 1:
                            nc.vector.reciprocal(sm[:, 6:7], sm[:, 2:3]).then_inc(a.norm, 1)
                        else:
                            if s >= 3:
                                dve.wait_ge(a.turned, s - 2)
                            link(nc.vector.reciprocal(sm[:, 6:8], sm[:, 2:4]))
                            link(nc.vector.tensor_scalar(sm[:, 5:6], sm[:, 2:3], sm[:, 7:8], d_lw[:, 14:15], ALU.mult, ALU.mult))
                            nc.vector.scalar_tensor_tensor(out=a.p[:, (s - 1) % 2, 0:nk], in0=a.logits(s - 1, 1), scalar=sm[:, 5:6],
                                                           in1=a.logits(s - 1, 0), op0=ALU.mult, op1=ALU.add).then_inc(a.norm, 1)
                    if 4 <= s < n + 4:
                        j, sm = jobs[s - 4], a.small[:, s - 4, :]
                        dve.wait_ge(a.o_done, s - 3)
                        dve.wait_ge(a.norm, s - 3)
                        nc.vector.tensor_scalar(a.onat[:, j["t"], j["c0"]:j["c0"] + j["width"]], bank[6 + (s - 4) % 2][:, 0:j["width"]],
                                                sm[:, 6:7], None, ALU.mult).then_inc(a.o_read, 1)
                    if s < n:
                        j = jobs[s]
                        nm, sm, nk = len(j["maps"]), a.small[:, s, :], j["nk"]
                        if nm == 2 and s >= 2:
                            dve.wait_ge(a.norm, s - 1)
                        if nm == 1 and s >= 4:
                            dve.wait_ge(a.turned, s - 3)
                        for m in range(nm):
                            dve.wait_ge(a.scores, nm * s + m + 1)
                            link(nc.vector.tensor_tensor_reduce(
                                out=a.logits(s, m), in0=bank[2 * (s % 2) + m][:, 0:nk], in1=j["mask"], scale=1.0,
                                scalar=-3e38, op0=ALU.add, op1=ALU.max, accum_out=sm[:, 6 + m:7 + m]))
                            if a.sink:
                                nc.vector.tensor_scalar(sm[:, 0:1], sm[:, 6:7], -HD ** -0.5, g_nsink[:, j["head"]:j["head"] + 1],
                                                        ALU.mult, ALU.min).then_inc(a.max, 1)
                            else:
                                nc.vector.tensor_scalar(sm[:, m:m + 1], sm[:, 6 + m:7 + m], -HD ** -0.5, None, ALU.mult).then_inc(a.max, 1)
                    if a.squares is None and s >= 7 and jobs[s - 7]["last"]:
                        o = jobs[s - 7]["o"]
                        dve.wait_ge(a.o_high, o + 1)
                        nc.vector.tensor_tensor(XL[:, a.x0 + o, 0:a.cols], bank[1 + 2 * (o % 2)][:, 0:a.cols],
                                                XH[:, a.x0 + o, 0:a.cols].bitcast(F32), ALU.subtract).then_inc(a.o_free, 1)

            def head_norm(h):
                for c in range(h.chunks):
                    d = h.data[:, 2 * c:2 * c + 2, :]
                    r = tn[:, c % 2, :].rearrange("p (e n) -> p e n", e=2)
                    if h.centre:
                        dve.wait_ge(h.mean, c + 1)
                        nc.vector.tensor_tensor(d, d, stat_of(h, c % 2), ALU.subtract).then_inc(h.centred, 1)
                    dve.wait_ge(h.root, c + 1)
                    link(nc.vector.reciprocal(r, r))
                    if h.gate:
                        link(nc.vector.tensor_tensor(d, d, r, ALU.mult))
                        dve.wait_ge(h.sig, c + 1)
                        nc.vector.tensor_tensor(d, d, sg[:, c % 2, :].rearrange("p (e n) -> p e n", e=2), ALU.mult).then_inc(h.gated, 1)
                    else:
                        nc.vector.scalar_tensor_tensor(out=d, in0=d, scalar=h.scale[:, 0:1], in1=r, op0=ALU.mult,
                                                       op1=ALU.mult).then_inc(h.gated, 1)
                    dve.wait_ge(h.high, c + 1)
                    nc.vector.tensor_tensor(XL[:, h.x0 + 2 * c:h.x0 + 2 * c + 2, 0:S], d,
                                            XH[:, h.x0 + 2 * c:h.x0 + 2 * c + 2, 0:S].bitcast(F32), ALU.subtract).then_inc(h.out, 2)

            def mix0():
                c = COL_AT["sinks"]
                rotate(0)
                link(nc.vector.tensor_scalar(g_nsink[:, :], cols[:, c:c + 16], -1.0, None, ALU.mult))
                attention(gqa)

            def mix1():
                dve.wait_ge(tables, tables_at[1])
                lp = d_lam[:, :].rearrange("p (a b) -> p a b", b=2)
                nc.vector.tensor_tensor(d_lw[0:64, 8:10], lp[:, :, 0], lp[:, :, 1], ALU.mult).then_inc(lam_prod, 1)
                c = COL_AT["subln"]
                nc.vector.tensor_scalar(d_lw[:, 0:1], cols[:, c:c + 1], 1.0 - LAMBDA_INIT, None, ALU.mult)
                link(nc.vector.memset(d_zero[:, :], 0.0))
                dve.wait_ge(lam_exp, 1)
                link(nc.vector.tensor_tensor(d_lw[:, 13:14], d_lw[:, 11:12], d_lw[:, 10:11], ALU.subtract))
                link(nc.vector.tensor_scalar(d_lw[:, 14:15], d_lw[:, 13:14], -LAMBDA_INIT, None, ALU.add))
                rotate(1)
                attention(dif)
                dve.wait_ge(dif_root, 1)
                link(nc.vector.reciprocal(d_ss[:, :], d_ss[:, :]))
                for half in range(2):
                    o = d_o[:, :, half * 512:half * 512 + 512].rearrange("p t (h n) -> p t h n", h=4)
                    inv = d_ss[:, :].rearrange("p (t h o) -> p t h o", t=2, o=1)[:, :, 4 * half:4 * half + 4, :]
                    nc.vector.tensor_tensor(o, o, inv.to_broadcast([P, 2, 4, P]), ALU.mult).then_inc(dif_scaled, 1)
                for i in range(4):
                    dve.wait_ge(dif_high, i + 1)
                    nc.vector.scalar_tensor_tensor(
                        out=XL[:, 2 * i:2 * i + 2, 0:S], in0=bank[i][:, :].rearrange("p (e n) -> p e n", e=2), scalar=d_lw[:, 0:1],
                        in1=XH[:, 2 * i:2 * i + 2, 0:S].bitcast(F32), op0=ALU.mult, op1=ALU.subtract).then_inc(mix_out[1], 2)

            def mix2():
                rotate(2)
                for h in range(H_RET):
                    dve.wait_ge(ret_scores, h + 1)
                    if h >= 2:
                        dve.wait_ge(ret_o, h - 1)
                    nc.vector.tensor_tensor(r_sm[:, h % 2, :], bank[h % 2][:, 0:384], r_mask[:, h, :], ALU.mult).then_inc(ret_masked, 1)
                head_norm(hn[2])
                attention(dil)

            def mix3():
                dve.wait_ge(tables, tables_at[3])
                link(nc.vector.tensor_copy(a_wh[:, :, :], a_wr[:, :, :]))
                nc.vector.tensor_tensor(a_wl[:, :, :], a_wr[:, :, :], a_wh[:, :, :].bitcast(F32), ALU.subtract).then_inc(gs["wsplit"], 1)
                nc.vector.memset(ones_e[:, :], 1.0 / GLA_DV)
                nc.vector.memset(a_sm[:, :, :], 0.0)
                for t in range(2):
                    dve.wait_ge(gs["z"], t + 1)
                    nc.vector.tensor_scalar(a_zm[:, t, :], bank[t][:, :], 0.0, None, ALU.min)
                    link(nc.vector.tensor_scalar(a_la[:, t, :], bank[t][:, :], -1.0, None, ALU.mult))
                    nc.vector.tensor_tensor(a_la[:, t, :], a_la[:, t, :], bank[t][:, :], ALU.min).then_inc(gs["znabs"], 1)
                dve.wait_ge(gs["ln"], 1)
                nc.vector.tensor_tensor(a_la[:, :, :], a_zm[:, :, :], a_la[:, :, :], ALU.subtract).then_inc(gs["la"], 1)
                dve.wait_ge(gs["b"], 1)
                for i in range(2):
                    last = nc.vector.tensor_copy(a_b[:, 2 * i:2 * i + 2, :], bank[2 + i][:, :].rearrange("p (h n) -> p h n", h=2))
                last.then_inc(gs["bs"], 1)
                dve.wait_ge(gs["bs"], 1)
                b3 = a_b[:, :, :].rearrange("p h (c n) -> p (h c) n", n=GLA_C)
                e3 = a_el[:, :, :].rearrange("p h (c n) -> p (h c) n", n=GLA_C)
                nc.vector.tensor_tensor(e3, b3[:, :, GLA_C - 1:GLA_C].to_broadcast([P, 16, GLA_C]), b3, ALU.subtract).then_inc(gs["bd"], 1)
                q, k = a_proj[:, 0:4, :], a_proj[:, 4:8, :]
                dve.wait_ge(gs["eb"], 1)
                nc.vector.scalar_tensor_tensor(out=q, in0=q, scalar=P ** -0.5, in1=a_eb[:, :, :], op0=ALU.mult, op1=ALU.mult).then_inc(gs["qt"], 1)
                dve.wait_ge(gs["el"], 1)
                nc.vector.tensor_tensor(a_el[:, :, :], k, a_el[:, :, :], ALU.mult).then_inc(gs["ko"], 1)
                dve.wait_ge(gs["eb"], 2)
                dve.wait_ge(gs["ko"], 1)
                nc.vector.tensor_tensor(k, k, a_en[:, :, :], ALU.mult).then_inc(gs["kt"], 1)
                for h in range(H_GLA):
                    dve.wait_ge(gs["sc"], h + 1)
                    if h >= 2:
                        dve.wait_ge(gs["o"], h - 1)
                    nc.vector.copy_predicated(a_sm[:, h % 2, :], a_mask[:, :], bank[h % 2][:, 0:S]).then_inc(gs["sm"], 1)
                    for n in range(3):
                        dve.wait_ge(gs["kv"], 3 * h + n + 1)
                        if n == 0:
                            nc.vector.tensor_copy(a_st[:, h % 2, 0, :], bank[2][:, 0:256]).then_inc(gs["st"], 1)
                        else:
                            dve.wait_ge(gs["st"], 3 * h + n)
                            c0 = n * GLA_C + GLA_C - 1
                            nc.vector.scalar_tensor_tensor(out=a_st[:, h % 2, n, :], in0=a_st[:, h % 2, n - 1, :],
                                                           scalar=a_eb[:, h, c0:c0 + 1], in1=bank[2 + n][:, 0:256],
                                                           op0=ALU.mult, op1=ALU.add).then_inc(gs["st"], 1)
                head_norm(hn[3])

            mixes = [mix0, mix1, mix2, mix3]
            for kind, what in steps:
                if kind == "gemm":
                    if what.kind == "proj" and what is last_proj[3]:
                        nc.vector.memset(a_wr[:, :, :], 0.0).then_inc(gs["zero"], 1)
                    gemm(what)
                elif kind == "norm":
                    norm_dve(what)
                elif kind == "mix":
                    mixes[what]()
                    release()
                elif kind == "ffn_end":
                    release()


_FIXED = ["ffn_w_gate", "ffn_w_up", "ffn_w_down", "gqa_w_in", "gqa_w_out", "diff_w_in", "diff_w_out", "ada_w",
          "ffn_pre_w_gate_2", "ffn_pre_w_up_2", "ffn_pre_w_down_2", "ab_w_in_2", "ab_w_out_2", "gla_w_in_2", "gla_w_out_2",
          "ffn_post_w_gate_2", "ffn_post_w_up_2", "ffn_post_w_down_2"]


def kernel(**inputs):
    import concourse.bacc as bacc
    from concourse.bass_utils import run_bass_kernel_spmd as run

    def col(a):
        return np.asarray(a).reshape(-1, P).T

    arrays = {n: np.ascontiguousarray(inputs[n]) for n in _FIXED}
    arrays["xT"] = np.ascontiguousarray(np.concatenate([np.asarray(inputs["x"])[0].T, np.asarray(inputs["ctx"])[0].T], 1))
    packed = {"norm_w": col(inputs["norm_w"]), "final_norm_w": col(inputs["final_norm_w"]), "ada_b": col(inputs["ada_b"]),
              "pre2": col(inputs["ffn_pre_norm_2"]), "mix2": col(inputs["mix_norm_2"]), "post2": col(inputs["ffn_post_norm_2"]),
              "final2": col(inputs["final_norm_2"]), "subln": col(inputs["diff_subln_w"]),
              "sinks": np.broadcast_to(np.asarray(inputs["gqa_sinks"]).reshape(1, -1), (P, H_GQA))}
    arrays["cols"] = np.ascontiguousarray(np.concatenate([packed[n] for n in COLS], 1))
    arrays["c_cols"] = np.ascontiguousarray(np.stack([col(inputs["c"]), col(inputs["c_ctx"])], 2))
    arrays["diff_lambda"] = np.ascontiguousarray(np.asarray(inputs["diff_lambda"])[0].T)
    arrays["gla_w_a2_2"] = np.ascontiguousarray(np.asarray(inputs["gla_w_a2_2"])[0])
    arrays["gla_b_a_2"] = np.ascontiguousarray(np.asarray(inputs["gla_b_a_2"]))
    arrays.update(constants())

    nc = bacc.Bacc("TRN2", target_bir_lowering=False, num_devices=1, dynamic_dma_scratch_size=2048)
    A = {n: nc.dram_tensor(f"in_{n}", a.shape, mybir.dt.from_np(a.dtype), kind="ExternalInput").ap() for n, a in arrays.items()}
    A["out"] = nc.dram_tensor("out_T", (D, S), F32, kind="ExternalOutput").ap()
    build(nc, A)
    r = run(nc, [{f"in_{n}": a for n, a in arrays.items()}], core_ids=[0])
    return np.ascontiguousarray(r.results[0]["out_T"].T).reshape(1, S, D)
```

```python
import math
from contextlib import ExitStack

import numpy as np

import concourse.bass as bass
from concourse import mybir

F32 = mybir.dt.float32
F32R = mybir.dt.float32r
U32 = mybir.dt.uint32
ACTF = mybir.ActivationFunctionType
ALU = mybir.AluOpType
AX = mybir.AxisListType

P = 128
S = 256
D = 1024
DT = D // P
FF = 2816
FT = FF // P
KH = FT // 2
NMOD = 9
EPS = 1e-6
NEG = -1e30
H_GQA, KV_GQA, HD = 16, 4, 64
H_DIFF = 8
LAMBDA_INIT = 0.8 - 0.6 * math.exp(-0.3 * 1)
H_RET, H_DIL = 4, 8
H_GLA, GLA_DV, GLA_C, GLA_R = 4, 256, 64, 16
ADA_FIRST = 20
ADA_TILES = NMOD * DT


def rope_rotation(dim, half, period):
    r = np.zeros((P, P), np.float32)
    for base in range(0, P, period):
        for block in range(0, dim, 2 * half):
            for j in range(half):
                lo, hi = base + block + j, base + block + half + j
                r[hi, lo] = -1.0
                r[lo, hi] = 1.0
    return r


def rope_angles(kind):
    pos = np.arange(S, dtype=np.float32)
    if kind == "axial":
        inv = (10000.0 ** (-np.arange(0, 32, 2, dtype=np.float32) / 32)).astype(np.float32)
        row, col = np.floor(pos / 64), pos % 64
        ang = np.concatenate([row[:, None] * inv, row[:, None] * inv, col[:, None] * inv, col[:, None] * inv], -1)
        return np.tile(ang, (1, 2)).T
    if kind == "ret":
        inv = (10000.0 ** (-np.linspace(0.0, 1.0, 64, dtype=np.float32))).astype(np.float32)
        ang = pos[:, None] * inv
        return np.concatenate([ang, ang], -1).T
    inv = (500000.0 ** (-np.arange(0, 16, 2, dtype=np.float32) / 16)).astype(np.float32)
    ang = pos[:, None] * inv
    one = np.concatenate([ang, ang, np.zeros((S, 48), np.float32)], -1)
    return np.tile(one, (1, 2)).T


def constants():
    c = {}
    i, j = np.arange(S)[:, None], np.arange(S)[None, :]
    for kind in ("axial", "ret", "dil"):
        ang = rope_angles(kind).astype(np.float32)
        c[f"{kind}_cos"], c[f"{kind}_sin"] = np.cos(ang), np.sin(ang)
    c["axial_rot"] = rope_rotation(64, 16, 64)
    c["ret_rot"] = rope_rotation(128, 64, 128)
    c["dil_rot"] = rope_rotation(16, 8, 64)
    swap = np.zeros((P, P), np.float32)
    swap[np.arange(P), (np.arange(P) + 64) % P] = 1.0
    c["swap"] = swap
    c["ident"] = np.eye(P, dtype=np.float32)
    band = np.where(np.abs(i - j) <= 128, 0.0, NEG)
    full = np.concatenate([band, np.zeros((S, S))], 1)
    c["gqa_mask"] = full.reshape(2, P, 2 * S).transpose(1, 0, 2)
    dist = i - j
    count = np.zeros((S, S))
    for window, dil in ((128, 1), (512, 4), (2048, 16)):
        count += (dist >= 0) & (dist <= window) & (dist % dil == 0)
    c["dil_mask"] = np.where(count > 0, np.log(np.maximum(count, 1)) * 8.0, NEG).reshape(2, P, S).transpose(1, 0, 2)
    decay = np.zeros((P, H_RET, 384))
    for h in range(H_RET):
        log_g = np.log(1.0 - 2.0 ** (-5.0 - h))
        m = np.where(dist >= 0, np.exp(log_g * np.maximum(dist, 0)), 0.0).T * 128 ** -0.5
        decay[:, h, 0:256] = m[0:128, :]
        decay[:, h, 256:384] = m[128:256, 128:256]
    c["ret_mask"] = decay
    a, b = np.arange(P)[:, None], np.arange(P)[None, :]
    inside = (a // GLA_C == b // GLA_C) & (a <= b)
    c["gla_sum"] = inside / 16.0
    c["gla_mask"] = np.tile(inside, (1, 2)).astype(np.uint32)
    return {k: np.ascontiguousarray(v.astype(v.dtype if v.dtype == np.uint32 else np.float32)) for k, v in c.items()}


COLS = {"norm_w": 48, "final_norm_w": 8, "ada_b": 144, "pre2": 16, "mix2": 16, "post2": 16, "final2": 8,
        "subln": 1, "sinks": 16}
COL_AT = dict(zip(COLS, np.cumsum([0] + list(COLS.values()))[:-1].tolist()))
N_COLS = sum(COLS.values())


class Gemm:

    def __init__(self, kind, iters, k, t, src, rhs=None, ready=None, dst=None, gate=None, hid0=0, i0=0, ada=None):
        self.kind, self.iters, self.k, self.t, self.src, self.rhs, self.ready = kind, iters, k, t, src, rhs, ready
        self.dst, self.gate, self.hid0, self.i0 = dst, gate, hid0, i0
        self.ada = ada
        if kind == "ada":
            self.order = [("a", b) for b in range(4)]
        elif ada is None:
            self.order = [("w", b) for b in range(4)]
        else:
            self.order = [(x, b) for b in range(4) for x in "aw"]
        self.n = len(self.order)
        self.p0 = self.e0 = self.r0 = self.a0 = 0


def build(nc, A):
    ctx = ExitStack()
    with ctx:
        def sem(name):
            return ctx.enter_context(nc.semaphore(name))

        def sb(name, shape, dt=F32, stack=ctx):
            return stack.enter_context(nc.sbuf_tensor(name, shape, dt))

        xT = sb("xT", [P, DT, 2 * S])
        XH = sb("XH", [P, DT, 2 * S], F32R)
        XL = sb("XL", [P, DT, 2 * S], F32R)
        raw = sb("raw", [P, 4, KH, P])
        WH = sb("WH", [P, 4, KH, P], F32R)
        WL = sb("WL", [P, 4, KH, P], F32R)
        mods = sb("mods", [P, 2 * ADA_TILES, 2])
        scaleA = sb("scaleA", [P, 2, 3, DT, 2])
        gates = sb("gates", [P, 2, 3, DT, 2])
        halves = sb("halves", [P, 2, DT])
        cols = sb("cols", [P, N_COLS])
        csil = sb("csil", [P, DT, 2])
        c4 = sb("c4", [P, DT, 4], F32R)
        ones_d = sb("ones_d", [P, P])
        ones_e = sb("ones_e", [P, P])
        ones_1 = sb("ones_1", [P, P])
        ident = sb("ident", [P, P])
        sq = sb("sq", [P, 2, 2 * S])
        rstd = sb("rstd", [P, 2 * S])
        tn = sb("tn", [P, 2, 2 * S])
        sg = sb("sg", [P, 2, 2 * S])
        fold = sb("fold", [4, 2])
        sums = sq[0:4, 0, :]
        hf = tn
        eps = sb("eps", [P, 1])
        token = sb("token", [P, 16])

        def arena(*specs):
            stack = ExitStack()
            got = [sb(n, s, d, stack) for n, s, d in specs]
            stack.close()
            return got

        HH, HL = arena(("HH", [P, FT, 2 * S], F32R), ("HL", [P, FT, 2 * S], F32R))
        att_tiles = lambda n: [(f"{n}_s", [P, 4, 512], F32), (f"{n}_p", [P, 2, 512], F32),
                               (f"{n}_pt", [P, 2, 512], F32), (f"{n}_small", [P, 64, 8], F32)]
        rope_t = lambda n: [(f"{n}_cos", [P, S], F32), (f"{n}_sin", [P, S], F32), (f"{n}_rot", [P, P], F32)]
        (g_proj, g_ks, g_vn, g_o, g_mask, g_swap, g_rt, g_nsink, g_cos, g_sin, g_rot, *g_att) = arena(
            ("g_proj", [P, 12, 2 * S], F32), ("g_ks", [P, 2, 2 * S], F32), ("g_vn", [P, 4, 256], F32),
            ("g_o", [P, 4, 1024], F32), ("g_mask", [P, 2, 512], F32), ("g_swap", [P, P], F32), ("g_rt", [P, 2, S], F32),
            ("g_nsink", [P, 16], F32), *rope_t("g"), *att_tiles("g"))
        (d_q, d_kv, d_vn, d_o, d_ss, d_rt, d_lam, d_lw, d_zero, d_cos, d_sin, d_rot, *d_att) = arena(
            ("d_q", [P, 8, S], F32), ("d_kv", [P, 16, 2 * S], F32), ("d_vn", [P, 4, 1024], F32),
            ("d_o", [P, 2, 1024], F32), ("d_ss", [P, 16], F32), ("d_rt", [P, 2, S], F32), ("d_lam", [64, 4], F32), ("d_lw", [P, 16], F32),
            ("d_zero", [P, 1], F32), *rope_t("d"), *att_tiles("d"))
        (r_proj, r_vn, r_o, l_o, r_rt, r_mask, r_dmask, r_sm, r_cos, r_sin, r_rot, l_cos, l_sin, l_rot, *l_att) = arena(
            ("r_proj", [P, 28, S], F32), ("r_vn", [P, 2, 1024], F32), ("r_o", [P, 4, S], F32), ("l_o", [P, 2, 512], F32),
            ("r_rt", [P, 2, S], F32), ("r_mask", [P, 4, 384], F32), ("r_dmask", [P, 2, S], F32),
            ("r_sm", [P, 2, 384], F32), *rope_t("r"), *rope_t("l"), *att_tiles("l"))
        (a_proj, a_vn, a_kn, a_o, a_la, a_zm, a_b, a_el, a_st, a_sm, a_sum, a_mask, a_low, a_w2, a_ba,
         a_wr, a_wh, a_wl) = arena(
            ("a_proj", [P, 24, S], F32), ("a_vn", [P, 2, 1024], F32), ("a_kn", [P, 2, 512], F32),
            ("a_o", [P, 8, S], F32), ("a_la", [P, 2, 512], F32), ("a_zm", [P, 2, 512], F32),
            ("a_b", [P, 4, S], F32), ("a_el", [P, 4, S], F32),
            ("a_st", [P, 2, 3, S], F32), ("a_sm", [P, 2, S], F32), ("a_sum", [P, P], F32), ("a_mask", [P, S], U32),
            ("a_low", [GLA_R, S], F32), ("a_w2", [GLA_R, 512], F32), ("a_ba", [1, 512], F32),
            ("a_wr", [P, DT, P], F32), ("a_wh", [P, DT, P], F32R), ("a_wl", [P, DT, P], F32R))
        a_eb = a_zm[:, :, :].rearrange("p a (h n) -> p (a h) n", h=2)
        a_en = a_b

        bank = [ctx.enter_context(nc.psum_tensor(f"bank{i}", [P, 512], F32)) for i in range(8)]

        in_loaded = sem("in_loaded")
        x_loaded = sem("x_loaded")
        raw_ready = [sem(f"raw_ready{b}") for b in range(4)]
        ada_rows = sem("ada_rows")
        ada_turned = sem("ada_turned")
        ada_out = sem("ada_out")
        c_high, c_low = sem("c_high"), sem("c_low")
        csil_ready = sem("csil_ready")
        fold_ready = sem("fold_ready")
        setup_done = sem("setup_done")
        h_done = sem("h_done")
        split_done = sem("split_done")
        piece_done = sem("piece_done")
        act_bank = sem("act_bank")
        dve_bank = sem("dve_bank")
        res_done = sem("res_done")
        hid_high = sem("hid_high")
        hid_low = sem("hid_low")
        sq_ready = sem("sq_ready")
        sq_sum = sem("sq_sum")
        n_root = sem("n_root")
        n_mul = sem("n_mul")
        n_high = sem("n_high")
        n_low = sem("n_low")
        dve_self = sem("dve_self")
        act_self = sem("act_self")
        tables = sem("tables")
        arena_free = sem("arena_free")
        out_done = sem("out_done")

        def rows(w):
            return w.rearrange("(k p) n -> p k n", p=P)

        gemms = []
        state = {"p0": 0, "e0": 0, "r0": 0, "norms": 0, "hid": 0, "split": 0, "a0": 0}
        steps = []

        def add(g):
            g.p0, g.e0, g.r0, g.a0 = state["p0"], state["e0"], state["r0"], state["a0"]
            state["p0"] += g.n * g.iters
            if g.kind == "res":
                state["r0"] += (2 if g.k == KH else 4) * g.iters
            elif g.kind != "ada":
                state["e0"] += g.iters
            if g.ada is not None:
                state["a0"] += g.iters
            gemms.append(g)
            steps.append(("gemm", g))
            return g

        def wide(weights, slot):
            return weights[:, slot, 0:DT, :].rearrange("p (k c) n -> p k (c n)", k=2)

        def x_in(k, t):
            return XH[:, k, 0:t], XL[:, k, 0:t]

        def hid_in(k, t):
            return HH[:, k, 0:t], HL[:, k, 0:t]

        def norm(t, weight, shift=None, mode="split"):
            n = dict(i=state["norms"], t=t, weight=weight, shift=shift, mode=mode, h0=state["split"],
                     last=gemms[-1] if gemms[-1].kind == "res" and steps[-1][0] != "norm" else None)
            state["norms"] += 1
            state["split"] += DT if mode == "split" else 0
            steps.append(("norm", n))
            return n

        def ada_norm(l, n, t):
            return norm(t, lambda k, half: scaleA[:, l, n, k, half:half + 1],
                        lambda k, half: mods[:, l * ADA_TILES + 3 * n * DT + k, half:half + 1])

        def plain_norm(name, l, mode="split"):
            at = COL_AT[name] + DT * l
            return norm(S, lambda k, half: cols[:, at + k:at + k + 1], None, mode)

        def ada_src(i, b, tile):
            layer = tile // ADA_TILES
            return rows(A["ada_w"][layer])[:, 2 * b:2 * b + 2, bass.ds(i * 512 + (tile * P - layer * ADA_TILES * P), 512)]

        def ffn(n, t, gate, wg, wu, wd, ada=((KH, None),)):
            wg, wu, wd = rows(wg), rows(wu), rows(wd)
            ready, hid0, i0 = (lambda k: (n_low, n["h0"] + k + 1)), state["hid"], 0
            for iters, tile in ada:
                def src(i, kind, b, i0=i0, tile=tile):
                    if kind == "w":
                        return (wg, wu)[b % 2][:, :, bass.ds((i + i0) * 256 + b // 2 * P, P)]
                    return ada_src(i, b, tile)
                add(Gemm("up", iters, DT, t, src, x_in, ready, hid0=hid0, i0=i0, ada=tile))
                i0 += iters
            if ada[0][1] is not None:
                derive(ada[0][1], {ADA_FIRST: A1, A1: A2, A2: 2 * ADA_TILES}[ada[0][1]])
            add(Gemm("res", 4, KH, t, lambda i, _, b: wd[:, KH * (b % 2):KH * (b % 2) + KH, bass.ds(i * 256 + b // 2 * P, P)],
                     hid_in, lambda k: (hid_low, hid0 + k + 3), gate=gate))
            state["hid"] += FT
            steps.append(("ffn_end", None))

        def proj(n, w, iters, t, dst, col0=0):
            w = rows(w)
            return add(Gemm("proj", iters, DT, t, lambda i, _, b: w[:, :, bass.ds(i * 512 + (col0 + P * b), P)],
                            x_in, lambda k: (n_low, n["h0"] + k + 1), dst=dst))

        def out_proj(w, t, ready, gate):
            w = rows(w)
            return add(Gemm("res", 2, DT, t, lambda i, _, b: w[:, :, bass.ds(i * 512 + P * b, P)],
                            x_in, ready, gate=gate))

        gate1 = lambda l, n: (lambda d, half: gates[:, l, n, bass.ds(d, 1), half:half + 1].rearrange("p o h -> p (o h)"))
        gate2 = lambda n: (lambda d, half: halves[:, n, bass.ds(d, 1)])
        mix_out = [sem(f"mix_out{m}") for m in range(4)]
        dil_out = sem("dil_out")
        mix_ready = [lambda k: (mix_out[0], k + 1), lambda k: (mix_out[1], k + 1),
                     lambda k: (mix_out[2], k + 1) if k < 4 else (dil_out, k - 3), lambda k: (mix_out[3], k + 1)]

        def mixer(m, n, projs, w_out, t, gate):
            steps.append(("mix_start", m))
            for w, iters, tt, dst, col0 in projs:
                proj(n, w, iters, tt, dst, col0)
            steps.append(("mix", m))
            out_proj(w_out, t, mix_ready[m], gate)

        def derive(t0, t1):
            steps.append(("derive", (t0, t1)))

        add(Gemm("ada", ADA_FIRST // 4, DT, 0, lambda i, _, b: ada_src(i, b, 0), ada=0))
        derive(0, ADA_FIRST)
        A1 = ADA_FIRST + 4 * KH
        A2 = A1 + 4 * KH
        last = (2 * ADA_TILES - A2) // 4
        in_ffn = [[(KH, ADA_FIRST)], [((ADA_TILES - A1) // 4, A1), (KH - (ADA_TILES - A1) // 4, ADA_TILES)],
                  [(last, A2), (KH - last, None)]]
        for l in range(2):
            ffn(ada_norm(l, 0, 2 * S), 2 * S, gate1(l, 0), A["ffn_w_gate"][l, 0], A["ffn_w_up"][l, 0], A["ffn_w_down"][l, 0],
                in_ffn[2 * l])
            if l == 0:
                mixer(0, ada_norm(0, 1, 2 * S), [(A["gqa_w_in"][0], 3, 2 * S, g_proj, 0)], A["gqa_w_out"][0], 2 * S, gate1(0, 1))
            else:
                mixer(1, ada_norm(1, 1, 2 * S), [(A["diff_w_in"][0], 2, S, d_q, 0), (A["diff_w_in"][0], 4, 2 * S, d_kv, 1024)],
                      A["diff_w_out"][0], S, gate1(1, 1))
            t = 2 * S if l == 0 else S
            ffn(ada_norm(l, 2, t), t, gate1(l, 2), A["ffn_w_gate"][l, 1], A["ffn_w_up"][l, 1], A["ffn_w_down"][l, 1],
                in_ffn[1] if l == 0 else ((KH, None),))
        plain_norm("final_norm_w", 0, "replace")
        for l in range(2):
            n = plain_norm("pre2", l)
            ffn(n, S, gate2(0), A["ffn_pre_w_gate_2"][l], A["ffn_pre_w_up_2"][l], A["ffn_pre_w_down_2"][l])
            n = plain_norm("mix2", l)
            if l == 0:
                mixer(2, n, [(A["ab_w_in_2"][0], 7, S, r_proj, 0)], A["ab_w_out_2"][0], S, gate2(1))
            else:
                mixer(3, n, [(A["gla_w_in_2"][0], 6, S, a_proj, 0)], A["gla_w_out_2"][0], S, gate2(1))
            n = plain_norm("post2", l)
            ffn(n, S, gate2(0), A["ffn_post_w_gate_2"][l], A["ffn_post_w_up_2"][l], A["ffn_post_w_down_2"][l])
        plain_norm("final2", 0, "out")
        def four_on(g, i, j, after):
            if j + 4 < g.n:
                return g, i, j + 4
            return (*after, j + 4 - g.n) if after else None

        following = {id(g): nxt for g, nxt in zip(gemms, gemms[1:] + [None])}

        def res_tile(g, i, b):
            return i * 2 + b // 2 if g.k == KH else i * 4 + b

        def x_ready(n, k):
            g = n["last"]
            return g.r0 + k + 3

        def gqa_jobs():
            jobs = []
            for h in range(H_GQA):
                kv, qb = h // 4, 64 * (h % 2)
                ksrc = g_proj[:, 8 + kv // 2, :] if 64 * (kv % 2) == qb else g_ks[:, kv // 2, :]
                for t in range(4):
                    keys = (0, 512) if t < 2 else (256, 512)
                    jobs.append(dict(
                        maps=[(g_proj[qb:qb + 64, h // 2, t * P:(t + 1) * P], ksrc[qb:qb + 64, keys[0]:keys[1]])],
                        nk=keys[1] - keys[0], mask=g_mask[:, t, :] if t < 2 else g_mask[:, 0, 256:512], head=h,
                        v=[g_vn[:, keys[0] // P + j, kv * 64:kv * 64 + 64] for j in range((keys[1] - keys[0]) // P)],
                        o=h // 2, t=t, c0=h * 64, width=64, last=(h % 2 == 1 and t == 3)))
            return jobs

        def diff_jobs():
            jobs = []
            for h in range(H_DIFF):
                for t in range(2):
                    jobs.append(dict(
                        maps=[(d_q[64 * m:64 * m + 64, h, t * P:(t + 1) * P], d_kv[64 * m:64 * m + 64, h, :]) for m in range(2)],
                        nk=512, mask=d_zero[:, :].to_broadcast([P, 512]), head=None, v=[d_vn[:, j, h * P:(h + 1) * P] for j in range(4)],
                        o=h, t=t, c0=h * P, width=P, last=False))
            return jobs

        def dil_jobs():
            jobs = []
            for h in range(H_DIL):
                qb = 64 * (h % 2)
                for t in range(2):
                    jobs.append(dict(
                        maps=[(r_proj[qb:qb + 64, 16 + h // 2, t * P:(t + 1) * P], r_proj[qb:qb + 64, 20 + h // 2, :])],
                        nk=256, mask=r_dmask[:, t, :], head=None,
                        v=[r_vn[:, j, 512 + h * 64:512 + h * 64 + 64] for j in range(2)],
                        o=h // 2, t=t, c0=h * 64, width=64, last=(h % 2 == 1 and t == 1)))
            return jobs

        class Att:

            def __init__(self, name, jobs, tiles, cols_o, onat, sink=False, x0=0, out=None, squares=None):
                self.jobs, (self.s, self.p, self.pt, self.small) = jobs, tiles
                self.cols, self.sink, self.onat, self.x0, self.squares = cols_o, sink, onat, x0, squares
                self.scores = sem(f"{name}_scores")
                self.max = sem(f"{name}_max")
                self.exp = sem(f"{name}_exp")
                self.norm = sem(f"{name}_norm")
                self.turned = sem(f"{name}_turned")
                self.pt_ready = sem(f"{name}_pt_ready")
                self.o_done = sem(f"{name}_o_done")
                self.o_read = sem(f"{name}_o_read")
                self.o_turned = sem(f"{name}_o_turned")
                self.o_high = sem(f"{name}_o_high")
                self.o_free = out
                self.squared = sem(f"{name}_squared")

            def logits(self, s, m=0):
                return self.s[:, (2 * (s % 2) + m) if len(self.jobs[s]["maps"]) == 2 else s % 4, 0:self.jobs[s]["nk"]]

        gqa = Att("gqa", gqa_jobs(), g_att, 512, g_o, sink=True, out=mix_out[0])
        dif = Att("dif", diff_jobs(), d_att, 256, d_o, squares=d_ss)
        dil = Att("dil", dil_jobs(), l_att, 256, l_o, x0=4, out=dil_out)
        dif_root, dif_scaled = sem("subln_root"), sem("subln_scaled")
        dif_turned, dif_high = sem("subln_turned"), sem("subln_high")

        ropes = {
            0: [(g_proj, n, g_rot, g_cos, g_sin) for n in (8, 9, 0, 1, 2, 3, 4, 5, 6, 7)],
            1: [(d_kv, n, d_rot, d_cos, d_sin) for n in range(8)] + [(d_q, n, d_rot, d_cos, d_sin) for n in range(8)],
            2: [(r_proj, n, r_rot, r_cos, r_sin) for n in range(8)] + [(r_proj, n, l_rot, l_cos, l_sin) for n in range(16, 24)],
        }
        rope_tmp = {0: g_rt, 1: d_rt, 2: r_rt}
        rot_done = [sem(f"rot_done{m}") for m in range(3)]
        rot_read = [sem(f"rot_read{m}") for m in range(3)]
        roped = [sem(f"roped{m}") for m in range(3)]
        v_turned = [sem(f"v_turned{m}") for m in range(4)]
        v_stored = [sem(f"v_stored{m}") for m in range(4)]
        kswap = sem("kswap")
        kswap_stored = sem("kswap_stored")

        def v_groups(m):
            out = []
            if m == 0:
                for i in range(2):
                    out.append(([g_proj[:, 10 + i, t * P:(t + 1) * P] for t in range(4)], g_vn[:, :, i * P:(i + 1) * P]))
            if m == 1:
                for i in range(8):
                    out.append(([d_kv[:, 8 + i, t * P:(t + 1) * P] for t in range(4)], d_vn[:, :, i * P:(i + 1) * P]))
            if m == 2:
                for t in range(2):
                    for tile0, c0 in ((8, 0), (24, 512)):
                        out.append(([r_proj[:, tile0 + i, t * P:(t + 1) * P] for i in range(4)],
                                    r_vn[:, t, c0:c0 + 512].rearrange("p (g n) -> p g n", g=4)))
            if m == 3:
                for t in range(2):
                    for c0 in (0, 4):
                        out.append(([a_proj[:, 8 + c0 + i, t * P:(t + 1) * P] for i in range(4)],
                                    a_vn[:, t, c0 * P:c0 * P + 512].rearrange("p (g n) -> p g n", g=4)))
            return out

        def stat_of(h, values):
            if h.joined:
                return values[:, 0:S].rearrange("p (o n) -> p o n", o=1).to_broadcast([P, 2, S])
            return values.rearrange("p (e n) -> p e n", e=2)

        class HeadNorm:
            def __init__(self, name, data, chunks, joined, gate, x0, out):
                self.data, self.chunks, self.joined, self.gate, self.x0, self.out = data, chunks, joined, gate, x0, out
                self.mean = sem(f"{name}_mean")
                self.centred = sem(f"{name}_centred")
                self.squared = sem(f"{name}_squared")
                self.var = sem(f"{name}_var")
                self.root = sem(f"{name}_root")
                self.gated = sem(f"{name}_gated")
                self.high = sem(f"{name}_high")
                self.sig = sem(f"{name}_sig")
        hn = {2: HeadNorm("rhn", r_o, 2, False, (r_proj, 12), 0, mix_out[2]),
              3: HeadNorm("ahn", a_o, 4, True, (a_proj, 16), 0, mix_out[3])}
        mix_in = [sem(f"mix_in{m}") for m in range(4)]
        ret_scores, ret_masked, ret_o = sem("ret_scores"), sem("ret_masked"), sem("ret_o")
        lam_prod, lam_sum, lam_exp, lam_done = sem("lam_prod"), sem("lam_sum"), sem("lam_exp"), sem("lam_done")
        gs = {n: sem("gla_" + n) for n in ("wsplit", "low", "lowc", "z", "znabs", "ln", "la", "b", "bs", "eb", "qt", "kt", "bd", "el",
                                           "ko", "kturn", "kstore", "sc", "sm", "kv", "st", "zero", "o")}

        last_proj = {}
        seen = None
        for kind, what in steps:
            if kind == "gemm":
                seen = what
            if kind == "mix":
                last_proj[what] = seen

        consts = {0: [(g_cos, "axial_cos"), (g_sin, "axial_sin"), (g_rot, "axial_rot"), (g_swap, "swap"), (g_mask, "gqa_mask")],
                  1: [(d_cos, "axial_cos"), (d_sin, "axial_sin"), (d_rot, "axial_rot"), (d_lam, "diff_lambda")],
                  2: [(r_cos, "ret_cos"), (r_sin, "ret_sin"), (r_rot, "ret_rot"), (l_cos, "dil_cos"), (l_sin, "dil_sin"),
                      (l_rot, "dil_rot"), (r_mask, "ret_mask"), (r_dmask, "dil_mask")],
                  3: [(a_sum, "gla_sum"), (a_mask, "gla_mask"), (a_w2, "gla_w_a2_2"), (a_ba, "gla_b_a_2"), (a_wr, None)]}
        tables_at = {}
        total = 0
        for m in range(4):
            total += 16 * len(consts[m])
            tables_at[m] = total
        turn_before_mix = {0: 2, 1: 5, 2: 8, 3: 11}

        block = ctx.enter_context(nc.Block())

        @block.sync
        def _(sp):
            for g in gemms:
                def load(i):
                    for j, (kind, b) in enumerate(g.order):
                        if g.p0 > 0 or not isinstance(i, int):
                            sp.wait_ge(split_done, i * g.n + (g.p0 + j - 3))
                        sp.dma_start(raw[:, j % 4, 0:g.k, :] if kind == "w" else wide(raw, j % 4), g.src(i, kind, b)).then_inc(raw_ready[j % 4], 16)
                load(0)
                with sp.Fori(1, g.iters) as i:
                    load(i)

        @block.gpsimd
        def _(pool):
            pool.dma_start(cols[:, :], A["cols"]).then_inc(in_loaded, 16)
            pool.dma_start(csil[:, :, :], A["c_cols"]).then_inc(in_loaded, 16)
            pool.dma_start(ident[:, :], A["ident"]).then_inc(in_loaded, 16)
            pool.dma_start(xT[:, :, :], A["xT"].rearrange("(k p) n -> p k n", p=P)).then_inc(x_loaded, 16)
            def load_tables(m):
                pool.wait_ge(arena_free, turn_before_mix[m])
                for dst, name in consts[m]:
                    if name is None:
                        pool.wait_ge(gs["zero"], 1)
                        pool.dma_start(a_wr[:, :, 0:GLA_R], rows(A["gla_w_in_2"][0])[:, :, 3072:3072 + GLA_R]).then_inc(tables, 16)
                    else:
                        src = A[name]
                        d = dst[tuple([slice(None)] * len(dst.shape))]
                        pool.dma_start(d, src).then_inc(tables, 16)

            for kind, what in steps:
                if kind == "mix_start":
                    load_tables(what)
            pool.wait_ge(tables, tables_at[3])

        @block.tensor
        def _(pe):
            pe.wait_ge(setup_done, 1)
            pe.wait_ge(c_high, 1)
            pe.wait_ge(c_low, 1)
            pe.wait_ge(fold_ready, 1)

            def ada_piece(g, i, j, b):
                pe.wait_ge(split_done, i * g.n + (g.p0 + j + 1))
                if b == 0 and (g.a0 > 0 or not isinstance(i, int)):
                    pe.wait_ge(ada_rows, i + g.a0)
                for k in range(2):
                    c = c4[:, 2 * b + k, :]
                    nc.tensor.matmul(bank[7][0:4, :], c, wide(WH, j % 4)[:, k, :], start=(b == 0 and k == 0), stop=False)
                    last = nc.tensor.matmul(bank[7][0:4, :], c, wide(WL, j % 4)[:, k, :], start=False, stop=(b == 3 and k == 1))
                last.then_inc(piece_done, 1)

            def ada_turn(g, i):
                pe.wait_ge(ada_rows, i + (g.a0 + 1))
                if g.a0 > 0 or not isinstance(i, int):
                    pe.wait_ge(ada_out, i + g.a0)
                for c in range(4):
                    last = nc.tensor.matmul(bank[6][:, 2 * c:2 * c + 2], sums[:, c * P:(c + 1) * P], fold[:, :], start=True, stop=True)
                last.then_inc(ada_turned, 1)

            def piece(g, i, j, b, first):
                a = b % 2
                pe.wait_ge(split_done, i * g.n + (g.p0 + j + 1))
                down = g.k == KH
                if g.kind == "res":
                    out = bank[4 + (b // 2 if down else b % 2)]
                    if not down or a == 0:
                        r = g.r0 + (2 * i + b // 2 if down else 4 * i + b)
                        pe.wait_ge(res_done, r + 1)
                else:
                    out = bank[b]
                    pe.wait_ge(dve_bank if a else act_bank, 2 * (g.e0 + i) + (1 + b // 2))
                for k in range(g.k):
                    kk = k + (KH * a if down else 0)
                    if first and (b < 2 if down else b == 0):
                        pe.wait_ge(*g.ready(kk))
                    high, low = g.rhs(kk, g.t)
                    start = k == 0 and (a == 0 or not down)
                    stop = k == g.k - 1 and (a == 1 or not down)
                    o = out[:, 0:g.t]
                    nc.tensor.matmul(o, WH[:, j % 4, k, :], high, start=start, stop=False)
                    nc.tensor.matmul(o, WH[:, j % 4, k, :], low, start=False, stop=False)
                    last = nc.tensor.matmul(o, WL[:, j % 4, k, :], high, start=False, stop=stop)
                last.then_inc(piece_done, 1)

            def gemm(g):
                def turn(i, first):
                    for j, (kind, b) in enumerate(g.order):
                        if kind == "w":
                            piece(g, i, j, b, first)
                        else:
                            ada_piece(g, i, j, b)
                    if g.ada is not None:
                        ada_turn(g, i)
                turn(0, True)
                with pe.Fori(1, g.iters) as i:
                    turn(i, False)

            def norm_sums(n):
                for k in range(DT):
                    pe.wait_ge(sq_ready, DT * n["i"] + k + 1)
                    nc.tensor.matmul(bank[6][:, 0:n["t"]], ones_d[:, :], sq[:, k % 2, 0:n["t"]], start=(k == 0),
                                     stop=(k == DT - 1)).then_inc(sq_sum, 1)

            def banks_free(g):
                pe.wait_ge(act_bank, 2 * (g.e0 + g.iters) + 2)
                pe.wait_ge(dve_bank, 2 * (g.e0 + g.iters) + 2)
                pe.wait_ge(res_done, g.r0 + 2)

            def rotate(m):
                for n, (src, tile, rot, _, _) in enumerate(ropes[m]):
                    if n >= 4:
                        pe.wait_ge(rot_read[m], n - 3)
                    nc.tensor.matmul(bank[n % 4][:, 0:S], rot[:, :], src[:, tile, 0:S], start=True,
                                     stop=True).then_inc(rot_done[m], 1)

            def turn_v(m):
                for n, (blocks, _) in enumerate(v_groups(m)):
                    if n >= 2:
                        pe.wait_ge(v_stored[m], n - 1)
                    for j, blk in enumerate(blocks):
                        last = nc.tensor.transpose(bank[6 + n % 2][:, j * P:(j + 1) * P], blk, ident[:, :])
                    last.then_inc(v_turned[m], 1)

            def attention(a):
                jobs, n = a.jobs, len(a.jobs)
                for s in range(n + 5):
                    if s < n:
                        j = jobs[s]
                        if s >= 2:
                            pe.wait_ge(a.max, len(j["maps"]) * (s - 1))
                        for m, (q, k) in enumerate(j["maps"]):
                            nc.tensor.matmul(bank[2 * (s % 2) + m][:, 0:j["nk"]], q, k, start=True,
                                             stop=True).then_inc(a.scores, 1)
                    if 2 <= s < n + 2:
                        j = jobs[s - 2]
                        two = len(j["maps"]) == 2
                        pe.wait_ge(a.norm if two else a.exp, s - 1)
                        if s >= 4:
                            pe.wait_ge(a.pt_ready, s - 3)
                        probs = a.p[:, s % 2, :] if two else a.logits(s - 2)
                        for c in range(j["nk"] // P):
                            last = nc.tensor.transpose(bank[4 + s % 2][:, c * P:(c + 1) * P], probs[:, c * P:(c + 1) * P], ident[:, :])
                        last.then_inc(a.turned, 1)
                    if 3 <= s < n + 3:
                        j = jobs[s - 3]
                        pe.wait_ge(a.pt_ready, s - 2)
                        if s >= 5:
                            pe.wait_ge(a.o_read, s - 4)
                        nk = j["nk"] // P
                        for c in range(nk):
                            last = nc.tensor.matmul(bank[6 + (s - 3) % 2][:, 0:j["width"]], a.pt[:, (s - 3) % 2, c * P:(c + 1) * P],
                                                    j["v"][c], start=(c == 0), stop=(c == nk - 1))
                        last.then_inc(a.o_done, 1)
                    if s >= 5 and jobs[s - 5]["last"]:
                        o = jobs[s - 5]["o"]
                        pe.wait_ge(a.o_read, s - 4)
                        if o >= 2:
                            pe.wait_ge(a.o_free, o - 1)
                        for t in range(a.cols // P):
                            last = nc.tensor.transpose(bank[1 + 2 * (o % 2)][:, t * P:(t + 1) * P],
                                                       a.onat[:, t, o * P:(o + 1) * P], ident[:, :])
                        last.then_inc(a.o_turned, 1)
                if a.squares is None:
                    pe.wait_ge(a.o_free, jobs[-1]["o"] + 1)

            def head_norm(h):
                w = S if h.joined else 2 * S
                def stat(c, src, b, done):
                    if h.joined:
                        for e in range(2):
                            last = nc.tensor.matmul(bank[b][:, 0:S], ones_e[:, :], src[:, e, :], start=(e == 0), stop=(e == 1))
                    else:
                        last = nc.tensor.matmul(bank[b][:, 0:w], ones_e[:, :], src, start=True, stop=True)
                    last.then_inc(done, 1)
                for step in range(h.chunks + 1):
                    if step < h.chunks:
                        if step >= 2:
                            pe.wait_ge(h.centred, step - 1)
                        stat(step, h.data[:, 2 * step:2 * step + 2, :], step % 2, h.mean)
                    if step == 0:
                        continue
                    c = step - 1
                    pe.wait_ge(h.squared, c + 1)
                    if c >= 2:
                        pe.wait_ge(h.gated, c - 1)
                    stat(c, sq[:, c % 2, :].rearrange("p (e n) -> p e n", e=2), 2 + c % 2, h.var)

            def mix0():
                pe.wait_ge(tables, tables_at[0])
                banks_free(last_proj[0])
                rotate(0)
                turn_v(0)
                for i in range(2):
                    pe.wait_ge(roped[0], i + 1)
                    nc.tensor.matmul(bank[4 + i][:, :], g_swap[:, :], g_proj[:, 8 + i, :], start=True, stop=True).then_inc(kswap, 1)
                pe.wait_ge(kswap_stored, 2)
                pe.wait_ge(v_stored[0], 2)
                pe.wait_ge(roped[0], len(ropes[0]))
                attention(gqa)

            def mix1():
                pe.wait_ge(tables, tables_at[1])
                banks_free(last_proj[1])
                pe.wait_ge(lam_prod, 1)
                nc.tensor.matmul(bank[4][:, 0:2], ones_1[0:64, :], d_lw[0:64, 8:10], start=True, stop=True).then_inc(lam_sum, 1)
                rotate(1)
                turn_v(1)
                pe.wait_ge(v_stored[1], 8)
                pe.wait_ge(lam_exp, 1)
                pe.wait_ge(roped[1], len(ropes[1]))
                attention(dif)
                for h in range(H_DIFF):
                    pe.wait_ge(dif_scaled, 1 + h // 4)
                    for t in range(2):
                        c0 = (h % 2) * S + t * P
                        last = nc.tensor.transpose(bank[h // 2][:, c0:c0 + P], d_o[:, t, h * P:(h + 1) * P], ident[:, :])
                    if h % 2:
                        last.then_inc(dif_turned, 1)

            def mix2():
                pe.wait_ge(tables, tables_at[2])
                banks_free(last_proj[2])
                rotate(2)
                turn_v(2)
                pe.wait_ge(v_stored[2], 4)
                pe.wait_ge(roped[2], len(ropes[2]))
                for h in range(H_RET):
                    if h >= 2:
                        pe.wait_ge(ret_masked, h - 1)
                    q, k = r_proj[:, h, :], r_proj[:, 4 + h, :]
                    nc.tensor.matmul(bank[h % 2][:, 0:256], k[:, 0:P], q[:, 0:256], start=True, stop=True)
                    nc.tensor.matmul(bank[h % 2][:, 256:384], k[:, P:256], q[:, P:256], start=True, stop=True).then_inc(ret_scores, 1)
                    pe.wait_ge(ret_masked, h + 1)
                    if h >= 2:
                        pe.wait_ge(mix_in[2], h - 1)
                    o = bank[2 + h % 2]
                    nc.tensor.matmul(o[:, 0:256], r_vn[:, 0, h * P:(h + 1) * P], r_sm[:, h % 2, 0:256], start=True, stop=False)
                    nc.tensor.matmul(o[:, P:256], r_vn[:, 1, h * P:(h + 1) * P], r_sm[:, h % 2, 256:384], start=False,
                                     stop=True).then_inc(ret_o, 1)
                pe.wait_ge(mix_in[2], H_RET)
                head_norm(hn[2])
                pe.wait_ge(hn[2].gated, 2)
                attention(dil)

            def mix3():
                pe.wait_ge(tables, tables_at[3])
                banks_free(last_proj[3])
                pe.wait_ge(gs["wsplit"], 1)
                for k in range(DT):
                    nc.tensor.matmul(bank[4][:, 0:S], a_wh[:, k, :], XH[:, k, 0:S], start=(k == 0), stop=False)
                    nc.tensor.matmul(bank[4][:, 0:S], a_wh[:, k, :], XL[:, k, 0:S], start=False, stop=False)
                    last = nc.tensor.matmul(bank[4][:, 0:S], a_wl[:, k, :], XH[:, k, 0:S], start=False, stop=(k == DT - 1))
                last.then_inc(gs["low"], 1)
                pe.wait_ge(gs["lowc"], 1)
                for t in range(2):
                    nc.tensor.matmul(bank[t][:, :], a_low[:, t * P:(t + 1) * P], a_w2[:, :], start=True, stop=False)
                    nc.tensor.matmul(bank[t][:, :], ones_1[0:1, :], a_ba[:, :], start=False, stop=True).then_inc(gs["z"], 1)
                turn_v(3)
                pe.wait_ge(gs["la"], 1)
                for h in range(H_GLA):
                    for t in range(2):
                        c0 = (h % 2) * S + t * P
                        last = nc.tensor.matmul(bank[2 + h // 2][:, c0:c0 + P], a_la[:, t, h * P:(h + 1) * P], a_sum[:, :],
                                                start=True, stop=True)
                last.then_inc(gs["b"], 1)
                pe.wait_ge(v_stored[3], 4)
                pe.wait_ge(gs["ko"], 1)
                for t in range(2):
                    for h in range(H_GLA):
                        last = nc.tensor.transpose(bank[6 + t][:, h * P:(h + 1) * P], a_el[:, h, t * P:(t + 1) * P], ident[:, :])
                    last.then_inc(gs["kturn"], 1)
                pe.wait_ge(gs["kstore"], 2)
                for h in range(H_GLA):
                    if h >= 2:
                        pe.wait_ge(gs["sm"], h - 1)
                    pe.wait_ge(gs["bs"], 1)
                    pe.wait_ge(gs["qt"], 1)
                    pe.wait_ge(gs["kt"], 1)
                    for t in range(2):
                        last = nc.tensor.matmul(bank[h % 2][:, t * P:(t + 1) * P], a_proj[:, 4 + h, t * P:(t + 1) * P],
                                                a_proj[:, h, t * P:(t + 1) * P], start=True, stop=True)
                    last.then_inc(gs["sc"], 1)
                    if h >= 1:
                        pe.wait_ge(gs["st"], 3 * h)
                    for n in range(3):
                        b0 = (n % 2) * 64
                        nc.tensor.matmul(bank[2 + n][:, 0:256], a_kn[b0:b0 + 64, n // 2, h * P:(h + 1) * P],
                                         a_vn[b0:b0 + 64, n // 2, h * 256:(h + 1) * 256], start=True, stop=True).then_inc(gs["kv"], 1)
                    pe.wait_ge(gs["sm"], h + 1)
                    pe.wait_ge(gs["st"], 3 * h + 3)
                    if h >= 2:
                        pe.wait_ge(mix_in[3], h - 1)
                    o = bank[6 + h % 2]
                    for e in range(2):
                        v0 = h * 256 + e * P
                        for t in range(2):
                            nc.tensor.matmul(o[:, e * 256 + t * P:e * 256 + (t + 1) * P], a_vn[:, t, v0:v0 + P],
                                             a_sm[:, h % 2, t * P:(t + 1) * P], start=(e == 0 and t == 0), stop=False)
                        for n in range(1, 4):
                            c0 = e * 256 + n * 64
                            last = nc.tensor.matmul(o[:, c0:c0 + 64], a_st[:, h % 2, n - 1, e * P:(e + 1) * P],
                                                    a_proj[:, h, n * 64:(n + 1) * 64], start=False, stop=(e == 1 and n == 3))
                    last.then_inc(gs["o"], 1)
                pe.wait_ge(mix_in[3], H_GLA)
                head_norm(hn[3])

            mixes = [mix0, mix1, mix2, mix3]
            for kind, what in steps:
                if kind == "gemm":
                    gemm(what)
                elif kind == "norm":
                    norm_sums(what)
                elif kind == "mix":
                    mixes[what]()

        @block.scalar
        def _(act):
            count = [0]

            def link(ins):
                count[0] += 1
                ins.then_inc(act_self, 1)
                act.wait_ge(act_self, count[0])

            act.wait_ge(in_loaded, 48)
            act.wait_ge(setup_done, 1)
            nc.scalar.activation(csil[:, :, :], csil[:, :, :], ACTF.Silu).then_inc(csil_ready, 1)
            act.wait_ge(csil_ready, 1)
            nc.scalar.activation(c4[:, :, 0:2], csil[:, :, :], ACTF.Copy).then_inc(c_high, 1)

            def high(g, i, j):
                q, b = i * g.n + (g.p0 + j), j % 4
                act.wait_ge(raw_ready[b], i * (4 * g.n) + (g.p0 // 4 + j // 4 + 1) * 16)
                if g.p0 + j > 3 or not isinstance(i, int) or i > 0:
                    act.wait_ge(piece_done, q - 3)
                nc.scalar.activation(WH[:, b, 0:g.k, :], raw[:, b, 0:g.k, :], ACTF.Copy).then_inc(h_done, 1)

            for b in range(4):
                high(gemms[0], 0, b)

            def body(g, i, after):
                q = i * g.n + g.p0
                t = g.t
                for j, (kind, b) in enumerate(g.order):
                    if kind == "a":
                        if four_on(g, i, j, after):
                            high(*four_on(g, i, j, after))
                        continue
                    if g.kind == "up" and b % 2 == 0:
                        act.wait_ge(piece_done, q + (j + 1))
                        nc.scalar.activation(sg[:, b // 2, 0:t], bank[b][:, 0:t], ACTF.Silu).then_inc(act_bank, 1)
                    if g.kind == "proj" and b % 2 == 0:
                        act.wait_ge(piece_done, q + (j + 1))
                        nc.scalar.activation(g.dst[:, bass.ds(i * 4 + b, 1), 0:t], bank[b][:, 0:t].rearrange("p (o n) -> p o n", o=1),
                                             ACTF.Copy).then_inc(act_bank, 1)
                    if g.kind == "up" and b == 2:
                        hidden(g, i, 0)
                    if four_on(g, i, j, after):
                        high(*four_on(g, i, j, after))
                    if g.kind == "up" and b == 3:
                        hidden(g, i, 1)

            def hidden(g, i, half):
                f = i * 2 + (2 * g.i0 + half)
                act.wait_ge(dve_bank, 2 * (g.e0 + i) + (3 + half))
                nc.scalar.activation(HH[:, bass.ds(f, 1), 0:g.t], hf[:, half:half + 1, 0:g.t], ACTF.Copy).then_inc(hid_high, 1)

            def gemm(g):
                if g.kind == "up":
                    act.wait_ge(arena_free, turn[0])
                if g.kind == "proj":
                    act.wait_ge(arena_free, turn[0])
                with act.Fori(0, g.iters - 1) as i:
                    body(g, i, (g, i + 1))
                nxt = following[id(g)]
                body(g, g.iters - 1, (nxt, 0) if nxt else None)

            def norm_act(n):
                t = n["t"]
                for k in range(DT):
                    if n["last"]:
                        act.wait_ge(res_done, x_ready(n, k))
                    if k == 0 and n["i"] == 0:
                        act.wait_ge(x_loaded, 16)
                        act.wait_ge(ada_out, ADA_FIRST // 4)
                    if k == 0 and not n["last"] and n["i"] > 0:
                        act.wait_ge(n_mul, DT * n["i"])
                    if k >= 2 or n["i"] > 0:
                        act.wait_ge(sq_sum, DT * n["i"] + k - 1)
                    nc.scalar.activation(sq[:, k % 2, 0:t], xT[:, k, 0:t], ACTF.Square).then_inc(sq_ready, 1)
                act.wait_ge(sq_sum, DT * n["i"] + DT)
                nc.scalar.activation(rstd[:, 0:t], bank[6][:, 0:t], ACTF.Sqrt, bias=eps[:, 0:1]).then_inc(n_root, 1)
                if n["mode"] != "split":
                    return
                for k in range(DT):
                    act.wait_ge(n_mul, DT * n["i"] + k + 1)
                    if n["shift"]:
                        for half in range(t // S):
                            cs = slice(half * S, half * S + S)
                            last = nc.scalar.activation(XH[:, k, cs], tn[:, k % 2, cs], ACTF.Identity, bias=n["shift"](k, half))
                    else:
                        last = nc.scalar.activation(XH[:, k, 0:t], tn[:, k % 2, 0:t], ACTF.Copy)
                    last.then_inc(n_high, 1)

            def store_v(m):
                for n, (_, dst) in enumerate(v_groups(m)):
                    act.wait_ge(v_turned[m], n + 1)
                    nc.scalar.activation(dst, bank[6 + n % 2][:, :].rearrange("p (g n) -> p g n", g=4), ACTF.Copy).then_inc(v_stored[m], 1)

            def attention(a):
                jobs, n = a.jobs, len(a.jobs)
                for s in range(n + 6):
                    if 2 <= s < n + 2:
                        nk = jobs[s - 2]["nk"]
                        act.wait_ge(a.turned, s - 1)
                        nc.scalar.activation(a.pt[:, s % 2, 0:nk], bank[4 + s % 2][:, 0:nk], ACTF.Copy).then_inc(a.pt_ready, 1)
                    if s < n:
                        nm, sm = len(jobs[s]["maps"]), a.small[:, s, :]
                        act.wait_ge(a.max, nm * s + nm)
                        for m in range(nm):
                            last = nc.scalar.activation(a.logits(s, m), a.logits(s, m), ACTF.Exp, bias=sm[:, m:m + 1],
                                                        scale=HD ** -0.5, accum_out=sm[:, 2 + m:3 + m])
                        if a.sink:
                            c = COL_AT["sinks"] + jobs[s]["head"]
                            last = nc.scalar.activation(sm[:, 4:5], cols[:, c:c + 1], ACTF.Exp, bias=sm[:, 0:1])
                        last.then_inc(a.exp, 1)
                    if a.squares is not None and 5 <= s < n + 5:
                        j = jobs[s - 5]
                        act.wait_ge(a.o_read, s - 4)
                        if s >= 13:
                            act.wait_ge(a.squared, s - 12)
                        i = s - 5
                        nc.scalar.activation(sq[:, (i // 4) % 2, (i % 4) * P:(i % 4 + 1) * P], a.onat[:, j["t"], j["c0"]:j["c0"] + P],
                                             ACTF.Square, accum_out=a.squares[:, j["t"] * 8 + j["o"]:j["t"] * 8 + j["o"] + 1]).then_inc(a.squared, 1)
                    if a.squares is None and s >= 6 and jobs[s - 6]["last"]:
                        o = jobs[s - 6]["o"]
                        act.wait_ge(a.o_turned, o + 1)
                        nc.scalar.activation(XH[:, a.x0 + o, 0:a.cols], bank[1 + 2 * (o % 2)][:, 0:a.cols], ACTF.Copy).then_inc(a.o_high, 1)

            def head_norm(h):
                def squares(c):
                    act.wait_ge(h.centred, c + 1)
                    if c >= 2:
                        act.wait_ge(h.var, c - 1)
                    nc.scalar.activation(sq[:, c % 2, :].rearrange("p (e n) -> p e n", e=2), h.data[:, 2 * c:2 * c + 2, :],
                                         ACTF.Square).then_inc(h.squared, 1)
                    src, t0 = h.gate
                    if c >= 2:
                        act.wait_ge(h.gated, c - 1)
                    nc.scalar.activation(sg[:, c % 2, :].rearrange("p (e n) -> p e n", e=2),
                                         src[:, t0 + 2 * c:t0 + 2 * c + 2, :], ACTF.Silu).then_inc(h.sig, 1)

                squares(0)
                for c in range(h.chunks):
                    if c + 1 < h.chunks:
                        squares(c + 1)
                    w = S if h.joined else 2 * S
                    act.wait_ge(h.var, c + 1)
                    nc.scalar.activation(tn[:, c % 2, 0:w], bank[2 + c % 2][:, 0:w], ACTF.Sqrt, bias=eps[:, 0:1]).then_inc(h.root, 1)
                    act.wait_ge(h.gated, c + 1)
                    nc.scalar.activation(XH[:, h.x0 + 2 * c:h.x0 + 2 * c + 2, 0:S], h.data[:, 2 * c:2 * c + 2, :],
                                         ACTF.Copy).then_inc(h.high, 1)

            def mix0():
                act.wait_ge(act_bank, 2 * (last_proj[0].e0 + last_proj[0].iters) + 2)
                store_v(0)
                for i in range(2):
                    act.wait_ge(kswap, i + 1)
                    nc.scalar.activation(g_ks[:, i, :], bank[4 + i][:, :], ACTF.Copy).then_inc(kswap_stored, 1)
                attention(gqa)

            def mix1():
                act.wait_ge(lam_sum, 1)
                nc.scalar.activation(d_lw[:, 10:12], bank[4][:, 0:2], ACTF.Exp).then_inc(lam_exp, 1)
                store_v(1)
                attention(dif)
                act.wait_ge(dif.squared, len(dif.jobs))
                nc.scalar.activation(d_ss[:, :], d_ss[:, :], ACTF.Sqrt, scale=1.0 / P, bias=eps[:, 0:1]).then_inc(dif_root, 1)
                for i in range(4):
                    act.wait_ge(dif_turned, i + 1)
                    nc.scalar.activation(XH[:, 2 * i:2 * i + 2, 0:S], bank[i][:, :].rearrange("p (e n) -> p e n", e=2), ACTF.Copy,
                                         scale=d_lw[:, 0:1]).then_inc(dif_high, 1)

            def mix2():
                store_v(2)
                for h in range(H_RET):
                    act.wait_ge(ret_o, h + 1)
                    nc.scalar.activation(r_o[:, h, :], bank[2 + h % 2][:, 0:256], ACTF.Copy).then_inc(mix_in[2], 1)
                head_norm(hn[2])
                attention(dil)

            def mix3():
                act.wait_ge(gs["low"], 1)
                nc.scalar.activation(a_low[:, :], bank[4][0:GLA_R, 0:S], ACTF.Copy).then_inc(gs["lowc"], 1)
                store_v(3)
                act.wait_ge(gs["znabs"], 2)
                link(nc.scalar.activation(a_la[:, :, :], a_la[:, :, :], ACTF.Exp))
                nc.scalar.activation(a_la[:, :, :], a_la[:, :, :], ACTF.Ln, bias=ones_1[:, 0:1]).then_inc(gs["ln"], 1)
                act.wait_ge(gs["bs"], 1)
                nc.scalar.activation(a_eb[:, :, :], a_b[:, :, :], ACTF.Exp).then_inc(gs["eb"], 1)
                act.wait_ge(gs["bd"], 1)
                nc.scalar.activation(a_en[:, :, :], a_b[:, :, :], ACTF.Exp, scale=-1.0).then_inc(gs["eb"], 1)
                nc.scalar.activation(a_el[:, :, :], a_el[:, :, :], ACTF.Exp).then_inc(gs["el"], 1)
                for t in range(2):
                    act.wait_ge(gs["kturn"], t + 1)
                    nc.scalar.activation(a_kn[:, t, :], bank[6 + t][:, :], ACTF.Copy).then_inc(gs["kstore"], 1)
                for h in range(H_GLA):
                    act.wait_ge(gs["o"], h + 1)
                    nc.scalar.activation(a_o[:, 2 * h:2 * h + 2, :], bank[6 + h % 2][:, :].rearrange("p (e n) -> p e n", e=2),
                                         ACTF.Copy).then_inc(mix_in[3], 1)
                act.wait_ge(mix_in[3], H_GLA)
                head_norm(hn[3])

            mixes = [mix0, mix1, mix2, mix3]
            turn = [1]
            for kind, what in steps:
                if kind == "gemm":
                    gemm(what)
                elif kind == "norm":
                    norm_act(what)
                elif kind == "mix":
                    mixes[what]()
                    turn[0] += 1
                elif kind == "ffn_end":
                    turn[0] += 1
            act.wait_ge(n_mul, DT * state["norms"])
            act.dma_start(A["out"].rearrange("(k p) n -> p k n", p=P), xT[:, :, 0:S]).then_inc(out_done, 16)
            act.wait_ge(out_done, 16)

        @block.vector
        def _(dve):
            count = [0]

            def link(ins):
                count[0] += 1
                ins.then_inc(dve_self, 1)
                dve.wait_ge(dve_self, count[0])

            turns = [0]

            def release():
                turns[0] += 1
                nc.vector.memset(token[:, turns[0]:turns[0] + 1], 0.0).then_inc(arena_free, 1)

            nc.vector.memset(ones_d[:, :], 1.0 / D)
            nc.vector.memset(ones_1[:, :], 1.0)
            nc.vector.memset(eps[:, :], EPS).then_inc(hid_low, 2)
            nc.vector.memset(ones_e[:, :], 1.0 / P).then_inc(setup_done, 1)
            nc.vector.memset(halves[:, 0, :], 0.5).then_inc(dve_bank, 2)
            nc.vector.memset(halves[:, 1, :], 1.0).then_inc(res_done, 2)
            nc.vector.memset(token[:, 0:1], 0.0).then_inc(act_bank, 2)

            def low(g, i, j):
                b = j % 4
                dve.wait_ge(h_done, i * g.n + (g.p0 + j + 1))
                nc.vector.tensor_tensor(WL[:, b, 0:g.k, :], raw[:, b, 0:g.k, :], WH[:, b, 0:g.k, :].bitcast(F32),
                                        ALU.subtract).then_inc(split_done, 1)

            ab = COL_AT["ada_b"]

            def ada_copy(g, i, j):
                dve.wait_ge(piece_done, i * g.n + (g.p0 + j + 1))
                nc.vector.tensor_copy(sums[:, :], bank[7][0:4, :]).then_inc(ada_rows, 1)

            def ada_store(g, i):
                tile = i * 4 + g.ada
                dve.wait_ge(ada_turned, i + (g.a0 + 1))
                bias = cols[:, bass.ds(tile + ab, 4)].rearrange("p (n o) -> p n o", o=1).to_broadcast([P, 4, 2])
                nc.vector.tensor_tensor(mods[:, bass.ds(tile, 4), :], bank[6][:, 0:8].rearrange("p (n o) -> p n o", o=2),
                                        bias, ALU.add).then_inc(ada_out, 1)

            def derive(t0, t1):
                dve.wait_ge(ada_out, t1 // 4)
                for l in range(2):
                    for n in range(3):
                        m0 = l * ADA_TILES + 3 * n * DT
                        if t0 < m0 + 2 * DT <= t1:
                            w0 = COL_AT["norm_w"] + (3 * l + n) * DT
                            w = cols[:, w0:w0 + DT].rearrange("p (n o) -> p n o", o=1).to_broadcast([P, DT, 2])
                            link(nc.vector.scalar_tensor_tensor(out=scaleA[:, l, n], in0=mods[:, m0 + DT:m0 + 2 * DT, :], scalar=1.0,
                                                                in1=w, op0=ALU.add, op1=ALU.mult))
                        if t0 < m0 + 3 * DT <= t1:
                            link(nc.vector.tensor_scalar(gates[:, l, n], mods[:, m0 + 2 * DT:m0 + 3 * DT, :],
                                                         1.0 if n == 1 else 0.5, None, ALU.mult))

            dve.wait_ge(in_loaded, 48)
            dve.wait_ge(c_high, 1)
            nc.vector.tensor_tensor(c4[:, :, 2:4], csil[:, :, :], c4[:, :, 0:2].bitcast(F32), ALU.subtract).then_inc(c_low, 1)
            nc.vector.tensor_tensor(fold[:, :], ident[0:4, 0:2], ident[0:4, 2:4], ALU.add).then_inc(fold_ready, 1)
            release()

            for b in range(4):
                low(gemms[0], 0, b)

            def body(g, i, after):
                q, t = i * g.n + g.p0, g.t
                down = g.k == KH
                for j, (kind, b) in enumerate(g.order):
                    if kind == "a":
                        if b == 3:
                            ada_copy(g, i, j)
                        if four_on(g, i, j, after):
                            low(*four_on(g, i, j, after))
                        continue
                    if g.kind == "up":
                        half = b // 2
                        if b % 2:
                            dve.wait_ge(piece_done, q + (j + 1))
                            dve.wait_ge(act_bank, 2 * (g.e0 + i) + (3 + half))
                            dve.wait_ge(hid_low, i * 2 + (g.hid0 + 2 * g.i0 + half + 1))
                            nc.vector.tensor_tensor(hf[:, half, 0:t], sg[:, half, 0:t], bank[b][:, 0:t], ALU.mult).then_inc(dve_bank, 1)
                    if g.kind == "proj" and b % 2:
                        dve.wait_ge(piece_done, q + (j + 1))
                        nc.vector.tensor_copy(g.dst[:, bass.ds(i * 4 + b, 1), 0:t],
                                              bank[b][:, 0:t].rearrange("p (o n) -> p o n", o=1)).then_inc(dve_bank, 1)
                    if g.kind == "res" and (b % 2 or not down):
                        dve.wait_ge(piece_done, q + (j + 1))
                        d = res_tile(g, i, b)
                        src = bank[4 + (b // 2 if down else b % 2)]
                        for half in range(t // S):
                            cs = slice(half * S, half * S + S)
                            x = xT[:, bass.ds(d, 1), cs]
                            last = nc.vector.scalar_tensor_tensor(
                                out=x, in0=src[:, cs].rearrange("p (o n) -> p o n", o=1), scalar=g.gate(d, half), in1=x,
                                op0=ALU.mult, op1=ALU.add)
                        last.then_inc(res_done, 1)
                    if g.kind == "up" and b == 2:
                        hidden_low(g, i, 0)
                    if four_on(g, i, j, after):
                        low(*four_on(g, i, j, after))
                    if g.kind == "up" and b == 3:
                        hidden_low(g, i, 1)
                if g.ada is not None:
                    ada_store(g, i)

            def hidden_low(g, i, half):
                f = i * 2 + (2 * g.i0 + half)
                dve.wait_ge(hid_high, g.hid0 + f + 1)
                nc.vector.tensor_tensor(HL[:, bass.ds(f, 1), 0:g.t], hf[:, half:half + 1, 0:g.t],
                                        HH[:, bass.ds(f, 1), 0:g.t].bitcast(F32), ALU.subtract).then_inc(hid_low, 1)

            def gemm(g):
                with dve.Fori(0, g.iters - 1) as i:
                    body(g, i, (g, i + 1))
                nxt = following[id(g)]
                body(g, g.iters - 1, (nxt, 0) if nxt else None)

            def norm_dve(n):
                t, i0 = n["t"], DT * n["i"]
                if n["i"] == 0:
                    dve.wait_ge(x_loaded, 16)
                dve.wait_ge(n_root, n["i"] + 1)
                link(nc.vector.reciprocal(rstd[:, 0:t], rstd[:, 0:t]))

                def scaled(k):
                    if n["mode"] == "split" and k >= 2:
                        dve.wait_ge(n_low, n["h0"] + k - 1)
                    for half in range(t // S):
                        cs = slice(half * S, half * S + S)
                        dst = tn[:, k % 2, cs] if n["mode"] == "split" else xT[:, k, cs]
                        last = nc.vector.scalar_tensor_tensor(out=dst, in0=xT[:, k, cs], scalar=n["weight"](k, half),
                                                              in1=rstd[:, cs], op0=ALU.mult, op1=ALU.mult)
                    last.then_inc(n_mul, 1)

                def rest(k):
                    dve.wait_ge(n_high, n["h0"] + k + 1)
                    if n["shift"]:
                        for half in range(t // S):
                            cs = slice(half * S, half * S + S)
                            last = nc.vector.scalar_tensor_tensor(
                                out=XL[:, k, cs], in0=tn[:, k % 2, cs], scalar=n["shift"](k, half),
                                in1=XH[:, k, cs].bitcast(F32), op0=ALU.add, op1=ALU.subtract)
                    else:
                        last = nc.vector.tensor_tensor(XL[:, k, 0:t], tn[:, k % 2, 0:t], XH[:, k, 0:t].bitcast(F32), ALU.subtract)
                    last.then_inc(n_low, 1)

                if n["mode"] != "split":
                    for k in range(DT):
                        scaled(k)
                    return
                scaled(0)
                for k in range(DT):
                    if k + 1 < DT:
                        scaled(k + 1)
                    rest(k)

            def rotate(m):
                tmp = rope_tmp[m]
                dve.wait_ge(tables, tables_at[m])
                for n, (src, tile, _, cos, sin) in enumerate(ropes[m]):
                    dve.wait_ge(rot_done[m], n + 1)
                    x = src[:, tile, 0:S]
                    if n >= 2:
                        dve.wait_ge(roped[m], n - 1)
                    nc.vector.tensor_tensor(tmp[:, n % 2, :], bank[n % 4][:, 0:S], sin[:, :], ALU.mult).then_inc(rot_read[m], 1)
                    link(nc.vector.tensor_tensor(x, x, cos[:, :], ALU.mult))
                    nc.vector.tensor_tensor(x, x, tmp[:, n % 2, :], ALU.add).then_inc(roped[m], 1)

            def attention(a):
                jobs, n = a.jobs, len(a.jobs)
                for s in range(n + 7):
                    if 1 <= s <= n:
                        nm, sm, nk = len(jobs[s - 1]["maps"]), a.small[:, s - 1, :], jobs[s - 1]["nk"]
                        dve.wait_ge(a.exp, s)
                        if a.sink:
                            link(nc.vector.tensor_tensor(sm[:, 2:3], sm[:, 2:3], sm[:, 4:5], ALU.add))
                        if nm == 1:
                            nc.vector.reciprocal(sm[:, 6:7], sm[:, 2:3]).then_inc(a.norm, 1)
                        else:
                            if s >= 3:
                                dve.wait_ge(a.turned, s - 2)
                            link(nc.vector.reciprocal(sm[:, 6:8], sm[:, 2:4]))
                            link(nc.vector.tensor_scalar(sm[:, 5:6], sm[:, 2:3], sm[:, 7:8], d_lw[:, 14:15], ALU.mult, ALU.mult))
                            nc.vector.scalar_tensor_tensor(out=a.p[:, (s - 1) % 2, 0:nk], in0=a.logits(s - 1, 1), scalar=sm[:, 5:6],
                                                           in1=a.logits(s - 1, 0), op0=ALU.mult, op1=ALU.add).then_inc(a.norm, 1)
                    if 4 <= s < n + 4:
                        j, sm = jobs[s - 4], a.small[:, s - 4, :]
                        dve.wait_ge(a.o_done, s - 3)
                        dve.wait_ge(a.norm, s - 3)
                        nc.vector.tensor_scalar(a.onat[:, j["t"], j["c0"]:j["c0"] + j["width"]], bank[6 + (s - 4) % 2][:, 0:j["width"]],
                                                sm[:, 6:7], None, ALU.mult).then_inc(a.o_read, 1)
                    if s < n:
                        j = jobs[s]
                        nm, sm, nk = len(j["maps"]), a.small[:, s, :], j["nk"]
                        if nm == 2 and s >= 2:
                            dve.wait_ge(a.norm, s - 1)
                        if nm == 1 and s >= 4:
                            dve.wait_ge(a.turned, s - 3)
                        for m in range(nm):
                            dve.wait_ge(a.scores, nm * s + m + 1)
                            link(nc.vector.tensor_tensor_reduce(
                                out=a.logits(s, m), in0=bank[2 * (s % 2) + m][:, 0:nk], in1=j["mask"], scale=1.0,
                                scalar=-3e38, op0=ALU.add, op1=ALU.max, accum_out=sm[:, 6 + m:7 + m]))
                            if a.sink:
                                nc.vector.tensor_scalar(sm[:, 0:1], sm[:, 6:7], -HD ** -0.5, g_nsink[:, j["head"]:j["head"] + 1],
                                                        ALU.mult, ALU.min).then_inc(a.max, 1)
                            else:
                                nc.vector.tensor_scalar(sm[:, m:m + 1], sm[:, 6 + m:7 + m], -HD ** -0.5, None, ALU.mult).then_inc(a.max, 1)
                    if a.squares is None and s >= 7 and jobs[s - 7]["last"]:
                        o = jobs[s - 7]["o"]
                        dve.wait_ge(a.o_high, o + 1)
                        nc.vector.tensor_tensor(XL[:, a.x0 + o, 0:a.cols], bank[1 + 2 * (o % 2)][:, 0:a.cols],
                                                XH[:, a.x0 + o, 0:a.cols].bitcast(F32), ALU.subtract).then_inc(a.o_free, 1)

            def head_norm(h):
                def centre(c):
                    d = h.data[:, 2 * c:2 * c + 2, :]
                    dve.wait_ge(h.mean, c + 1)
                    nc.vector.tensor_tensor(d, d, stat_of(h, bank[c % 2][:, :]), ALU.subtract).then_inc(h.centred, 1)

                centre(0)
                for c in range(h.chunks):
                    if c + 1 < h.chunks:
                        centre(c + 1)
                    d = h.data[:, 2 * c:2 * c + 2, :]
                    r = tn[:, c % 2, 0:S if h.joined else 2 * S]
                    dve.wait_ge(h.sig, c + 1)
                    link(nc.vector.tensor_tensor(d, d, sg[:, c % 2, :].rearrange("p (e n) -> p e n", e=2), ALU.mult))
                    dve.wait_ge(h.root, c + 1)
                    link(nc.vector.reciprocal(r, r))
                    nc.vector.tensor_tensor(d, d, stat_of(h, tn[:, c % 2, :]), ALU.mult).then_inc(h.gated, 1)
                    dve.wait_ge(h.high, c + 1)
                    nc.vector.tensor_tensor(XL[:, h.x0 + 2 * c:h.x0 + 2 * c + 2, 0:S], d,
                                            XH[:, h.x0 + 2 * c:h.x0 + 2 * c + 2, 0:S].bitcast(F32), ALU.subtract).then_inc(h.out, 2)

            def mix0():
                c = COL_AT["sinks"]
                rotate(0)
                link(nc.vector.tensor_scalar(g_nsink[:, :], cols[:, c:c + 16], -1.0, None, ALU.mult))
                attention(gqa)

            def mix1():
                dve.wait_ge(tables, tables_at[1])
                lp = d_lam[:, :].rearrange("p (a b) -> p a b", b=2)
                nc.vector.tensor_tensor(d_lw[0:64, 8:10], lp[:, :, 0], lp[:, :, 1], ALU.mult).then_inc(lam_prod, 1)
                c = COL_AT["subln"]
                nc.vector.tensor_scalar(d_lw[:, 0:1], cols[:, c:c + 1], 1.0 - LAMBDA_INIT, None, ALU.mult)
                link(nc.vector.memset(d_zero[:, :], 0.0))
                dve.wait_ge(lam_exp, 1)
                link(nc.vector.tensor_tensor(d_lw[:, 13:14], d_lw[:, 11:12], d_lw[:, 10:11], ALU.subtract))
                link(nc.vector.tensor_scalar(d_lw[:, 14:15], d_lw[:, 13:14], -LAMBDA_INIT, None, ALU.add))
                rotate(1)
                attention(dif)
                dve.wait_ge(dif_root, 1)
                link(nc.vector.reciprocal(d_ss[:, :], d_ss[:, :]))
                for half in range(2):
                    o = d_o[:, :, half * 512:half * 512 + 512].rearrange("p t (h n) -> p t h n", h=4)
                    inv = d_ss[:, :].rearrange("p (t h o) -> p t h o", t=2, o=1)[:, :, 4 * half:4 * half + 4, :]
                    nc.vector.tensor_tensor(o, o, inv.to_broadcast([P, 2, 4, P]), ALU.mult).then_inc(dif_scaled, 1)
                for i in range(4):
                    dve.wait_ge(dif_high, i + 1)
                    nc.vector.scalar_tensor_tensor(
                        out=XL[:, 2 * i:2 * i + 2, 0:S], in0=bank[i][:, :].rearrange("p (e n) -> p e n", e=2), scalar=d_lw[:, 0:1],
                        in1=XH[:, 2 * i:2 * i + 2, 0:S].bitcast(F32), op0=ALU.mult, op1=ALU.subtract).then_inc(mix_out[1], 2)

            def mix2():
                rotate(2)
                for h in range(H_RET):
                    dve.wait_ge(ret_scores, h + 1)
                    if h >= 2:
                        dve.wait_ge(ret_o, h - 1)
                    nc.vector.tensor_tensor(r_sm[:, h % 2, :], bank[h % 2][:, 0:384], r_mask[:, h, :], ALU.mult).then_inc(ret_masked, 1)
                head_norm(hn[2])
                attention(dil)

            def mix3():
                dve.wait_ge(tables, tables_at[3])
                link(nc.vector.tensor_copy(a_wh[:, :, :], a_wr[:, :, :]))
                nc.vector.tensor_tensor(a_wl[:, :, :], a_wr[:, :, :], a_wh[:, :, :].bitcast(F32), ALU.subtract).then_inc(gs["wsplit"], 1)
                nc.vector.memset(ones_e[:, :], 1.0 / GLA_DV)
                nc.vector.memset(a_sm[:, :, :], 0.0)
                for t in range(2):
                    dve.wait_ge(gs["z"], t + 1)
                    nc.vector.tensor_scalar(a_zm[:, t, :], bank[t][:, :], 0.0, None, ALU.min)
                    link(nc.vector.tensor_scalar(a_la[:, t, :], bank[t][:, :], -1.0, None, ALU.mult))
                    nc.vector.tensor_tensor(a_la[:, t, :], a_la[:, t, :], bank[t][:, :], ALU.min).then_inc(gs["znabs"], 1)
                dve.wait_ge(gs["ln"], 1)
                nc.vector.tensor_tensor(a_la[:, :, :], a_zm[:, :, :], a_la[:, :, :], ALU.subtract).then_inc(gs["la"], 1)
                dve.wait_ge(gs["b"], 1)
                for i in range(2):
                    last = nc.vector.tensor_copy(a_b[:, 2 * i:2 * i + 2, :], bank[2 + i][:, :].rearrange("p (h n) -> p h n", h=2))
                last.then_inc(gs["bs"], 1)
                dve.wait_ge(gs["bs"], 1)
                b3 = a_b[:, :, :].rearrange("p h (c n) -> p (h c) n", n=GLA_C)
                e3 = a_el[:, :, :].rearrange("p h (c n) -> p (h c) n", n=GLA_C)
                nc.vector.tensor_tensor(e3, b3[:, :, GLA_C - 1:GLA_C].to_broadcast([P, 16, GLA_C]), b3, ALU.subtract).then_inc(gs["bd"], 1)
                q, k = a_proj[:, 0:4, :], a_proj[:, 4:8, :]
                dve.wait_ge(gs["eb"], 1)
                nc.vector.scalar_tensor_tensor(out=q, in0=q, scalar=P ** -0.5, in1=a_eb[:, :, :], op0=ALU.mult, op1=ALU.mult).then_inc(gs["qt"], 1)
                dve.wait_ge(gs["el"], 1)
                nc.vector.tensor_tensor(a_el[:, :, :], k, a_el[:, :, :], ALU.mult).then_inc(gs["ko"], 1)
                dve.wait_ge(gs["eb"], 2)
                dve.wait_ge(gs["ko"], 1)
                nc.vector.tensor_tensor(k, k, a_en[:, :, :], ALU.mult).then_inc(gs["kt"], 1)
                for h in range(H_GLA):
                    dve.wait_ge(gs["sc"], h + 1)
                    if h >= 2:
                        dve.wait_ge(gs["o"], h - 1)
                    nc.vector.copy_predicated(a_sm[:, h % 2, :], a_mask[:, :], bank[h % 2][:, 0:S]).then_inc(gs["sm"], 1)
                    for n in range(3):
                        dve.wait_ge(gs["kv"], 3 * h + n + 1)
                        if n == 0:
                            nc.vector.tensor_copy(a_st[:, h % 2, 0, :], bank[2][:, 0:256]).then_inc(gs["st"], 1)
                        else:
                            dve.wait_ge(gs["st"], 3 * h + n)
                            c0 = n * GLA_C + GLA_C - 1
                            nc.vector.scalar_tensor_tensor(out=a_st[:, h % 2, n, :], in0=a_st[:, h % 2, n - 1, :],
                                                           scalar=a_eb[:, h, c0:c0 + 1], in1=bank[2 + n][:, 0:256],
                                                           op0=ALU.mult, op1=ALU.add).then_inc(gs["st"], 1)
                head_norm(hn[3])

            mixes = [mix0, mix1, mix2, mix3]
            for kind, what in steps:
                if kind == "gemm":
                    if what.kind == "proj" and what is last_proj[3]:
                        nc.vector.memset(a_wr[:, :, :], 0.0).then_inc(gs["zero"], 1)
                    gemm(what)
                elif kind == "norm":
                    norm_dve(what)
                elif kind == "mix":
                    mixes[what]()
                    release()
                elif kind == "ffn_end":
                    release()
                elif kind == "derive":
                    derive(*what)


_FIXED = ["ffn_w_gate", "ffn_w_up", "ffn_w_down", "gqa_w_in", "gqa_w_out", "diff_w_in", "diff_w_out", "ada_w",
          "ffn_pre_w_gate_2", "ffn_pre_w_up_2", "ffn_pre_w_down_2", "ab_w_in_2", "ab_w_out_2", "gla_w_in_2", "gla_w_out_2",
          "ffn_post_w_gate_2", "ffn_post_w_up_2", "ffn_post_w_down_2"]


def kernel(**inputs):
    import concourse.bacc as bacc
    from concourse.bass_utils import run_bass_kernel_spmd as run

    def col(a):
        return np.asarray(a).reshape(-1, P).T

    arrays = {n: np.ascontiguousarray(inputs[n]) for n in _FIXED}
    arrays["xT"] = np.ascontiguousarray(np.concatenate([np.asarray(inputs["x"])[0].T, np.asarray(inputs["ctx"])[0].T], 1))
    packed = {"norm_w": col(inputs["norm_w"]), "final_norm_w": col(inputs["final_norm_w"]), "ada_b": col(inputs["ada_b"]),
              "pre2": col(inputs["ffn_pre_norm_2"]), "mix2": col(inputs["mix_norm_2"]), "post2": col(inputs["ffn_post_norm_2"]),
              "final2": col(inputs["final_norm_2"]), "subln": col(inputs["diff_subln_w"]),
              "sinks": np.broadcast_to(np.asarray(inputs["gqa_sinks"]).reshape(1, -1), (P, H_GQA))}
    arrays["cols"] = np.ascontiguousarray(np.concatenate([packed[n] for n in COLS], 1))
    arrays["c_cols"] = np.ascontiguousarray(np.stack([col(inputs["c"]), col(inputs["c_ctx"])], 2))
    arrays["diff_lambda"] = np.ascontiguousarray(np.asarray(inputs["diff_lambda"])[0].T)
    arrays["gla_w_a2_2"] = np.ascontiguousarray(np.asarray(inputs["gla_w_a2_2"])[0])
    arrays["gla_b_a_2"] = np.ascontiguousarray(np.asarray(inputs["gla_b_a_2"]))
    arrays.update(constants())

    nc = bacc.Bacc("TRN2", target_bir_lowering=False, num_devices=1, dynamic_dma_scratch_size=2048)
    A = {n: nc.dram_tensor(f"in_{n}", a.shape, mybir.dt.from_np(a.dtype), kind="ExternalInput").ap() for n, a in arrays.items()}
    A["out"] = nc.dram_tensor("out_T", (D, S), F32, kind="ExternalOutput").ap()
    build(nc, A)
    r = run(nc, [{f"in_{n}": a for n, a in arrays.items()}], core_ids=[0])
    return np.ascontiguousarray(r.results[0]["out_T"].T).reshape(1, S, D)
```
